# Optimizing a Trainium2 kernel written in Bass

```python
import jax, jax.numpy as jnp
from jax import lax
import numpy as np

D_MODEL = 1024
BATCH = 1
SEQ = 1024
DEPTH = 1

D_MIX = D_MODEL
GLA_HEADS = 4
GLA_DV = (D_MIX // 2) // GLA_HEADS
GLA_DK = GLA_DV // 2
GLA_RANK = 16
GLA_GATE_NORMALIZER = 16.0
GLA_CHUNK = 64
ATT_Q_HEADS = 8
ATT_KV_HEADS = 2
ATT_HEAD_DIM = (D_MIX // 2) // ATT_Q_HEADS
ATT_WINDOW = 128
ATT_BLOCK = 128
ROT_DIM = ATT_HEAD_DIM // 4
ROPE_THETA = 500000.0
N_EXPERTS = 32
TOP_K = 4
D_FF = D_MODEL
SWIGLU_LIMIT = 7.0
SWIGLU_ALPHA = 1.702
MOE_BLOCK = 128
NORM_EPS = 1e-6
NEG_INF = -1e30
IN_SPLITS = (GLA_HEADS * GLA_DK, GLA_HEADS * GLA_DK, GLA_HEADS * GLA_DV, GLA_HEADS * GLA_DV, 2 * GLA_RANK, ATT_Q_HEADS * ATT_HEAD_DIM, ATT_KV_HEADS * ATT_HEAD_DIM, ATT_KV_HEADS * ATT_HEAD_DIM)
D_IN = sum(IN_SPLITS)
D_MIX_OUT = GLA_HEADS * GLA_DV + ATT_Q_HEADS * ATT_HEAD_DIM

kernel_name = 'hybrid_gla_swa_moe_block'

def rms_norm(x, g):
    xf = x.astype(jnp.float32)
    y = xf * lax.rsqrt(jnp.mean(xf * xf, axis=-1, keepdims=True) + NORM_EPS)
    return (y * g.astype(jnp.float32)).astype(x.dtype)

def partial_rotary(x, positions):
    half = ROT_DIM // 2
    inv_freq = ROPE_THETA ** (-2.0 * jnp.arange(half, dtype=jnp.float32) / ROT_DIM)
    ang = positions.astype(jnp.float32)[:, None] * inv_freq[None, :]
    cos = jnp.cos(ang)[None, :, None, :]
    sin = jnp.sin(ang)[None, :, None, :]
    x1 = x[..., :half].astype(jnp.float32)
    x2 = x[..., half:ROT_DIM].astype(jnp.float32)
    rot = jnp.concatenate([x1 * cos - x2 * sin, x2 * cos + x1 * sin], axis=-1).astype(x.dtype)
    return jnp.concatenate([rot, x[..., ROT_DIM:]], axis=-1)

def gla_one_direction(q, k, v, log_a):
    B, S, H, DK = q.shape
    DV = v.shape[-1]
    C = GLA_CHUNK
    N = S // C

    def chunks(t):
        return t.astype(jnp.float32).reshape(B, N, C, H, t.shape[-1]).transpose(1, 0, 3, 2, 4)

    qc, kc, vc, ac = chunks(q), chunks(k), chunks(v), chunks(log_a)
    b = jnp.cumsum(ac, axis=3)
    b_last = b[:, :, :, -1:, :]
    b_ref = b[:, :, :, C // 2 - 1:C // 2, :]
    scores = jnp.einsum('nbhid,nbhjd->nbhij', qc * jnp.exp(b - b_ref), kc * jnp.exp(b_ref - b))
    causal_in_chunk = jnp.tril(jnp.ones((C, C), dtype=bool))
    scores = jnp.where(causal_in_chunk, scores, 0.0)
    o_intra = jnp.einsum('nbhij,nbhjv->nbhiv', scores, vc)
    q_inter = qc * jnp.exp(b)
    k_state = kc * jnp.exp(b_last - b)
    chunk_decay = jnp.exp(b_last[:, :, :, 0, :])

    def step(state, inp):
        q_n, k_n, v_n, d_n = inp
        o_n = jnp.einsum('bhid,bhdv->bhiv', q_n, state)
        state = state * d_n[..., None] + jnp.einsum('bhjd,bhjv->bhdv', k_n, v_n)
        return state, o_n

    state0 = jnp.zeros((B, H, DK, DV), jnp.float32)
    _, o_inter = lax.scan(step, state0, (q_inter, k_state, vc, chunk_decay))
    o = o_intra + o_inter
    return o.transpose(1, 0, 3, 2, 4).reshape(B, S, H, DV)

def window_attention(q, k, v, sink):
    B, S, HQ, HD = q.shape
    HKV = k.shape[2]
    G = HQ // HKV
    QB = ATT_BLOCK
    NB = S // QB
    pad = ((0, 0), (QB, QB), (0, 0), (0, 0))

    def band(t):
        tp = jnp.pad(t, pad).reshape(B, NB + 2, QB, HKV, HD)
        return jnp.concatenate([tp[:, :-2], tp[:, 1:-1], tp[:, 2:]], axis=2)

    kb, vb = band(k), band(v)
    qb = q.reshape(B, NB, QB, HKV, G, HD)
    s = jnp.einsum('bnikgd,bnjkd->bnkgij', qb, kb).astype(jnp.float32) * (HD ** -0.5)
    blk = jnp.arange(NB)[:, None, None] * QB
    qpos = blk + jnp.arange(QB)[None, :, None]
    kpos = blk - QB + jnp.arange(3 * QB)[None, None, :]
    valid = (jnp.abs(kpos - qpos) <= ATT_WINDOW) & (kpos >= 0) & (kpos < S)
    s = jnp.where(valid[None, :, None, None], s, NEG_INF)
    sink_logit = jnp.broadcast_to(sink.astype(jnp.float32).reshape(HKV, G)[None, None, :, :, None, None], s.shape[:-1] + (1,))
    p = jax.nn.softmax(jnp.concatenate([s, sink_logit], axis=-1), axis=-1)[..., :-1]
    o = jnp.einsum('bnkgij,bnjkd->bnikgd', p.astype(v.dtype), vb)
    return o.reshape(B, S, HQ, HD)

def hybrid_mixer(h, w_in, w_gk_fwd, b_gk_fwd, w_gk_bwd, b_gk_bwd, g_gla_out, attn_sink, w_out):
    B, S, _ = h.shape
    proj = h @ w_in
    split_at = np.cumsum(IN_SPLITS)[:-1].tolist()
    gq, gk, gv, gg, glr, aq, ak, av = jnp.split(proj, split_at, axis=-1)
    q = (gq * (GLA_DK ** -0.5)).reshape(B, S, GLA_HEADS, GLA_DK)
    k = gk.reshape(B, S, GLA_HEADS, GLA_DK)
    v = gv.reshape(B, S, GLA_HEADS, GLA_DV)
    lr_f, lr_b = jnp.split(glr, 2, axis=-1)
    la_f = (jax.nn.log_sigmoid((lr_f @ w_gk_fwd + b_gk_fwd).astype(jnp.float32)) / GLA_GATE_NORMALIZER).reshape(B, S, GLA_HEADS, GLA_DK)
    la_b = (jax.nn.log_sigmoid((lr_b @ w_gk_bwd + b_gk_bwd).astype(jnp.float32)) / GLA_GATE_NORMALIZER).reshape(B, S, GLA_HEADS, GLA_DK)
    o_f = gla_one_direction(q, k, v, la_f)
    o_b = jnp.flip(gla_one_direction(jnp.flip(q, 1), jnp.flip(k, 1), jnp.flip(v, 1), jnp.flip(la_b, 1)), 1)
    o_gla = (o_f + o_b).astype(h.dtype)
    o_gla = rms_norm(o_gla, g_gla_out) * jax.nn.silu(gg.reshape(B, S, GLA_HEADS, GLA_DV))
    positions = jnp.arange(S)
    qa = partial_rotary(aq.reshape(B, S, ATT_Q_HEADS, ATT_HEAD_DIM), positions)
    ka = partial_rotary(ak.reshape(B, S, ATT_KV_HEADS, ATT_HEAD_DIM), positions)
    va = av.reshape(B, S, ATT_KV_HEADS, ATT_HEAD_DIM)
    o_att = window_attention(qa, ka, va, attn_sink)
    o = jnp.concatenate([o_gla.reshape(B, S, GLA_HEADS * GLA_DV), o_att.reshape(B, S, ATT_Q_HEADS * ATT_HEAD_DIM)], axis=-1)
    return o @ w_out

def moe_ffn(h, w_router, b_router, w_gate_up, b_gate_up, w_down, b_down):
    B, S, D = h.shape
    T = B * S
    A = T * TOP_K
    xf = h.reshape(T, D)
    logits = (xf @ w_router + b_router).astype(jnp.float32)
    top_v, top_i = lax.top_k(logits, TOP_K)
    gates = jax.nn.softmax(top_v, axis=-1)
    e_flat = top_i.reshape(A)
    tok_flat = jnp.arange(A, dtype=jnp.int32) // TOP_K
    order = jnp.argsort(e_flat)
    e_sorted = e_flat[order]
    counts = jnp.bincount(e_flat, length=N_EXPERTS)
    padded = (counts + MOE_BLOCK - 1) // MOE_BLOCK * MOE_BLOCK
    pad_end = jnp.cumsum(padded)
    pad_start = pad_end - padded
    start = jnp.cumsum(counts) - counts
    dest = pad_start[e_sorted] + jnp.arange(A, dtype=jnp.int32) - start[e_sorted]
    R = A + N_EXPERTS * MOE_BLOCK
    n_blocks = R // MOE_BLOCK
    row_tok = jnp.zeros((R,), jnp.int32).at[dest].set(tok_flat[order])
    row_gate = jnp.zeros((R,), jnp.float32).at[dest].set(gates.reshape(A)[order])
    block_expert = jnp.minimum(jnp.searchsorted(pad_end, jnp.arange(n_blocks) * MOE_BLOCK, side='right'), N_EXPERTS - 1)
    xs = xf[row_tok].reshape(n_blocks, MOE_BLOCK, D)

    def expert_block(args):
        xb, e = args
        gu = xb @ w_gate_up[e] + b_gate_up[e]
        gate, up = jnp.split(gu, 2, axis=-1)
        gate = jnp.minimum(gate, SWIGLU_LIMIT)
        up = jnp.clip(up, -SWIGLU_LIMIT, SWIGLU_LIMIT)
        act = (up + 1.0) * gate * jax.nn.sigmoid(SWIGLU_ALPHA * gate)
        return act @ w_down[e] + b_down[e]

    ys = lax.map(expert_block, (xs, block_expert)).reshape(R, D)
    out = jnp.zeros((T, D), h.dtype).at[row_tok].add(ys * row_gate[:, None].astype(ys.dtype))
    return out.reshape(B, S, D)

def setup_inputs(seed: int = 0) -> dict:
    key = jax.random.key(seed)
    ks = jax.random.split(key, 24)
    f32 = jnp.float32
    L, D = DEPTH, D_MODEL
    gk_w = GLA_HEADS * GLA_DK

    def nrm(k, shape, scale):
        return jax.random.normal(k, shape, f32) * scale

    return {
        'x': nrm(ks[0], (BATCH, SEQ, D), 1.0),
        'c': nrm(ks[1], (BATCH, D), 1.0),
        'w_ada': nrm(ks[2], (L, D, 6 * D), D ** -0.5),
        'b_ada': nrm(ks[3], (L, 6 * D), 0.02),
        'g_pre_mix': 1.0 + nrm(ks[4], (L, D), 0.02),
        'g_post_mix': 1.0 + nrm(ks[5], (L, D), 0.02),
        'w_in': nrm(ks[6], (L, D, D_IN), D ** -0.5),
        'w_gk_fwd': nrm(ks[7], (L, GLA_RANK, gk_w), GLA_RANK ** -0.5),
        'b_gk_fwd': nrm(ks[8], (L, gk_w), 0.1),
        'w_gk_bwd': nrm(ks[9], (L, GLA_RANK, gk_w), GLA_RANK ** -0.5),
        'b_gk_bwd': nrm(ks[10], (L, gk_w), 0.1),
        'g_gla_out': 1.0 + nrm(ks[11], (L, GLA_DV), 0.02),
        'attn_sink': nrm(ks[12], (L, ATT_Q_HEADS), 1.0),
        'w_out': nrm(ks[13], (L, D_MIX_OUT, D), D_MIX_OUT ** -0.5),
        'g_pre_ffn': 1.0 + nrm(ks[14], (L, D), 0.02),
        'g_post_ffn': 1.0 + nrm(ks[15], (L, D), 0.02),
        'w_router': nrm(ks[16], (L, D, N_EXPERTS), D ** -0.5),
        'b_router': nrm(ks[17], (L, N_EXPERTS), 0.01),
        'w_gate_up': nrm(ks[18], (L, N_EXPERTS, D, 2 * D_FF), D ** -0.5),
        'b_gate_up': nrm(ks[19], (L, N_EXPERTS, 2 * D_FF), 0.01),
        'w_down': nrm(ks[20], (L, N_EXPERTS, D_FF, D), D_FF ** -0.5),
        'b_down': nrm(ks[21], (L, N_EXPERTS, D), 0.01),
    }

def reference(x, c, w_ada, b_ada, g_pre_mix, g_post_mix, w_in, w_gk_fwd, b_gk_fwd, w_gk_bwd, b_gk_bwd, g_gla_out, attn_sink, w_out, g_pre_ffn, g_post_ffn, w_router, b_router, w_gate_up, b_gate_up, w_down, b_down):
    B = x.shape[0]
    D = x.shape[-1]
    c_act = jax.nn.silu(c)
    for l in range(DEPTH):
        mod = (c_act @ w_ada[l] + b_ada[l]).reshape(B, 6, D)[:, :, None, :]
        shift1, scale1, gate1, shift2, scale2, gate2 = (mod[:, i] for i in range(6))
        h = rms_norm(x, g_pre_mix[l]) * (1.0 + scale1) + shift1
        y = hybrid_mixer(h, w_in[l], w_gk_fwd[l], b_gk_fwd[l], w_gk_bwd[l], b_gk_bwd[l], g_gla_out[l], attn_sink[l], w_out[l])
        x = x + gate1 * rms_norm(y, g_post_mix[l])
        h = rms_norm(x, g_pre_ffn[l]) * (1.0 + scale2) + shift2
        y = moe_ffn(h, w_router[l], b_router[l], w_gate_up[l], b_gate_up[l], w_down[l], b_down[l])
        x = x + gate2 * rms_norm(y, g_post_ffn[l])
    return x


_drawn_inputs = setup_inputs


def setup_inputs(seed=0):
    import zlib

    import numpy as np

    out = dict(_drawn_inputs(seed))
    spreads = {}
    factors = {'attn_sink': 8.0, 'g_post_ffn': 5.922, 'b_gate_up': 8.0, 'b_down': 8.0}
    for name, (base, spread) in spreads.items():
        noise = np.random.default_rng([zlib.crc32(name.encode()), seed]).standard_normal(out[name].shape)
        drawn = base * np.exp(spread * noise) if base else spread * noise
        out[name] = __import__('jax').numpy.asarray(drawn.astype(out[name].dtype))
    for name, factor in factors.items():
        out[name] = (out[name] * factor).astype(out[name].dtype)
    return out
```

```python
from contextlib import ExitStack

import numpy as np

import concourse.bass as bass
from concourse import mybir

P = 128
D = 1024
SEQ = 1024
NT = SEQ // P
KD = D // P
HEADS, DK, DV, RANK = 4, 64, 128, 16
CHUNK = 64
NCH = SEQ // CHUNK
QH, KVH, HD = 8, 2, 64
ROT = HD // 4
HALF = ROT // 2
THETA = 500000.0
NE, TOPK, FF = 32, 4, 1024
BLK = P
MAXB = SEQ * TOPK // BLK + NE
EPS = 1e-6
LIMIT, ALPHA = 7.0, 1.702
NEG = -1e30

F32 = mybir.dt.float32
I32 = mybir.dt.int32
U32 = mybir.dt.uint32
ALU = mybir.AluOpType
ACT = mybir.ActivationFunctionType
AX = mybir.AxisListType

C_Q, C_K, C_V, C_G, C_LR, C_AQ, C_AK = 0, 256, 512, 1024, 1536, 1568, 2080


def rotary_table():
    inv = (np.float32(THETA) ** (np.float32(-2.0) * np.arange(HALF, dtype=np.float32) / np.float32(ROT))).astype(np.float32)
    ang = (np.arange(SEQ, dtype=np.float32)[:, None] * inv[None, :]).astype(np.float32)
    t = np.stack([np.cos(ang), np.sin(ang)]).astype(np.float32)
    return np.ascontiguousarray(t.reshape(2, NT, P, HALF).transpose(2, 0, 1, 3).reshape(P, 2 * NT * HALF))


def block_kernel(nc, x, c, w_ada, b_ada, g_pre_mix, g_post_mix, w_in, w_gk_fwd, b_gk_fwd, w_gk_bwd, b_gk_bwd,
                 g_gla_out, attn_sink, w_out, g_pre_ffn, g_post_ffn, w_router, b_router,
                 w_gate_up, b_gate_up, w_down, b_down, out):
    ctx = ExitStack()
    with ctx:
        def sb(name, shape, dt=F32):
            return ctx.enter_context(nc.sbuf_tensor(name, shape, dt))

        def sem(name):
            return ctx.enter_context(nc.semaphore(name))

        ctx.enter_context(nc.allow_non_contiguous_dma(reason="small index and vector loads"))

        h2_dram = nc.dram_tensor("h2_rows", [SEQ, D], F32, kind="Internal").ap()
        tok_dram = nc.dram_tensor("slot_token", [(MAXB + 1) * BLK, 1], I32, kind="Internal").ap()
        y_dram = nc.dram_tensor("expert_rows", [MAXB * BLK, D], F32, kind="Internal").ap()
        rot_dram = nc.inline_tensor(rotary_table(), name="rotary_table")
        rot_dram = rot_dram.ap() if hasattr(rot_dram, "ap") else rot_dram

        W = sb("W", [P, 24576])
        X = sb("X", [P, NT, D])
        R = sb("R", [P, 12288])
        hT = W[:, 0:8192].rearrange("p (k s) -> p k s", k=KD)
        gbc = W[:, 0:4096].rearrange("p (g d) -> p g d", g=4)
        ada_ring = W[:, 8192:16384].rearrange("p (r n) -> p r n", r=4)
        AQ = W[:, 8192:12288].rearrange("p (t n) -> p t n", t=NT)
        AKV = W[:, 12288:14336].rearrange("p (t n) -> p t n", t=NT)
        LR = W[0:RANK, 14336:16384].rearrange("p (b s) -> p b s", b=2)
        win_ring = W[:, 16384:24576].rearrange("p (r k n) -> p r k n", r=2, k=KD)
        GI = W[:, 16384:24576].rearrange("p (a s) -> p a s", a=8)
        wout_sb = W[:, 16384:24576].rearrange("p (k n) -> p k n", k=KD)
        O = W[:, 0:4096].rearrange("p (t n) -> p t n", t=NT)
        QKT = R[:, 0:4096].rearrange("p (a s) -> p a s", a=4)
        V = R[:, 4096:8192].rearrange("p (t n) -> p t n", t=NT)
        GG = R[:, 8192:12288].rearrange("p (t n) -> p t n", t=NT)
        acc = R[:, 0:6144]
        xn = R[:, 0:2048].rearrange("p (b d) -> p b d", b=2)
        S1 = R[:, 8192:9216]
        SH1 = R[:, 9216:10240]
        OT = R[:, 0:8192].rearrange("p (k s) -> p k s", k=KD)
        kT = R[:, 8192:9216]
        qT = R[:, 9216:9728]
        SC = W[:, 4096:7168].rearrange("p (h n) -> p h n", h=QH)
        xn2 = R[:, 8192:10240].rearrange("p (b d) -> p b d", b=2)
        h2T = R[:, 10240:11264].rearrange("p (k s) -> p k s", k=KD)
        wgu = W[:, 0:16384].rearrange("p (k n) -> p k n", k=KD)
        wdn = W[:, 16384:24576].rearrange("p (k n) -> p k n", k=KD)
        XG = R[:, 0:1024]
        XT = R[:, 1024:2048].rearrange("p (k s) -> p k s", k=KD)
        AB = R[:, 2048:3072].rearrange("p (h n) -> p h n", h=2)
        AT = R[:, 3072:4096].rearrange("p (k s) -> p k s", k=KD)
        YS = R[:, 4096:5120]
        BI = R[:, 5120:7168]
        GS = R[:, 7168:8192].rearrange("p (h n) -> p h n", h=2)
        US = R[:, 8192:9216].rearrange("p (h n) -> p h n", h=2)
        SG = R[:, 9216:10240].rearrange("p (h n) -> p h n", h=2)
        YR = W[:, 0:16384].rearrange("p (r n) -> p r n", r=16)
        FO = R[:, 0:4096].rearrange("p (r n) -> p r n", r=4)

        MODR = sb("MODR", [P, 4, D])
        GP1, S2, SH2, GP2 = (MODR[:, j, :] for j in range(4))
        ident = sb("ident", [P, P])
        ones = sb("ones", [P, P])
        tri = sb("tri", [P, P])
        cmask = sb("cmask", [P, 2, P])
        amask = sb("amask", [P, 3, P])
        scanm = W[:, 7168:8192]
        rot = sb("rot", [P, 2, NT, HALF])
        rtmp = W[:, 5760:6016].rearrange("p (a t f) -> p a t f", a=4, t=NT)
        cvec = sb("cvec", [KD, P])
        cT = sb("cT", [P, 2, KD])
        bgk = sb("bgk", [4, P])
        bgT = sb("bgT", [P, 4])
        wgk = sb("wgk", [RANK, 2, 256])
        wlr = sb("wlr", [P, KD, 2 * RANK])
        wrt = sb("wrt", [P, KD, NE])
        ggla = sb("ggla", [P, DV])
        sinkb = sb("sinkb", [P, QH])
        brt = sb("brt", [P, NE])
        st = sb("st", [P, 64])
        held_done = sem("held_done")
        held = sb("held", [P, 1])
        mhalf = sb("mhalf", [P, HEADS])
        dec = sb("dec", [P, NCH])
        KS = W[:, 5120:5248]
        ST = W[:, 5248:5504].rearrange("p (h n) -> p h n", h=2)
        S = W[:, 5504:5760].rearrange("p (h n) -> p h n", h=2)
        am = sb("am", [P, 6, QH])
        LG = W[:, 3584:3840].rearrange("p (t e) -> p t e", t=NT)
        M8 = sb("M8", [P, NT, 8])
        I8 = sb("I8", [P, NT, 8], U32)
        IF = sb("IF", [P, NT, TOPK])
        GT8 = sb("GT8", [P, NT, TOPK])
        gsum = sb("gsum", [P, 2, NT])
        OH = W[:, 2048:3072].rearrange("p (t k e) -> p t k e", t=NT, k=TOPK)
        OM = R[:, 11264:12288].rearrange("p (t k e) -> p t k e", t=NT, k=TOPK)
        MK = W[:, 3072:3328].rearrange("p (t e) -> p t e", t=NT)
        GM = W[:, 3840:4096].rearrange("p (t e) -> p t e", t=NT)
        GMT = R[0:NE, 10240:11264].rearrange("p (t e) -> p t e", t=NT)
        PO = W[:, 3328:3584].rearrange("p (t e) -> p t e", t=NT)
        cn = sb("cn", [P, 4, NE])
        iot = sb("iot", [P, 64])
        SL = sb("SL", [P, NT, TOPK])
        SLI = sb("SLI", [P, NT * TOPK], I32)
        TI = sb("TI", [P, NT], I32)
        EB = sb("EB", [1, MAXB])
        EBI = sb("EBI", [1, MAXB], I32)
        CEI = sb("CEI", [1, 2 * NE], I32)
        ZI = sb("ZI", [P, MAXB + 1], I32)
        IX = sb("IX", [P, 1], I32)
        bdn = R[0:NE, 11264:12288]
        PTv = [W[:, 7168:7552], W[:, 7552:7936]]
        SQ = sb("SQ", [P, D], mybir.dt.bfloat16)
        XS = W[:, 4096:5120]
        OMX = W[0:1, 0:MAXB * NE]
        PS = ctx.enter_context(nc.psum_tensor("PS", [P, 8, 512], F32))

        x_in = sem("x_in")
        small_in = sem("small_in")
        bada_in = sem("bada_in")
        acc_zero = sem("acc_zero")
        const_done = sem("const_done")
        ada_in = [sem(f"ada_in{r}") for r in range(4)]
        ada_used = sem("ada_used")
        win_in = [sem(f"win_in{r}") for r in range(2)]
        wlr_in = sem("wlr_in")
        vec_T = sem("vec_T")
        c_ready = sem("c_ready")
        silu_sig = sem("silu_sig")
        mod_ps = sem("mod_ps")
        mod_ready = sem("mod_ready")
        dve = sem("dve")
        act = sem("act")
        pool = sem("pool")
        h_ssq = sem("h_ssq")
        og_ssq = sem("og_ssq")
        f_rstd = sem("f_rstd")
        x1_rstd = sem("x1_rstd")
        y_rstd = sem("y_rstd")
        og_rstd = sem("og_rstd")
        h_rstd = sem("h_rstd")
        h_row = sem("h_row")
        h_tps = sem("h_tps")
        h_ready = sem("h_ready")
        pj_ps = sem("pj_ps")
        pj_ev = sem("pj_ev")
        gg_sig = sem("gg_sig")
        gg_done = sem("gg_done")
        z_ps = sem("z_ps")
        z_rd = sem("z_rd")
        z_exp = sem("z_exp")
        z_ln = sem("z_ln")
        la_ready = sem("la_ready")
        ex_in = sem("ex_in")
        ex_out = sem("ex_out")
        gi_ready = sem("gi_ready")
        gl_ks = sem("gl_ks")
        gl_ksr = sem("gl_ksr")
        gl_st = sem("gl_st")
        gl_str = sem("gl_str")
        gl_u = sem("gl_u")
        gl_s = sem("gl_s")
        gl_o = sem("gl_o")
        gl_ev = sem("gl_ev")
        og_ready = sem("og_ready")
        rot_ready = sem("rot_ready")
        at_T = sem("at_T")
        at_Tr = sem("at_Tr")
        at_s = sem("at_s")
        at_sr = sem("at_sr")
        at_m = sem("at_m")
        at_e = sem("at_e")
        at_n = sem("at_n")
        at_p = sem("at_p")
        at_pr = sem("at_pr")
        at_o = sem("at_o")
        at_or = sem("at_or")
        og_T = sem("og_T")
        og_Tr = sem("og_Tr")
        wout_in = sem("wout_in")
        y_ps = sem("y_ps")
        y_ssq = sem("y_ssq")
        x1_ready = sem("x1_ready")
        x1_ssq = sem("x1_ssq")
        h2_row = sem("h2_row")
        h2_st = [sem(f"h2_st{b}") for b in range(2)]
        h2_tps = sem("h2_tps")
        h2_tr = sem("h2_tr")
        lg_ps = sem("lg_ps")
        lg_ready = sem("lg_ready")
        g_exp = sem("g_exp")
        mk_ready = sem("mk_ready")
        po_ps = sem("po_ps")
        gmt_ps = sem("gmt_ps")
        gmt_r = sem("gmt_r")
        plan_ready = sem("plan_ready")
        zero_st = sem("zero_st")
        tok_st = sem("tok_st")
        gu_in = [sem(f"gu_in{g}") for g in range(4)]
        dn_in = [sem(f"dn_in{g}") for g in range(2)]
        bi_in = sem("bi_in")
        gu_used = [sem(f"gu_used{g}") for g in range(4)]
        dn_used = [sem(f"dn_used{g}") for g in range(2)]
        bi_used = sem("bi_used")
        ix_in = sem("ix_in")
        xg_in = sem("xg_in")
        tx_ps = sem("tx_ps")
        tx_ready = sem("tx_ready")
        gu_ps = sem("gu_ps")
        gu_add = sem("gu_add")
        gu_g = sem("gu_g")
        gu_m = sem("gu_m")
        gu_c = sem("gu_c")
        gu_sig = sem("gu_sig")
        ab_ready = sem("ab_ready")
        ta_ps = sem("ta_ps")
        ta_ready = sem("ta_ready")
        yb_rd = sem("yb_rd")
        yb_st = sem("yb_st")
        fill_st = sem("fill_st")
        yr_in = [sem(f"yr_in{r}") for r in range(16)]
        bd_ps = sem("bd_ps")
        bdn_in = sem("bdn_in")
        scan_ready = sem("scan_ready")
        f_acc = sem("f_acc")
        f_ssq = sem("f_ssq")
        f_out = sem("f_out")
        out_st = [sem(f"out_st{b}") for b in range(4)]

        N_SMALL = 15
        N_FILL = 16 * (MAXB - NE) // NT
        GJ = 12 + NT
        groups = [("qk", C_Q, 512, 0), ("v", C_V, 512, 1), ("g", C_G, 512, 0), ("aq", C_AQ, 512, 1), ("akv", C_AK, 256, 0)]

        block = ctx.enter_context(nc.Block())

        @block.sync
        def _(sp):
            small = 0

            def load(dst, src):
                nonlocal small
                sp.dma_start(dst, src).then_inc(small_in, 16)
                small += 1

            load(cvec[:, :], c.rearrange("a (k p) -> (a k) p", p=P))
            sp.dma_start(X[:, 0:4, :], x[0, 0:512, :].rearrange("(t p) d -> p t d", p=P)).then_inc(x_in, 16)
            sp.wait_ge(acc_zero, 1)
            sp.dma_start(acc[0:1, :], b_ada).then_inc(bada_in, 16)
            load(bgk[0:2, :], b_gk_fwd.rearrange("a (k p) -> (a k) p", p=P))
            load(bgk[2:4, :], b_gk_bwd.rearrange("a (k p) -> (a k) p", p=P))
            load(wgk[:, 0, :], w_gk_fwd[0])
            load(wgk[:, 1, :], w_gk_bwd[0])
            load(wrt[:, :, :], w_router[0].rearrange("(k p) e -> p k e", p=P))
            load(rot[:, :, :, :].rearrange("p a t f -> p (a t f)"), rot_dram)
            for g, v in enumerate((g_pre_mix, g_post_mix, g_pre_ffn, g_post_ffn)):
                load(gbc[:, g, :], v.broadcast_to([P, D]))
            load(ggla[:, :], g_gla_out.broadcast_to([P, DV]))
            load(sinkb[:, :], attn_sink.broadcast_to([P, QH]))
            load(brt[:, :], b_router.broadcast_to([P, NE]))
            load(wlr[:, :, :], w_in[0, :, C_LR:C_LR + 2 * RANK].rearrange("(k p) n -> p k n", p=P))
            assert small == N_SMALL, small
            for j in range(3 * KD):
                n, k = divmod(j, KD)
                if j >= 4:
                    sp.wait_ge(ada_used, j - 3)
                sp.dma_start(ada_ring[:, j % 4, :], w_ada[0, k * P:(k + 1) * P, n * 2048:(n + 1) * 2048]).then_inc(ada_in[j % 4], 16)
                if j == 7:
                    sp.dma_start(X[:, 4:8, :], x[0, 512:1024, :].rearrange("(t p) d -> p t d", p=P)).then_inc(x_in, 16)
            for g, (_, c0, n, slot) in enumerate(groups):
                if g >= 2:
                    sp.wait_ge(pj_ps, (8, 20, 28)[g - 2])
                sp.dma_start(win_ring[:, slot, :, 0:n], w_in[0, :, c0:c0 + n].rearrange("(k p) n -> p k n", p=P)).then_inc(win_in[slot], 16)
            for b in range(NE, MAXB, NT):
                sp.dma_start(y_dram[b * BLK:(b + NT) * BLK, :].rearrange("(t p) d -> p t d", p=P), X[:, :, :]).then_inc(fill_st, 16)
            sp.wait_ge(gl_o, 32)
            sp.dma_start(wout_sb[:, :, :], w_out[0].rearrange("(k p) n -> p k n", p=P)).then_inc(wout_in, 16)
            sp.wait_ge(const_done, 1)
            sp.dma_start(tok_dram.rearrange("(p b) a -> p (b a)", p=P), ZI[:, :]).then_inc(zero_st, 16)
            for t in range(NT):
                sp.wait_ge(h2_row, t + 1)
                sp.dma_start(h2_dram[t * P:(t + 1) * P, :], xn2[:, t % 2, :]).then_inc(h2_st[t % 2], 16)

            def weights(e, before):
                for g in range(4):
                    if before is not None:
                        sp.wait_ge(gu_used[g], before)
                    sp.dma_start(wgu[:, 2 * g:2 * g + 2, :],
                                 w_gate_up[0, bass.ds(e, 1), g * 256:(g + 1) * 256, :].rearrange("a (k p) n -> p (a k) n", p=P)).then_inc(gu_in[g], 16)
                if before is not None:
                    sp.wait_ge(bi_used, before * 2)
                sp.dma_start(BI, b_gate_up[0, bass.ds(e, 1), :].broadcast_to([P, 2 * FF])).then_inc(bi_in, 16)
                for g in range(2):
                    if before is not None:
                        sp.wait_ge(dn_used[g], before)
                    sp.dma_start(wdn[:, 4 * g:4 * g + 4, :],
                                 w_down[0, bass.ds(e, 1), g * 512:(g + 1) * 512, :].rearrange("a (k p) n -> p (a k) n", p=P)).then_inc(dn_in[g], 16)

            sp.wait_ge(y_ps, NT)
            sp.wait_ge(plan_ready, 1)
            sp.wait_ge(gmt_r, 1)
            sp.dma_start(bdn[:, :], b_down[0]).then_inc(bdn_in, 16)
            weights(0, None)
            with sp.Fori(1, NE) as e:
                before = sp.value_load(CEI[0:1, bass.ds(e, 1)], min_val=1, max_val=MAXB)
                weights(e, before)
            for t in range(NT):
                sp.wait_ge(f_out, t + 1)
                sp.dma_start(out[0, t * P:(t + 1) * P, :], FO[:, t % 4, :]).then_inc(out_st[t % 4], 16)
            for b in range(4):
                sp.wait_ge(out_st[b], 32)

        @block.gpsimd
        def _(pl):
            n = 0

            def link(ins):
                nonlocal n
                n += 1
                ins.then_inc(pool, 1)
                pl.wait_ge(pool, n)

            def hold():
                pl.tensor_tensor(held[:, 0:1], mhalf[:, 0:1], mhalf[:, 1:2], ALU.mult).then_inc(held_done, 1)

            def rstd(dst, dim, ready):
                link(pl.tensor_scalar(dst, dst, 1.0 / dim, EPS, ALU.mult, ALU.add))
                pl.tensor_tensor(dst, dst, mhalf[:, 0:dst.shape[1]], ALU.pow).then_inc(ready, 1)

            link(pl.memset(acc, 0.0))
            link(pl.memset(mhalf[:, :], -0.5))
            pl.nop().then_inc(acc_zero, 1)
            link(pl.memset(ZI[:, :], 0))
            link(pl.memset(ident[:, :], 0.0))
            link(pl.memset(ones[:, :], 1.0))
            link(pl.memset(cmask[:, :, :], 1.0))
            link(pl.memset(tri[:, :], 1.0))
            link(pl.memset(amask[:, :, :], 0.0))
            link(pl.affine_select(out=ident[:, :], in_=ident[:, :], compare_op=ALU.not_equal, fill=1.0, base=0,
                                  pattern=[[-1, P]], channel_multiplier=1))
            link(pl.affine_select(out=tri[:, :], in_=tri[:, :], compare_op=ALU.is_gt, fill=0.0, base=0,
                                  pattern=[[1, P]], channel_multiplier=-1))
            link(pl.affine_select(out=cmask[:, 0, :], in_=cmask[:, 0, :], compare_op=ALU.is_ge, fill=0.0, base=0,
                                  pattern=[[1, P]], channel_multiplier=-1))
            link(pl.affine_select(out=cmask[:, 1, :], in_=cmask[:, 1, :], compare_op=ALU.is_ge, fill=0.0, base=0,
                                  pattern=[[-1, P]], channel_multiplier=1))
            link(pl.memset(cmask[0:CHUNK, :, CHUNK:P], 0.0))
            link(pl.memset(cmask[CHUNK:P, :, 0:CHUNK], 0.0))
            link(pl.affine_select(out=amask[:, 0, :], in_=amask[:, 0, :], compare_op=ALU.is_ge, fill=NEG, base=0,
                                  pattern=[[1, P]], channel_multiplier=-1))
            link(pl.affine_select(out=amask[:, 2, :], in_=amask[:, 2, :], compare_op=ALU.is_ge, fill=NEG, base=0,
                                  pattern=[[-1, P]], channel_multiplier=1))
            link(pl.iota(iot[:, :], pattern=[[1, 64]], base=0, channel_multiplier=0, allow_small_or_imprecise_dtypes=True))
            link(pl.iota(TI[:, :], pattern=[[P, NT]], base=0, channel_multiplier=1))
            pl.nop().then_inc(const_done, 1)
            for t in range(NT):
                pl.wait_ge(h_ssq, t + 1)
                rstd(st[:, t:t + 1], D, h_rstd)
            pl.wait_ge(pj_ev, 12 + 3 * NT)
            link(pl.memset(scanm, 1.0))
            link(pl.memset(scanm[:, 0:SEQ:CHUNK], 0.0))
            pl.nop().then_inc(scan_ready, 1)
            for t in range(NT):
                pl.wait_ge(og_ssq, t + 1)
                rstd(st[:, 48:52], DV, og_rstd)
            for t in range(NT):
                pl.wait_ge(y_ssq, t + 1)
                rstd(st[:, 16 + t:17 + t], D, y_rstd)
                pl.wait_ge(x1_ssq, t + 1)
                rstd(st[:, 24 + t:25 + t], D, x1_rstd)

            pl.wait_ge(plan_ready, 1)
            pl.wait_ge(zero_st, 16)
            for j in range(NT * TOPK):
                pl.indirect_dma_start(tok_dram, bass.IndirectOffsetOnAxis(ap=SLI[:, j:j + 1], axis=0),
                                      TI[:, j // TOPK:j // TOPK + 1], None).then_inc(tok_st, 16)
            pl.wait_ge(tok_st, 16 * NT * TOPK)
            for b in range(2):
                pl.wait_ge(h2_st[b], 16 * NT // 2)
            total = pl.value_load(CEI[0:1, NE:NE + 1], min_val=1, max_val=MAXB)
            hold()
            with pl.Fori(0, total + 1) as i:
                pl.wait_ge(held_done, i + 1)
                pl.wait_ge(tx_ps, i * 2 + 1)
                pl.dma_start(IX[:, :], tok_dram[bass.ds(i * BLK, BLK), :]).then_inc(ix_in, 16)
                pl.wait_ge(ix_in, i * 16 + 16)
                hold()
                pl.indirect_dma_start(XG, None, h2_dram, bass.IndirectOffsetOnAxis(ap=IX[:, 0:1], axis=0)).then_inc(xg_in, 16)
            def final_rstd(t):
                pl.wait_ge(f_ssq, t + 1)
                rstd(st[:, 40 + t:41 + t], D, f_rstd)

            for j in range(NT * TOPK):
                if j >= 16:
                    pl.wait_ge(f_acc, j - 15)
                    if j % TOPK == 0:
                        final_rstd(j // TOPK - 4)
                if j == 0:
                    pl.wait_ge(yb_st, total * 16 + 16)
                    pl.wait_ge(dn_used[1], total)
                    pl.wait_ge(held_done, total + 2)
                    hold()
                pl.indirect_dma_start(YR[:, j % 16, :], None, y_dram, bass.IndirectOffsetOnAxis(ap=SLI[:, j:j + 1], axis=0)).then_inc(yr_in[j % 16], 16)
            for t in range(NT - 4, NT):
                final_rstd(t)

        @block.tensor
        def _(pe):
            def tr(dst, src, n=P):
                return pe.transpose(dst, src, ident[0:n, 0:n])

            pe.wait_ge(const_done, 1)
            pe.wait_ge(small_in, 16 * N_SMALL)
            tr(PS[:, 0, 0:KD], cvec[:, :], KD)
            tr(PS[:, 0, 16:20], bgk[:, :], 4).then_inc(vec_T, 1)
            for n in range(12):
                if n % 4 == 0:
                    pe.wait_ge(ada_used, 8 * (n // 4) + 8)
                if n >= 6:
                    pe.wait_ge(mod_ready, n - 5)
                pe.matmul(PS[:, 1 + n % 6, :], ones[:, :], acc[:, n * 512:(n + 1) * 512], start=True, stop=True).then_inc(mod_ps, 1)
            for t in range(NT):
                pe.wait_ge(h_row, t + 1)
                if t == 0:
                    pe.wait_ge(mod_ready, 12)
                if t >= 2:
                    pe.wait_ge(h_ready, 2 * (t - 1))
                for k in range(KD):
                    m = tr(PS[:, 2 * (t % 2) + k // 4, (k % 4) * P:(k % 4 + 1) * P], xn[:, t % 2, k * P:(k + 1) * P])
                    if k % 4 == 3:
                        m.then_inc(h_tps, 1)
            j = 0

            def freed(q):
                if GJ <= q < GJ + NT:
                    pe.wait_ge(gg_done, q - GJ + 1)
                else:
                    pe.wait_ge(pj_ev, q + 1 - (NT if q >= GJ else 0))

            def bank():
                nonlocal j
                if j >= 6:
                    freed(j - 6)
                j += 1
                return (j - 1) % 6

            pe.wait_ge(h_ready, 2 * NT)
            for g, (what, c0, n, slot) in enumerate(groups):
                pe.wait_ge(win_in[slot], 16 * (g // 2 + 1))
                if what == "qk":
                    for a in range(4):
                        for s in range(2):
                            b = bank()
                            for k in range(KD):
                                m = pe.matmul(PS[:, b, :], win_ring[:, slot, k, a * P:(a + 1) * P], hT[:, k, s * 512:(s + 1) * 512],
                                              start=(k == 0), stop=(k == KD - 1))
                            m.then_inc(pj_ps, 1)
                    for d in range(2):
                        for s in range(2):
                            b = bank()
                            for k in range(KD):
                                m = pe.matmul(PS[0:RANK, b, :], wlr[:, k, d * RANK:(d + 1) * RANK], hT[:, k, s * 512:(s + 1) * 512],
                                              start=(k == 0), stop=(k == KD - 1))
                            m.then_inc(pj_ps, 1)
                else:
                    for t in range(NT):
                        b = bank()
                        for k in range(KD):
                            m = pe.matmul(PS[:, b, 0:n], hT[:, k, t * P:(t + 1) * P], win_ring[:, slot, k, 0:n],
                                          start=(k == 0), stop=(k == KD - 1))
                        m.then_inc(pj_ps, 1)
            freed(j - 1)
            for u in range(4):
                p, d = divmod(u, 2)
                for s in range(2):
                    if u:
                        pe.wait_ge(z_rd, 2 * (u - 1) + s + 1)
                        pe.wait_ge(gl_s, 17 * u)
                    pe.matmul(PS[:, 6 + s, :], wgk[:, d, p * P:(p + 1) * P], LR[:, d, s * 512:(s + 1) * 512],
                              start=True, stop=True).then_inc(z_ps, 1)
                base = 8 * u
                pe.wait_ge(gi_ready, u + 1)

                def first(i):
                    t = i if d == 0 else NT - 1 - i
                    n = base + i
                    ts = slice(t * P, (t + 1) * P)
                    if n:
                        pe.wait_ge(gl_ksr, n)
                        pe.wait_ge(gl_str, n)
                    tr(PS[:, 0, 0:P], GI[:, 3, ts]).then_inc(gl_ks, 1)
                    for h in range(2):
                        hs = slice(64 * h, 64 * h + 64)
                        m = pe.matmul(PS[:, 1 + 4 * h, 0:P], GI[hs, 1, ts], GI[hs, 0, ts], start=True, stop=True)
                    m.then_inc(gl_st, 1)

                for i in range(NT):
                    first(i)
                    t = i if d == 0 else NT - 1 - i
                    n = base + i
                    order = (0, 1) if d == 0 else (1, 0)
                    if n:
                        pe.wait_ge(gl_ev, n)
                    pe.wait_ge(gl_str, n + 1)
                    for h in range(2):
                        pe.matmul(PS[:, 2 + h, 0:P], ST[:, h, :], V[:, t, (2 * p + h) * DV:(2 * p + h + 1) * DV],
                                  start=True, stop=False, skip_group_check=True)
                    pe.wait_ge(gl_ksr, n + 1)
                    if n:
                        pe.wait_ge(gl_s, 2 * n + u + 1)
                    for q, ch in enumerate(order):
                        cs = slice(64 * ch, 64 * ch + 64)
                        for h in range(2):
                            m = pe.matmul(PS[64 * h:64 * h + 64, 4 + 2 * ch, 0:P], KS[cs, 64 * h:64 * h + 64],
                                          V[cs, t, (2 * p + h) * DV:(2 * p + h + 1) * DV], start=True, stop=True)
                        m.then_inc(gl_u, 1)
                    for q, ch in enumerate(order):
                        cs = slice(64 * ch, 64 * ch + 64)
                        pe.wait_ge(gl_s, 2 * n + u + 1 + q)
                        for h in range(2):
                            hs = slice(64 * h, 64 * h + 64)
                            m = pe.matmul(PS[cs, 2 + h, 0:P], GI[hs, 2, t * P + 64 * ch:t * P + 64 * ch + 64],
                                          S[hs, q, :], start=False, stop=True, skip_group_check=True)
                    m.then_inc(gl_o, 1)
            pe.wait_ge(gl_ev, 32)
            pe.wait_ge(rot_ready, 1)
            for t in range(NT):
                m = tr(PS[:, t // 4, (t % 4) * P:(t % 4 + 1) * P], AKV[:, t, 0:P])
                if t % 4 == 3:
                    m.then_inc(at_T, 1)
            pe.wait_ge(at_Tr, 2)
            pu = 0
            for t in range(NT):
                lo, hi = max(0, t - 1), min(NT, t + 2)
                n = (hi - lo) * P
                if t:
                    pe.wait_ge(at_sr, 8 * t)
                for cc in range(4):
                    m = tr(PS[:, 4, cc * P:(cc + 1) * P], AQ[:, t, cc * P:(cc + 1) * P])
                m.then_inc(at_T, 1)
                pe.wait_ge(at_Tr, 3 + t)
                for h in range(QH):
                    g, cc = divmod(h, 4)
                    i = 8 * t + h
                    if i >= 4:
                        pe.wait_ge(at_sr, i - 3)
                    gs = slice(64 * g, 64 * g + 64)
                    pe.matmul(PS[:, i % 4, 0:n], qT[gs, cc * P:(cc + 1) * P], kT[gs, lo * P:hi * P],
                              start=True, stop=True).then_inc(at_s, 1)
                for h in range(QH):
                    g = h // 4
                    i = 8 * t + h
                    pe.wait_ge(at_n, i + 1)
                    if i:
                        pe.wait_ge(at_pr, i)
                    for b in range(hi - lo):
                        m = tr(PS[:, 5, b * P:(b + 1) * P], SC[:, h, b * P:(b + 1) * P])
                    m.then_inc(at_p, 1)
                    pe.wait_ge(at_pr, i + 1)
                    if h % 2 == 0 and i >= 4:
                        pe.wait_ge(at_or, i // 2 - 1)
                    ob = 6 + (i // 2) % 2
                    for b in range(hi - lo):
                        m = pe.matmul(PS[64 * (h % 2):64 * (h % 2) + 64, ob, 0:P], AKV[:, lo + b, P + g * HD:P + (g + 1) * HD],
                                      PTv[i % 2][:, b * P:(b + 1) * P],
                                      start=(b == 0), stop=(b == hi - lo - 1))
                    if h % 2:
                        m.then_inc(at_o, 1)
            for t in range(NT):
                pe.wait_ge(og_ready, t + 1)
                if t >= 2:
                    pe.wait_ge(og_Tr, t - 1)
                else:
                    pe.wait_ge(at_or, 32)
                for k in range(4):
                    m = tr(PS[:, t % 2, k * P:(k + 1) * P], O[:, t, k * P:(k + 1) * P])
                m.then_inc(og_T, 1)
            pe.wait_ge(og_Tr, NT)
            pe.wait_ge(wout_in, 16)

            def h2_part(t):
                pe.wait_ge(h2_row, t + 1)
                if t:
                    pe.wait_ge(h2_tr, 2 * t)
                for k in range(KD):
                    m = tr(PS[:, 4 + k // 4, (k % 4) * P:(k % 4 + 1) * P], xn2[:, t % 2, k * P:(k + 1) * P])
                    if k % 4 == 3:
                        m.then_inc(h2_tps, 1)
                pe.wait_ge(h2_tr, 2 * t + 2)
                if t:
                    pe.wait_ge(lg_ready, t)
                for k in range(KD):
                    m = pe.matmul(PS[:, 6, 0:NE], h2T[:, k, :], wrt[:, k, :], start=(k == 0), stop=(k == KD - 1))
                m.then_inc(lg_ps, 1)

            for t in range(NT):
                if t >= 2:
                    pe.wait_ge(x1_ready, t - 1)
                for k in range(KD):
                    for s in range(2):
                        m = pe.matmul(PS[:, 2 * (t % 2) + s, :], OT[:, k, t * P:(t + 1) * P], wout_sb[:, k, s * 512:(s + 1) * 512],
                                      start=(k == 0), stop=(k == KD - 1))
                m.then_inc(y_ps, 1)
                if t:
                    h2_part(t - 1)
            h2_part(NT - 1)
            pe.wait_ge(mk_ready, 1)
            pe.matmul(PS[:, 0, 0:256], ones[:, :], MK[:, :, :].rearrange("p t e -> p (t e)"), start=True, stop=True)
            pe.matmul(PS[:, 1, 0:256], tri[:, :], MK[:, :, :].rearrange("p t e -> p (t e)"), start=True, stop=True).then_inc(po_ps, 1)
            for t in range(NT):
                m = tr(PS[0:NE, 2 + t // 4, (t % 4) * P:(t % 4 + 1) * P], GM[:, t, :])
            m.then_inc(gmt_ps, 1)
            pe.wait_ge(plan_ready, 1)
            pe.wait_ge(gmt_r, 1)

            def x_T(half, bk):
                for k in range(4):
                    m = tr(PS[:, bk, k * P:(k + 1) * P], XG[:, (4 * half + k) * P:(4 * half + k + 1) * P])
                m.then_inc(tx_ps, 1)
                return m

            total = pe.value_load(CEI[0:1, NE:NE + 1], min_val=1, max_val=MAXB)
            pe.nop().then_inc(tx_ps, 1)
            pe.wait_ge(xg_in, 16)
            x_T(0, 7)
            x_T(1, 6)
            with pe.Fori(0, total) as i:
                e1 = pe.value_load(EBI[0:1, bass.ds(i, 1)], min_val=1, max_val=NE)
                pe.wait_ge(tx_ready, i * 2 + 2)
                for h in range(2):
                    pe.wait_ge(gu_m, i * 2 + h + 1)
                    for k in range(KD):
                        if h == 0 and k % 2 == 0:
                            pe.wait_ge(gu_in[k // 2], e1 * 16)
                        for a in range(2):
                            m = pe.matmul(PS[:, 2 * h + a, :], XT[:, k, :], wgu[:, k, a * FF + h * 512:a * FF + (h + 1) * 512],
                                          start=(k == 0), stop=(k == KD - 1))
                        if h == 1 and k % 2 == 1:
                            m.then_inc(gu_used[k // 2], 1)
                    if h == 0:
                        m.then_inc(gu_ps, 1)
                pe.wait_ge(ab_ready, i * 2 + 2)
                for k in range(4):
                    m = tr(PS[:, 6, k * P:(k + 1) * P], AB[:, 0, k * P:(k + 1) * P])
                m.then_inc(ta_ps, 1)
                pe.wait_ge(xg_in, i * 16 + 32)
                pe.wait_ge(ta_ready, i * 2 + 1)
                x_T(0, 7)
                pe.wait_ge(yb_rd, i + 1)
                pe.wait_ge(ta_ready, i * 2 + 2)
                pe.wait_ge(dn_in[0], e1 * 16)

                def down(k0, k1):
                    for k in range(k0, k1):
                        for s in range(2):
                            m = pe.matmul(PS[:, 4 + s, :], AT[:, k, :], wdn[:, k, s * 512:(s + 1) * 512],
                                          start=(k == 0), stop=(k == KD - 1))
                    return m

                down(0, 2)
                x_T(1, 6)
                down(2, 4).then_inc(dn_used[0], 1)
                pe.wait_ge(ab_ready, i * 2 + 3)
                pe.wait_ge(tx_ready, i * 2 + 3)
                for k in range(4):
                    m = tr(PS[:, 7, k * P:(k + 1) * P], AB[:, 1, k * P:(k + 1) * P])
                m.then_inc(ta_ps, 1)
                pe.wait_ge(ta_ready, i * 2 + 3)
                pe.wait_ge(dn_in[1], e1 * 16)
                down(4, KD).then_inc(dn_used[1], 1)
            for t in range(NT):
                if t == 0:
                    pe.wait_ge(yb_rd, total + 1)
                    pe.wait_ge(bdn_in, 16)
                if t >= 4:
                    pe.wait_ge(f_acc, 4 * (t - 3))
                for s in range(2):
                    m = pe.matmul(PS[:, 2 * (t % 4) + s, :], GMT[:, t, :], bdn[:, s * 512:(s + 1) * 512], start=True, stop=True)
                m.then_inc(bd_ps, 1)

        @block.scalar
        def _(a):
            n = 0

            def link(ins):
                nonlocal n
                n += 1
                ins.then_inc(act, 1)
                a.wait_ge(act, n)

            a.wait_ge(c_ready, 1)
            a.activation(cT[:, 1, :], cT[:, 0, :], ACT.Sigmoid).then_inc(silu_sig, 1)
            for t in range(NT):
                a.wait_ge(x_in, 16 if t < 4 else 32)
                if t == 0:
                    a.wait_ge(mod_ready, 12)
                link(a.activation(SQ[:, :], X[:, t, :], ACT.Square, accum_out=st[:, t:t + 1]))
                a.nop().then_inc(h_ssq, 1)
            for t in range(NT):
                for s in range(2):
                    a.wait_ge(h_tps, 2 * t + s + 1)
                    a.activation(hT[:, 4 * s:4 * s + 4, t * P:(t + 1) * P],
                                 PS[:, 2 * (t % 2) + s, :].rearrange("p (k s) -> p k s", k=4), ACT.Copy).then_inc(h_ready, 1)
            j = 0
            for g, (what, c0, nn, slot) in enumerate(groups):
                if what == "qk":
                    for aa in range(4):
                        for s in range(2):
                            a.wait_ge(pj_ps, j + 1)
                            a.activation(QKT[:, aa, s * 512:(s + 1) * 512], PS[:, j % 6, :], ACT.Copy,
                                         scale=(DK ** -0.5 if aa < 2 else 1.0)).then_inc(pj_ev, 1)
                            j += 1
                    for d in range(2):
                        for s in range(2):
                            a.wait_ge(pj_ps, j + 1)
                            a.activation(LR[:, d, s * 512:(s + 1) * 512], PS[0:RANK, j % 6, :], ACT.Copy).then_inc(pj_ev, 1)
                            j += 1
                    continue
                for t in range(NT):
                    a.wait_ge(pj_ps, j + 1)
                    if what == "v":
                        a.activation(V[:, t, :], PS[:, j % 6, :], ACT.Copy).then_inc(pj_ev, 1)
                    elif what == "g":
                        a.activation(GG[:, t, :], PS[:, j % 6, :], ACT.Sigmoid).then_inc(gg_sig, 1)
                    elif what == "aq":
                        a.activation(AQ[:, t, :].rearrange("p (c g d) -> p g c d", c=4, g=2),
                                     PS[:, j % 6, :].rearrange("p (g c d) -> p g c d", g=2, c=4), ACT.Copy).then_inc(pj_ev, 1)
                    else:
                        a.activation(AKV[:, t, :], PS[:, j % 6, 0:256], ACT.Copy).then_inc(pj_ev, 1)
                    j += 1
            gla = [0]
            for u in range(4):
                a.wait_ge(z_rd, 2 * u + 2)
                a.wait_ge(z_exp, u + 1)
                link(a.activation(GI[:, 5, :], GI[:, 5, :], ACT.Exp, scale=-1.0))
                a.activation(GI[:, 5, :], GI[:, 5, :], ACT.Ln, bias=1.0).then_inc(z_ln, 1)
                a.wait_ge(ex_in, 4 * u + 1)
                a.activation(GI[:, 0, :], GI[:, 6, :], ACT.Exp, scale=1.0 / 16).then_inc(ex_out, 1)
                a.activation(GI[:, 1, :], GI[:, 6, :], ACT.Exp, scale=-1.0 / 16).then_inc(ex_out, 1)
                a.activation(GI[:, 2, :], GI[:, 4, :], ACT.Exp, scale=1.0 / 16).then_inc(ex_out, 1)
                a.wait_ge(ex_in, 4 * u + 2)
                a.activation(GI[:, 3, :], GI[:, 7, :], ACT.Exp, scale=1.0 / 16).then_inc(ex_out, 1)
                last = CHUNK - 1 if u % 2 == 0 else 0
                a.activation(dec[:, :], GI[:, 4, last:SEQ:CHUNK], ACT.Exp, scale=1.0 / 16).then_inc(ex_out, 1)
                for i in range(NT):
                    m = 8 * u + i
                    a.wait_ge(gl_ks, m + 1)
                    if m:
                        a.wait_ge(gl_u, 2 * m)
                    a.activation(KS[:, :], PS[:, 0, 0:P], ACT.Copy).then_inc(gl_ksr, 1)
            for b in range(2):
                a.wait_ge(at_T, b + 1)
                a.activation(kT[:, b * 512:(b + 1) * 512], PS[:, b, :], ACT.Copy).then_inc(at_Tr, 1)
            for t in range(NT):
                nn = (min(NT, t + 2) - max(0, t - 1)) * P
                a.wait_ge(at_T, 3 + t)
                a.activation(qT, PS[:, 4, :], ACT.Copy).then_inc(at_Tr, 1)
                a.wait_ge(at_m, t + 1)
                for h in range(QH):
                    a.activation(SC[:, h, 0:nn], SC[:, h, 0:nn], ACT.Exp, bias=am[:, 1, h:h + 1], accum_out=am[:, 2, h:h + 1]).then_inc(at_e, 1)
                a.activation(am[:, 4, :], am[:, 3, :], ACT.Exp).then_inc(at_e, 1)
                for h in range(QH):
                    i = 8 * t + h
                    a.wait_ge(at_p, i + 1)
                    if i >= 4:
                        a.wait_ge(at_o, i // 2 - 1)
                    a.activation(PTv[i % 2][:, 0:nn], PS[:, 5, 0:nn], ACT.Copy).then_inc(at_pr, 1)
                    if h % 2:
                        a.wait_ge(at_o, i // 2 + 1)
                        a.activation(OT[:, 4 + h // 2, t * P:(t + 1) * P], PS[:, 6 + (i // 2) % 2, 0:P], ACT.Copy).then_inc(at_or, 1)
            for t in range(NT):
                a.wait_ge(og_T, t + 1)
                a.activation(OT[:, 0:4, t * P:(t + 1) * P], PS[:, t % 2, :].rearrange("p (k s) -> p k s", k=4), ACT.Copy).then_inc(og_Tr, 1)

            def x1_part(t):
                a.wait_ge(x1_ready, t + 1)
                link(a.activation(SQ[:, :], X[:, t, :], ACT.Square, accum_out=st[:, 24 + t:25 + t]))
                a.nop().then_inc(x1_ssq, 1)
                for s in range(2):
                    a.wait_ge(h2_tps, 2 * t + s + 1)
                    if t:
                        a.wait_ge(lg_ps, t)
                    a.activation(h2T[:, 4 * s:4 * s + 4, :], PS[:, 4 + s, :].rearrange("p (k s) -> p k s", k=4), ACT.Copy).then_inc(h2_tr, 1)

            for t in range(NT):
                a.wait_ge(y_ps, t + 1)
                link(a.activation(SQ[:, :].rearrange("p (a n) -> p a n", a=2), PS[:, 2 * (t % 2):2 * (t % 2) + 2, :], ACT.Square,
                                  accum_out=st[:, 16 + t:17 + t]))
                a.nop().then_inc(y_ssq, 1)
                if t:
                    x1_part(t - 1)
            x1_part(NT - 1)
            a.wait_ge(g_exp, 1)
            link(a.activation(GT8[:, :, :], GT8[:, :, :], ACT.Exp))
            a.nop().then_inc(g_exp, 1)
            a.wait_ge(gmt_ps, 1)
            a.activation(GMT[:, :, :].rearrange("p (b t) s -> p b (t s)", b=2), PS[0:NE, 2:4, :], ACT.Copy).then_inc(gmt_r, 1)

            a.wait_ge(plan_ready, 1)
            total = a.value_load(CEI[0:1, NE:NE + 1], min_val=1, max_val=MAXB)

            def x_ev(half, bk, count):
                a.wait_ge(tx_ps, count)
                a.activation(XT[:, 4 * half:4 * half + 4, :], PS[:, bk, :].rearrange("p (k s) -> p k s", k=4), ACT.Copy).then_inc(tx_ready, 1)

            a.wait_ge(fill_st, N_FILL)
            a.nop().then_inc(ta_ready, 1)
            a.nop().then_inc(yb_rd, 1)
            a.nop().then_inc(yb_st, 16)
            x_ev(0, 7, 2)
            x_ev(1, 6, 3)
            with a.Fori(0, total) as i:
                for h in range(2):
                    a.wait_ge(gu_g, i * 2 + h + 1)
                    a.wait_ge(ab_ready, i * 2 + h + 1)
                    a.activation(SG[:, h, :], GS[:, h, :], ACT.Sigmoid, scale=ALPHA).then_inc(gu_sig, 1)
                a.wait_ge(ta_ps, i * 2 + 1)
                a.activation(AT[:, 0:4, :], PS[:, 6, :].rearrange("p (k s) -> p k s", k=4), ACT.Copy).then_inc(ta_ready, 1)
                x_ev(0, 7, i * 2 + 4)
                x_ev(1, 6, i * 2 + 5)
                a.wait_ge(ta_ps, i * 2 + 2)
                a.activation(AT[:, 4:8, :], PS[:, 7, :].rearrange("p (k s) -> p k s", k=4), ACT.Copy).then_inc(ta_ready, 1)
                a.wait_ge(dn_used[1], i + 1)
                a.wait_ge(yb_st, i * 16 + 16)
                a.activation(YS.rearrange("p (a n) -> p a n", a=2), PS[:, 4:6, :], ACT.Copy).then_inc(yb_rd, 1)
                a.wait_ge(yb_rd, i + 2)
                a.dma_start(y_dram[bass.ds(i * BLK, BLK), :], YS).then_inc(yb_st, 16)
            for t in range(NT):
                a.wait_ge(f_acc, 4 * (t + 1))
                link(a.activation(SQ[:, :], FO[:, t % 4, :], ACT.Square, accum_out=st[:, 40 + t:41 + t]))
                a.nop().then_inc(f_ssq, 1)

        @block.vector
        def _(v):
            n = 0

            def link(ins):
                nonlocal n
                n += 1
                ins.then_inc(dve, 1)
                v.wait_ge(dve, n)

            v.wait_ge(vec_T, 1)
            link(v.tensor_copy(cT[:, 0, :], PS[:, 0, 0:KD]))
            link(v.tensor_copy(bgT[:, :], PS[:, 0, 16:20]))
            v.nop().then_inc(c_ready, 1)
            v.wait_ge(silu_sig, 1)
            link(v.tensor_tensor(cT[:, 0, :], cT[:, 0, :], cT[:, 1, :], ALU.mult))
            v.wait_ge(bada_in, 16)
            for j in range(3 * KD):
                nn, k = divmod(j, KD)
                v.wait_ge(ada_in[j % 4], 16 * (j // 4 + 1))
                if k:
                    v.wait_ge(ada_used, j)
                ac = acc[:, nn * 2048:(nn + 1) * 2048]
                v.scalar_tensor_tensor(out=ac, in0=ada_ring[:, j % 4, :], scalar=cT[:, 0, k:k + 1], in1=ac,
                                       op0=ALU.mult, op1=ALU.add).then_inc(ada_used, 1)
            for m in range(12):
                v.wait_ge(mod_ps, m + 1)
                what, s = divmod(m, 2)
                hs = slice(s * 512, (s + 1) * 512)
                src = PS[:, 1 + m % 6, :]
                if what in (0, 3):
                    ins = v.tensor_copy((SH1 if what == 0 else SH2)[:, hs], src)
                elif what in (1, 4):
                    ins = v.scalar_tensor_tensor(out=(S1 if what == 1 else S2)[:, hs], in0=src, scalar=1.0,
                                                 in1=gbc[:, 0 if what == 1 else 2, hs], op0=ALU.add, op1=ALU.mult)
                else:
                    ins = v.tensor_tensor((GP1 if what == 2 else GP2)[:, hs], src, gbc[:, 1 if what == 2 else 3, hs], ALU.mult)
                ins.then_inc(mod_ready, 1)
            v.wait_ge(mod_ready, 12)
            for t in range(NT):
                v.wait_ge(h_rstd, t + 1)
                if t >= 2:
                    v.wait_ge(h_tps, 2 * (t - 1))
                link(v.scalar_tensor_tensor(out=xn[:, t % 2, :], in0=X[:, t, :], scalar=st[:, t:t + 1], in1=S1, op0=ALU.mult, op1=ALU.mult))
                v.tensor_tensor(xn[:, t % 2, :], xn[:, t % 2, :], SH1, ALU.add).then_inc(h_row, 1)
            for t in range(NT):
                j = GJ + t
                v.wait_ge(gg_sig, t + 1)
                link(v.tensor_tensor(GG[:, t, :], PS[:, j % 6, :], GG[:, t, :], ALU.mult))
                v.nop().then_inc(gg_done, 1)
                v.tensor_tensor(GG[:, t, :].rearrange("p (h n) -> p h n", h=HEADS), GG[:, t, :].rearrange("p (h n) -> p h n", h=HEADS),
                                ggla[:, :].unsqueeze(1).broadcast_to([P, HEADS, DV]), ALU.mult).then_inc(dve, 1)
                n += 1
            chv = lambda ap: ap.rearrange("p (c s) -> p c s", s=CHUNK)
            for u in range(4):
                p, d = divmod(u, 2)
                if u:
                    v.wait_ge(gl_o, 8 * u)
                for s in range(2):
                    v.wait_ge(z_ps, 2 * u + s + 1)
                    v.tensor_scalar(GI[:, 4, s * 512:(s + 1) * 512], PS[:, 6 + s, :], bgT[:, 2 * d + p:2 * d + p + 1], None, ALU.add).then_inc(z_rd, 1)
                v.wait_ge(z_rd, 2 * u + 2)
                link(v.scalar_tensor_tensor(out=GI[:, 5, :], in0=GI[:, 4, :], scalar=-1.0, in1=GI[:, 4, :], op0=ALU.mult, op1=ALU.max))
                v.nop().then_inc(z_exp, 1)
                v.wait_ge(z_ln, u + 1)
                link(v.scalar_tensor_tensor(out=GI[:, 7, :], in0=GI[:, 4, :], scalar=0.0, in1=GI[:, 5, :], op0=ALU.min, op1=ALU.subtract))
                if u == 0:
                    v.wait_ge(scan_ready, 1)
                link(v.tensor_tensor_scan(GI[:, 6, :], scanm[:, :], GI[:, 7, :], 0.0, ALU.mult, ALU.add))
                if d == 0:
                    link(v.tensor_copy(GI[:, 4, :], GI[:, 6, :]))
                    ref, last = CHUNK // 2 - 1, CHUNK - 1
                else:
                    link(v.tensor_tensor(GI[:, 5, :], GI[:, 7, :], GI[:, 6, :], ALU.subtract))
                    link(v.tensor_tensor(chv(GI[:, 4, :]), chv(GI[:, 5, :]), chv(GI[:, 6, :])[:, :, CHUNK - 1:CHUNK].broadcast_to([P, NCH, CHUNK]), ALU.add))
                    ref, last = CHUNK // 2, 0
                b = chv(GI[:, 4, :])
                link(v.tensor_tensor(chv(GI[:, 6, :]), b, b[:, :, ref:ref + 1].broadcast_to([P, NCH, CHUNK]), ALU.subtract))
                v.nop().then_inc(ex_in, 1)
                link(v.tensor_tensor(chv(GI[:, 7, :]), b[:, :, last:last + 1].broadcast_to([P, NCH, CHUNK]), b, ALU.subtract))
                v.nop().then_inc(ex_in, 1)
                q, k = QKT[:, p, :], QKT[:, 2 + p, :]
                v.wait_ge(ex_out, 5 * u + 5)
                v.nop().then_inc(ex_in, 2)
                link(v.tensor_tensor(GI[:, 0, :], GI[:, 0, :], q, ALU.mult))
                link(v.tensor_tensor(GI[:, 1, :], GI[:, 1, :], k, ALU.mult))
                link(v.tensor_tensor(GI[:, 2, :], GI[:, 2, :], q, ALU.mult))
                link(v.tensor_tensor(GI[:, 3, :], GI[:, 3, :], k, ALU.mult))
                v.nop().then_inc(gi_ready, 1)
                v.memset(S[:, 0, :], 0.0).then_inc(gl_s, 1)
                for i in range(NT):
                    t = i if d == 0 else NT - 1 - i
                    m = 8 * u + i
                    v.wait_ge(gl_st, m + 1)
                    v.tensor_tensor(ST[:, :, :], PS[:, 1:6:4, 0:P],
                                    cmask[:, d, :].unsqueeze(1).broadcast_to([P, 2, P]), ALU.mult).then_inc(gl_str, 1)
                    for qq, ch in enumerate((0, 1) if d == 0 else (1, 0)):
                        v.wait_ge(gl_u, 2 * m + qq + 1)
                        v.wait_ge(gl_s, 2 * m + u + 1 + qq)
                        if qq == 1:
                            v.wait_ge(gl_o, m + 1)
                        v.scalar_tensor_tensor(out=S[:, 1 - qq, :], in0=S[:, qq, :], scalar=dec[:, 2 * t + ch:2 * t + ch + 1],
                                               in1=PS[:, 4 + 2 * ch, 0:P], op0=ALU.mult, op1=ALU.add).then_inc(gl_s, 1)
                    v.wait_ge(gl_o, m + 1)
                    o = O[:, t, 2 * p * DV:(2 * p + 2) * DV].rearrange("p (h n) -> p h n", h=2)
                    src = PS[:, 2:4, 0:P]
                    if d == 0:
                        v.tensor_copy(o, src).then_inc(gl_ev, 1)
                    else:
                        v.tensor_tensor(o, src, o, ALU.add).then_inc(gl_ev, 1)
            v.wait_ge(gl_ev, 32)
            for t in range(NT):
                o = O[:, t, :].rearrange("p (h n) -> p h n", h=HEADS)
                tmp = XS[:, 0:512].rearrange("p (h n) -> p h n", h=HEADS)
                link(v.tensor_tensor(tmp, o, o, ALU.mult))
                v.tensor_reduce(st[:, 48:52], tmp, AX.X, ALU.add).then_inc(og_ssq, 1)
                v.wait_ge(og_rstd, t + 1)
                link(v.tensor_tensor(o, o, st[:, 48:52].unsqueeze(2).broadcast_to([P, HEADS, DV]), ALU.mult))
                v.tensor_tensor(O[:, t, :], O[:, t, :], GG[:, t, :], ALU.mult).then_inc(og_ready, 1)
            cos, sin = rot[:, 0, :, :], rot[:, 1, :, :]
            for buf, nh in ((AQ[:, :, :], QH), (AKV[:, :, 0:P], KVH)):
                hv = buf.rearrange("p t (h d) -> p t h d", d=HD)
                for h in range(nh):
                    x1, x2 = hv[:, :, h, 0:HALF], hv[:, :, h, HALF:ROT]
                    v.tensor_tensor(rtmp[:, 0, :, :], x1, cos, ALU.mult)
                    v.tensor_tensor(rtmp[:, 1, :, :], x2, sin, ALU.mult)
                    v.tensor_tensor(rtmp[:, 2, :, :], x2, cos, ALU.mult)
                    link(v.tensor_tensor(rtmp[:, 3, :, :], x1, sin, ALU.mult))
                    v.tensor_tensor(x1, rtmp[:, 0, :, :], rtmp[:, 1, :, :], ALU.subtract)
                    link(v.tensor_tensor(x2, rtmp[:, 2, :, :], rtmp[:, 3, :, :], ALU.add))
            v.nop().then_inc(rot_ready, 1)
            for t in range(NT):
                lo, hi = max(0, t - 1), min(NT, t + 2)
                nn = (hi - lo) * P
                am0 = lo - (t - 1)
                for h in range(QH):
                    i = 8 * t + h
                    v.wait_ge(at_s, i + 1)
                    if t:
                        v.wait_ge(at_p, i - 7)
                    v.scalar_tensor_tensor(out=SC[:, h, 0:nn].rearrange("p (b n) -> p b n", n=P),
                                           in0=PS[:, i % 4, 0:nn].rearrange("p (b n) -> p b n", n=P), scalar=HD ** -0.5,
                                           in1=amask[:, am0:am0 + hi - lo, :], op0=ALU.mult, op1=ALU.add).then_inc(at_sr, 1)
                v.wait_ge(at_sr, 8 * t + 8)
                link(v.tensor_reduce(am[:, 0, :], SC[:, :, 0:nn], AX.X, ALU.max))
                link(v.tensor_tensor(am[:, 0, :], am[:, 0, :], sinkb[:, :], ALU.max))
                link(v.tensor_scalar(am[:, 1, :], am[:, 0, :], -1.0, None, ALU.mult))
                link(v.tensor_tensor(am[:, 3, :], sinkb[:, :], am[:, 0, :], ALU.subtract))
                v.nop().then_inc(at_m, 1)
                v.wait_ge(at_e, 9 * t + 9)
                link(v.tensor_tensor(am[:, 5, :], am[:, 2, :], am[:, 4, :], ALU.add))
                link(v.reciprocal(am[:, 5, :], am[:, 5, :]))
                for h in range(QH):
                    v.tensor_scalar(SC[:, h, 0:nn], SC[:, h, 0:nn], am[:, 5, h:h + 1], None, ALU.mult).then_inc(at_n, 1)
            v.wait_ge(fill_st, N_FILL)
            for t in range(NT):
                v.wait_ge(y_rstd, t + 1)
                for s in range(2):
                    v.scalar_tensor_tensor(out=XS[:, s * 512:(s + 1) * 512], in0=PS[:, 2 * (t % 2) + s, :], scalar=st[:, 16 + t:17 + t],
                                           in1=GP1[:, s * 512:(s + 1) * 512], op0=ALU.mult, op1=ALU.mult).then_inc(dve, 1)
                n += 2
                v.wait_ge(dve, n)
                v.tensor_tensor(X[:, t, :], X[:, t, :], XS[:, :], ALU.add).then_inc(x1_ready, 1)
                v.wait_ge(x1_rstd, t + 1)
                if t >= 2:
                    v.wait_ge(h2_tps, 2 * (t - 1))
                    v.wait_ge(h2_st[t % 2], 16 * (t // 2))
                link(v.scalar_tensor_tensor(out=xn2[:, t % 2, :], in0=X[:, t, :], scalar=st[:, 24 + t:25 + t], in1=S2, op0=ALU.mult, op1=ALU.mult))
                link(v.tensor_tensor(xn2[:, t % 2, :], xn2[:, t % 2, :], SH2, ALU.add))
                v.nop().then_inc(h2_row, 1)
                v.wait_ge(lg_ps, t + 1)
                link(v.tensor_tensor(LG[:, t, :], PS[:, 6, 0:NE], brt[:, :], ALU.add))
                v.nop().then_inc(lg_ready, 1)
                link(v.max(M8[:, t, :], LG[:, t, :]))
                link(v.max_index(I8[:, t, :], M8[:, t, :], LG[:, t, :]))
            link(v.tensor_copy(IF[:, :, :], I8[:, :, 0:TOPK]))
            link(v.tensor_tensor(GT8[:, :, :], M8[:, :, 0:TOPK], M8[:, :, 0:1].broadcast_to([P, NT, TOPK]), ALU.subtract))
            v.nop().then_inc(g_exp, 1)
            for t in range(NT):
                v.tensor_tensor(OH[:, t, :, :], iot[:, 0:NE].unsqueeze(1).broadcast_to([P, TOPK, NE]),
                                IF[:, t, :].unsqueeze(2).broadcast_to([P, TOPK, NE]), ALU.is_equal).then_inc(dve, 1)
                n += 1
            v.wait_ge(dve, n)
            link(v.tensor_reduce(MK[:, :, :], OH[:, :, :, :].rearrange("p t k e -> p t e k"), AX.X, ALU.add))
            v.wait_ge(g_exp, 2)
            link(v.tensor_reduce(gsum[:, 0, :], GT8[:, :, :], AX.X, ALU.add))
            link(v.reciprocal(gsum[:, 1, :], gsum[:, 0, :]))
            link(v.tensor_tensor(GT8[:, :, :], GT8[:, :, :], gsum[:, 1, :].unsqueeze(2).broadcast_to([P, NT, TOPK]), ALU.mult))
            link(v.tensor_tensor(OM, OH[:, :, :, :], GT8[:, :, :].unsqueeze(3).broadcast_to([P, NT, TOPK, NE]), ALU.mult))
            link(v.tensor_reduce(GM[:, :, :], OM.rearrange("p t k e -> p t e k"), AX.X, ALU.add))
            v.nop().then_inc(mk_ready, 1)
            v.wait_ge(po_ps, 1)
            tot = PS[:, 0, 0:256].rearrange("p (t e) -> p t e", t=NT)
            link(v.tensor_copy(PO[:, :, :], PS[:, 1, 0:256].rearrange("p (t e) -> p t e", t=NT)))
            link(v.tensor_copy(cn[:, 0, :], tot[:, 0, :]))
            for t in range(1, NT):
                link(v.tensor_tensor(PO[:, t, :], PO[:, t, :], cn[:, 0, :], ALU.add))
                link(v.tensor_tensor(cn[:, 0, :], tot[:, t, :], cn[:, 0, :], ALU.add))
            link(v.tensor_scalar(cn[:, 1, :], cn[:, 0, :], float(BLK), 1.0, ALU.is_gt, ALU.add))
            for m in range(2, SEQ // BLK):
                link(v.scalar_tensor_tensor(out=cn[:, 1, :], in0=cn[:, 0, :], scalar=float(m * BLK), in1=cn[:, 1, :], op0=ALU.is_gt, op1=ALU.add))
            link(v.tensor_tensor_scan(cn[:, 2, :], ones[:, 0:NE], cn[:, 1, :], 0.0, ALU.mult, ALU.add))
            link(v.tensor_tensor(cn[:, 3, :], cn[:, 2, :], cn[:, 1, :], ALU.subtract))
            link(v.tensor_copy(CEI[:, 0:NE], cn[0:1, 3, :]))
            link(v.tensor_copy(CEI[:, NE:NE + 1], cn[0:1, 2, NE - 1:NE]))
            link(v.tensor_scalar(cn[:, 3, :], cn[:, 3, :], float(BLK), None, ALU.mult))
            link(v.tensor_tensor(PO[:, :, :], PO[:, :, :], cn[:, 3, :].unsqueeze(1).broadcast_to([P, NT, NE]), ALU.add))
            for t in range(NT):
                v.tensor_tensor(OM[:, t], OH[:, t, :, :], PO[:, t, :].unsqueeze(1).broadcast_to([P, TOPK, NE]), ALU.mult).then_inc(dve, 1)
                n += 1
            v.wait_ge(dve, n)
            link(v.tensor_reduce(SL[:, :, :], OM, AX.X, ALU.add))
            link(v.tensor_copy(SLI[:, :], SL[:, :, :].rearrange("p t k -> p (t k)")))
            eb = OMX[0:1, :].rearrange("p (b e) -> p b e", e=NE)
            link(v.tensor_tensor(eb, cn[0:1, 2, :].unsqueeze(1).broadcast_to([1, MAXB, NE]),
                                 iot[0:1, 0:MAXB].unsqueeze(2).broadcast_to([1, MAXB, NE]), ALU.is_le))
            link(v.tensor_reduce(EB[:, :], eb, AX.X, ALU.add))
            link(v.tensor_scalar(EB[:, :], EB[:, :], float(NE - 1), 1.0, ALU.min, ALU.add))
            link(v.tensor_copy(EBI[:, :], EB[:, :]))
            v.nop().then_inc(plan_ready, 1)

            total = v.value_load(CEI[0:1, NE:NE + 1], min_val=1, max_val=MAXB)
            v.nop().then_inc(gu_m, 1)
            v.nop().then_inc(ab_ready, 1)
            with v.Fori(0, total) as i:
                e1 = v.value_load(EBI[0:1, bass.ds(i, 1)], min_val=1, max_val=NE)
                v.wait_ge(bi_in, e1 * 16)
                for h in range(2):
                    hs = slice(h * 512, (h + 1) * 512)
                    v.wait_ge(gu_used[3] if h else gu_ps, i + 1)
                    v.tensor_tensor(GS[:, h, :], PS[:, 2 * h, :], BI[:, h * 512:(h + 1) * 512], ALU.add).then_inc(gu_add, 1)
                    v.tensor_tensor(US[:, h, :], PS[:, 2 * h + 1, :], BI[:, FF + h * 512:FF + (h + 1) * 512], ALU.add).then_inc(gu_m, 1)
                    v.wait_ge(gu_add, i * 2 + h + 1)
                    v.tensor_scalar(GS[:, h, :], GS[:, h, :], LIMIT, None, ALU.min).then_inc(gu_g, 1)
                    v.wait_ge(gu_m, i * 2 + h + 2)
                    v.nop().then_inc(bi_used, 1)
                    v.tensor_scalar(US[:, h, :], US[:, h, :], LIMIT, -LIMIT, ALU.min, ALU.max).then_inc(gu_c, 1)
                    v.wait_ge(gu_g, i * 2 + h + 1)
                    v.wait_ge(gu_c, i * 4 + 2 * h + 1)
                    v.scalar_tensor_tensor(out=US[:, h, :], in0=US[:, h, :], scalar=1.0, in1=GS[:, h, :], op0=ALU.add, op1=ALU.mult).then_inc(gu_c, 1)
                    v.wait_ge(gu_c, i * 4 + 2 * h + 2)
                    v.wait_ge(gu_sig, i * 2 + h + 1)
                    v.tensor_tensor(AB[:, h, :], US[:, h, :], SG[:, h, :], ALU.mult).then_inc(ab_ready, 1)
            for t in range(NT):
                v.wait_ge(bd_ps, t + 1)
                if t >= 4:
                    v.wait_ge(out_st[t % 4], 16 * (t // 4))
                f = FO[:, t % 4, :]
                for k in range(TOPK):
                    j = TOPK * t + k
                    v.wait_ge(yr_in[j % 16], 16 * (j // 16 + 1))
                    if k:
                        v.wait_ge(f_acc, j)
                    src = f.rearrange("p (a n) -> p a n", a=2) if k else PS[:, 2 * (t % 4):2 * (t % 4) + 2, :]
                    v.scalar_tensor_tensor(out=f.rearrange("p (a n) -> p a n", a=2), in0=YR[:, j % 16, :].rearrange("p (a n) -> p a n", a=2),
                                           scalar=GT8[:, t, k:k + 1], in1=src, op0=ALU.mult, op1=ALU.add).then_inc(f_acc, 1)
                v.wait_ge(f_rstd, t + 1)
                link(v.scalar_tensor_tensor(out=f, in0=f, scalar=st[:, 40 + t:41 + t], in1=GP2, op0=ALU.mult, op1=ALU.mult))
                v.tensor_tensor(f, f, X[:, t, :], ALU.add).then_inc(f_out, 1)


_INS = ['x', 'c', 'w_ada', 'b_ada', 'g_pre_mix', 'g_post_mix', 'w_in', 'w_gk_fwd', 'b_gk_fwd', 'w_gk_bwd', 'b_gk_bwd',
        'g_gla_out', 'attn_sink', 'w_out', 'g_pre_ffn', 'g_post_ffn', 'w_router', 'b_router',
        'w_gate_up', 'b_gate_up', 'w_down', 'b_down']
_OUTS = [((1, SEQ, D), 'float32')]


def kernel(**inputs):
    import numpy as _np
    import concourse.bacc as _bacc
    from concourse import mybir as _mybir
    from concourse.bass_utils import run_bass_kernel_spmd as _run

    nc = _bacc.Bacc("TRN2", target_bir_lowering=False, num_devices=1)
    arrays, args = {}, []
    for name in _INS:
        a = _np.ascontiguousarray(inputs[name])
        arrays[f"in_{name}_dram"] = a
        args.append(nc.dram_tensor(f"in_{name}_dram", a.shape, _mybir.dt.from_np(a.dtype), kind="ExternalInput").ap())
    for i, (shape, dtype) in enumerate(_OUTS):
        dt = _mybir.dt.from_np(_np.dtype(dtype))
        args.append(nc.dram_tensor(f"out_{i}_dram", shape, dt, kind="ExternalOutput").ap())
    block_kernel(nc, *args)
    r = _run(nc, [arrays], core_ids=[0])
    return r.results[0]["out_0_dram"]
```

```python
from contextlib import ExitStack

import numpy as np

import concourse.bass as bass
from concourse import mybir

P = 128
D = 1024
SEQ = 1024
NT = SEQ // P
KD = D // P
HEADS, DK, DV, RANK = 4, 64, 128, 16
CHUNK = 64
NCH = SEQ // CHUNK
QH, KVH, HD = 8, 2, 64
ROT = HD // 4
HALF = ROT // 2
THETA = 500000.0
NE, TOPK, FF = 32, 4, 1024
BLK = P
MAXB = SEQ * TOPK // BLK + NE
EPS = 1e-6
LIMIT, ALPHA = 7.0, 1.702
NEG = -1e30

F32 = mybir.dt.float32
I32 = mybir.dt.int32
U32 = mybir.dt.uint32
ALU = mybir.AluOpType
ACT = mybir.ActivationFunctionType
AX = mybir.AxisListType

C_Q, C_K, C_V, C_G, C_LR, C_AQ, C_AK = 0, 256, 512, 1024, 1536, 1568, 2080


def rotary_table():
    inv = (np.float32(THETA) ** (np.float32(-2.0) * np.arange(HALF, dtype=np.float32) / np.float32(ROT))).astype(np.float32)
    ang = (np.arange(SEQ, dtype=np.float32)[:, None] * inv[None, :]).astype(np.float32)
    t = np.stack([np.cos(ang), np.sin(ang)]).astype(np.float32)
    return np.ascontiguousarray(t.reshape(2, NT, P, HALF).transpose(2, 0, 1, 3).reshape(P, 2 * NT * HALF))


def block_kernel(nc, x, c, w_ada, b_ada, g_pre_mix, g_post_mix, w_in, w_gk_fwd, b_gk_fwd, w_gk_bwd, b_gk_bwd,
                 g_gla_out, attn_sink, w_out, g_pre_ffn, g_post_ffn, w_router, b_router,
                 w_gate_up, b_gate_up, w_down, b_down, out):
    ctx = ExitStack()
    with ctx:
        def sb(name, shape, dt=F32):
            return ctx.enter_context(nc.sbuf_tensor(name, shape, dt))

        def sem(name):
            return ctx.enter_context(nc.semaphore(name))

        ctx.enter_context(nc.allow_non_contiguous_dma(reason="small index and vector loads"))

        h2_dram = nc.dram_tensor("h2_rows", [SEQ, D], F32, kind="Internal").ap()
        tok_dram = nc.dram_tensor("slot_token", [(MAXB + 1) * BLK, 1], I32, kind="Internal").ap()
        y_dram = nc.dram_tensor("expert_rows", [MAXB * BLK, D], F32, kind="Internal").ap()
        rot_dram = nc.inline_tensor(rotary_table(), name="rotary_table")
        rot_dram = rot_dram.ap() if hasattr(rot_dram, "ap") else rot_dram

        W = sb("W", [P, 24576])
        X = sb("X", [P, NT, D])
        R = sb("R", [P, 12288])
        hT = W[:, 0:8192].rearrange("p (k s) -> p k s", k=KD)
        ada_ring = W[:, 8192:16384].rearrange("p (r n) -> p r n", r=4)
        AQ = W[:, 8192:12288].rearrange("p (t n) -> p t n", t=NT)
        AKV = W[:, 12288:14336].rearrange("p (t n) -> p t n", t=NT)
        LR = W[0:RANK, 14336:16384].rearrange("p (b s) -> p b s", b=2)
        win_ring = W[:, 16384:24576].rearrange("p (r k n) -> p r k n", r=2, k=KD)
        GI = W[:, 16384:24576].rearrange("p (a s) -> p a s", a=8)
        wout_sb = W[:, 16384:24576].rearrange("p (k n) -> p k n", k=KD)
        O = W[:, 0:4096].rearrange("p (t n) -> p t n", t=NT)
        QKT = R[:, 0:4096].rearrange("p (a s) -> p a s", a=4)
        V = R[:, 4096:8192].rearrange("p (t n) -> p t n", t=NT)
        GG = R[:, 8192:12288].rearrange("p (t n) -> p t n", t=NT)
        acc = [R[:, 10240:12288], R[:, 4096:6144], R[:, 6144:8192]]
        xn = R[:, 0:2048].rearrange("p (b d) -> p b d", b=2)
        S1 = R[:, 8192:9216]
        SH1 = R[:, 9216:10240]
        OT = R[:, 0:8192].rearrange("p (k s) -> p k s", k=KD)
        kT = R[:, 8192:9216]
        qT = R[:, 9216:10240].rearrange("p (b n) -> p b n", b=2)
        SC = W[:, 4096:7168].rearrange("p (b j n) -> p b j n", b=2, j=4)
        xn2 = R[:, 8192:10240].rearrange("p (b d) -> p b d", b=2)
        h2T = R[:, 10240:11264].rearrange("p (k s) -> p k s", k=KD)
        wgu = W[:, 0:16384].rearrange("p (k n) -> p k n", k=KD)
        wdn = W[:, 16384:24576].rearrange("p (k n) -> p k n", k=KD)
        XG = R[:, 0:1024]
        XT = R[:, 1024:2048].rearrange("p (k s) -> p k s", k=KD)
        AB = R[:, 2048:3072].rearrange("p (h n) -> p h n", h=2)
        AT = R[:, 3072:4096].rearrange("p (k s) -> p k s", k=KD)
        YS = R[:, 4096:5120]
        BI = R[:, 5120:7168]
        GS = R[:, 7168:8192].rearrange("p (h n) -> p h n", h=2)
        US = R[:, 8192:9216].rearrange("p (h n) -> p h n", h=2)
        SG = R[:, 9216:10240].rearrange("p (h n) -> p h n", h=2)
        YR = W[:, 0:16384].rearrange("p (r n) -> p r n", r=16)
        FO = R[:, 0:4096].rearrange("p (r n) -> p r n", r=4)

        MODR = sb("MODR", [P, 4, D])
        GP1, S2, SH2, GP2 = (MODR[:, j, :] for j in range(4))
        ident = sb("ident", [P, P])
        ones = sb("ones", [P, P])
        tri = sb("tri", [P, P])
        cmask = sb("cmask", [P, 2, P])
        amask = sb("amask", [P, 3, P])
        scanm = W[:, 7168:8192]
        rot = sb("rot", [P, 2, NT, HALF])
        rtmp = W[:, 6144:6400].rearrange("p (a t f) -> p a t f", a=4, t=NT)
        cvec = sb("cvec", [KD, P])
        cT = sb("cT", [P, 2, KD])
        bgk = sb("bgk", [4, P])
        bgT = sb("bgT", [P, 4])
        wgk = sb("wgk", [RANK, 2, 256])
        wlr = sb("wlr", [P, KD, 2 * RANK])
        wrt = sb("wrt", [P, KD, NE])
        ggla = sb("ggla", [P, DV])
        sinkb = sb("sinkb", [P, QH])
        brt = sb("brt", [P, NE])
        st = sb("st", [P, 64])
        held_done = sem("held_done")
        held = sb("held", [P, 1])
        mhalf = sb("mhalf", [P, HEADS])
        dec = sb("dec", [P, NCH])
        KS = W[:, 5120:5376].rearrange("p (b n) -> p b n", b=2)
        ST = W[:, 5376:5888].rearrange("p (b h n) -> p b h n", b=2, h=2)
        S = W[:, 5888:6144].rearrange("p (h n) -> p h n", h=2)
        am = sb("am", [P, 2, 6, 4])
        LG = W[:, 3584:3840].rearrange("p (t e) -> p t e", t=NT)
        M8 = sb("M8", [P, NT, 8])
        I8 = sb("I8", [P, NT, 8], U32)
        IF = sb("IF", [P, NT, TOPK])
        GT8 = sb("GT8", [P, NT, TOPK])
        gsum = sb("gsum", [P, 2, NT])
        OH = W[:, 2048:3072].rearrange("p (t k e) -> p t k e", t=NT, k=TOPK)
        OM = R[:, 11264:12288].rearrange("p (t k e) -> p t k e", t=NT, k=TOPK)
        MK = W[:, 3072:3328].rearrange("p (t e) -> p t e", t=NT)
        GM = W[:, 3840:4096].rearrange("p (t e) -> p t e", t=NT)
        GMT = R[0:NE, 10240:11264].rearrange("p (t e) -> p t e", t=NT)
        PO = W[:, 3328:3584].rearrange("p (t e) -> p t e", t=NT)
        cn = sb("cn", [P, 4, NE])
        iot = sb("iot", [P, 64])
        SL = sb("SL", [P, NT, TOPK])
        SLI = sb("SLI", [P, NT * TOPK], I32)
        TI = sb("TI", [P, NT], I32)
        EB = sb("EB", [1, MAXB])
        EBI = sb("EBI", [1, MAXB], I32)
        CEI = sb("CEI", [1, 2 * NE], I32)
        ZI = sb("ZI", [P, MAXB + 1], I32)
        IX = sb("IX", [P, 1], I32)
        bdn = R[0:NE, 11264:12288]
        PTv = [W[:, 7168:7552], W[:, 7552:7936]]
        SQ = sb("SQ", [P, D], mybir.dt.bfloat16)
        XS = W[:, 4096:5120]
        OMX = W[0:1, 0:MAXB * NE]
        PS = ctx.enter_context(nc.psum_tensor("PS", [P, 8, 512], F32))

        x_in = [sem(f"x_in{b}") for b in range(2)]
        small_in = sem("small_in")
        bada_in = sem("bada_in")
        acc_zero = sem("acc_zero")
        const_done = sem("const_done")
        ada_in = [sem(f"ada_in{r}") for r in range(4)]
        ada_used = sem("ada_used")
        win_in = [sem(f"win_in{r}") for r in range(2)]
        wlr_in = sem("wlr_in")
        vec_T = sem("vec_T")
        c_ready = sem("c_ready")
        silu_sig = sem("silu_sig")
        mod_ps = sem("mod_ps")
        mod_ready = sem("mod_ready")
        dve = sem("dve")
        act = sem("act")
        pool = sem("pool")
        h_ssq = sem("h_ssq")
        og_ssq = sem("og_ssq")
        f_rstd = sem("f_rstd")
        x1_rstd = sem("x1_rstd")
        y_rstd = sem("y_rstd")
        og_rstd = sem("og_rstd")
        h_rstd = sem("h_rstd")
        h_row = sem("h_row")
        h_tps = sem("h_tps")
        h_ready = sem("h_ready")
        pj_ps = sem("pj_ps")
        pj_ev = sem("pj_ev")
        gg_sig = sem("gg_sig")
        gg_done = sem("gg_done")
        z_ps = sem("z_ps")
        z_rd = sem("z_rd")
        z_exp = sem("z_exp")
        z_ln = sem("z_ln")
        la_ready = sem("la_ready")
        ex_in = sem("ex_in")
        ex_out = sem("ex_out")
        gi_ready = sem("gi_ready")
        gl_ks = sem("gl_ks")
        gl_ksr = sem("gl_ksr")
        gl_st = sem("gl_st")
        gl_str = sem("gl_str")
        gl_u = sem("gl_u")
        gl_s = sem("gl_s")
        gl_o = sem("gl_o")
        gl_i = sem("gl_i")
        gl_in = sem("gl_in")
        gl_ev = sem("gl_ev")
        og_ready = sem("og_ready")
        rot_ready = sem("rot_ready")
        at_T = sem("at_T")
        at_Tr = sem("at_Tr")
        at_s = sem("at_s")
        at_sr = sem("at_sr")
        at_m = sem("at_m")
        at_e = sem("at_e")
        at_n = sem("at_n")
        at_p = sem("at_p")
        at_pr = sem("at_pr")
        at_o = sem("at_o")
        at_or = sem("at_or")
        og_T = sem("og_T")
        og_Tr = sem("og_Tr")
        wout_in = sem("wout_in")
        y_ps = sem("y_ps")
        y_ssq = sem("y_ssq")
        x1_ready = sem("x1_ready")
        x1_ssq = sem("x1_ssq")
        h2_row = sem("h2_row")
        h2_st = [sem(f"h2_st{b}") for b in range(2)]
        h2_tps = sem("h2_tps")
        h2_tr = sem("h2_tr")
        lg_ps = sem("lg_ps")
        lg_ready = sem("lg_ready")
        g_exp = sem("g_exp")
        mk_ready = sem("mk_ready")
        po_ps = sem("po_ps")
        gmt_ps = sem("gmt_ps")
        gmt_r = sem("gmt_r")
        plan_ready = sem("plan_ready")
        zero_st = sem("zero_st")
        tok_st = sem("tok_st")
        gu_in = [sem(f"gu_in{g}") for g in range(4)]
        dn_in = [sem(f"dn_in{g}") for g in range(2)]
        bi_in = sem("bi_in")
        gu_used = [sem(f"gu_used{g}") for g in range(4)]
        dn_used = [sem(f"dn_used{g}") for g in range(2)]
        bi_used = sem("bi_used")
        ix_in = sem("ix_in")
        xg_in = sem("xg_in")
        tx_ps = sem("tx_ps")
        tx_ready = sem("tx_ready")
        gu_ps = sem("gu_ps")
        gu_add = sem("gu_add")
        gu_g = sem("gu_g")
        gu_m = sem("gu_m")
        gu_c = sem("gu_c")
        gu_sig = sem("gu_sig")
        ab_ready = sem("ab_ready")
        ta_ps = sem("ta_ps")
        ta_ready = sem("ta_ready")
        yb_rd = sem("yb_rd")
        yb_st = sem("yb_st")
        fill_st = sem("fill_st")
        yr_in = [sem(f"yr_in{r}") for r in range(16)]
        bd_ps = sem("bd_ps")
        bdn_in = sem("bdn_in")
        scan_ready = sem("scan_ready")
        f_acc = sem("f_acc")
        f_ssq = sem("f_ssq")
        f_out = sem("f_out")
        out_st = [sem(f"out_st{b}") for b in range(4)]

        N_SMALL = 15
        HEAD_ORDER = (0, 2, 1, 3)
        N_FILL = 16 * (MAXB - NE) // NT
        GJ = 12 + NT
        groups = [("qk", C_Q, 512, 0), ("v", C_V, 512, 1), ("g", C_G, 512, 0), ("aq", C_AQ, 512, 1), ("akv", C_AK, 256, 0)]

        block = ctx.enter_context(nc.Block())

        @block.sync
        def _(sp):
            small = 0

            def load(dst, src):
                nonlocal small
                sp.dma_start(dst, src).then_inc(small_in, 16)
                small += 1

            load(cvec[:, :], c.rearrange("a (k p) -> (a k) p", p=P))
            load(bgk[0:2, :], b_gk_fwd.rearrange("a (k p) -> (a k) p", p=P))
            load(bgk[2:4, :], b_gk_bwd.rearrange("a (k p) -> (a k) p", p=P))
            load(wgk[:, 0, :], w_gk_fwd[0])
            load(wgk[:, 1, :], w_gk_bwd[0])
            load(wrt[:, :, :], w_router[0].rearrange("(k p) e -> p k e", p=P))
            load(rot[:, :, :, :].rearrange("p a t f -> p (a t f)"), rot_dram)
            for dst, vec in ((S1, g_pre_mix), (GP1, g_post_mix), (S2, g_pre_ffn), (GP2, g_post_ffn)):
                load(dst, vec.broadcast_to([P, D]))
            load(ggla[:, :], g_gla_out.broadcast_to([P, DV]))
            load(sinkb[:, :], attn_sink.broadcast_to([P, QH]))
            load(brt[:, :], b_router.broadcast_to([P, NE]))
            load(wlr[:, :, :], w_in[0, :, C_LR:C_LR + 2 * RANK].rearrange("(k p) n -> p k n", p=P))
            assert small == N_SMALL, small
            sp.wait_ge(acc_zero, 1)
            for n in range(3):
                sp.dma_start(acc[n][0:1, :], b_ada[:, n * 2048:(n + 1) * 2048]).then_inc(bada_in, 16)

            def ada(j):
                n, k = divmod(j, KD)
                if j >= 4:
                    sp.wait_ge(ada_used, j - 3)
                sp.dma_start(ada_ring[:, j % 4, :], w_ada[0, k * P:(k + 1) * P, n * 2048:(n + 1) * 2048]).then_inc(ada_in[j % 4], 16)

            def project(g):
                _, c0, n, slot = groups[g]
                if g >= 2:
                    sp.wait_ge(pj_ps, (8, 20, 28)[g - 2])
                sp.dma_start(win_ring[:, slot, :, 0:n], w_in[0, :, c0:c0 + n].rearrange("(k p) n -> p k n", p=P)).then_inc(win_in[slot], 16)

            for j in range(KD):
                ada(j)
            for b in range(2):
                sp.dma_start(X[:, 4 * b:4 * b + 4, :], x[0, b * 512:(b + 1) * 512, :].rearrange("(t p) d -> p t d", p=P)).then_inc(x_in[b], 16)
            project(0)
            for j in range(KD, 2 * KD):
                ada(j)
            project(1)
            for j in range(2 * KD, 3 * KD):
                ada(j)
            for g in range(2, 5):
                project(g)
            for b in range(NE, MAXB, NT):
                sp.dma_start(y_dram[b * BLK:(b + NT) * BLK, :].rearrange("(t p) d -> p t d", p=P), X[:, :, :]).then_inc(fill_st, 16)
            sp.wait_ge(gl_o, 32)
            sp.dma_start(wout_sb[:, :, :], w_out[0].rearrange("(k p) n -> p k n", p=P)).then_inc(wout_in, 16)
            sp.wait_ge(const_done, 1)
            sp.dma_start(tok_dram.rearrange("(p b) a -> p (b a)", p=P), ZI[:, :]).then_inc(zero_st, 16)
            for t in range(NT):
                sp.wait_ge(h2_row, t + 1)
                sp.dma_start(h2_dram[t * P:(t + 1) * P, :], xn2[:, t % 2, :]).then_inc(h2_st[t % 2], 16)

            def weights(e, before):
                for g in range(4):
                    if before is not None:
                        sp.wait_ge(gu_used[g], before)
                    sp.dma_start(wgu[:, 2 * g:2 * g + 2, :],
                                 w_gate_up[0, bass.ds(e, 1), g * 256:(g + 1) * 256, :].rearrange("a (k p) n -> p (a k) n", p=P)).then_inc(gu_in[g], 16)
                if before is not None:
                    sp.wait_ge(bi_used, before * 2)
                sp.dma_start(BI, b_gate_up[0, bass.ds(e, 1), :].broadcast_to([P, 2 * FF])).then_inc(bi_in, 16)
                for g in range(2):
                    if before is not None:
                        sp.wait_ge(dn_used[g], before)
                    sp.dma_start(wdn[:, 4 * g:4 * g + 4, :],
                                 w_down[0, bass.ds(e, 1), g * 512:(g + 1) * 512, :].rearrange("a (k p) n -> p (a k) n", p=P)).then_inc(dn_in[g], 16)

            sp.wait_ge(y_ps, NT)
            sp.wait_ge(plan_ready, 1)
            sp.wait_ge(gmt_r, 1)
            sp.dma_start(bdn[:, :], b_down[0]).then_inc(bdn_in, 16)
            weights(0, None)
            with sp.Fori(1, NE) as e:
                before = sp.value_load(CEI[0:1, bass.ds(e, 1)], min_val=1, max_val=MAXB)
                weights(e, before)
            for t in range(NT):
                sp.wait_ge(f_out, t + 1)
                sp.dma_start(out[0, t * P:(t + 1) * P, :], FO[:, t % 4, :]).then_inc(out_st[t % 4], 16)
            for b in range(4):
                sp.wait_ge(out_st[b], 32)

        @block.gpsimd
        def _(pl):
            n = 0

            def link(ins):
                nonlocal n
                n += 1
                ins.then_inc(pool, 1)
                pl.wait_ge(pool, n)

            def hold():
                pl.tensor_tensor(held[:, 0:1], mhalf[:, 0:1], mhalf[:, 1:2], ALU.mult).then_inc(held_done, 1)

            def rstd(dst, dim, ready):
                link(pl.tensor_scalar(dst, dst, 1.0 / dim, EPS, ALU.mult, ALU.add))
                pl.tensor_tensor(dst, dst, mhalf[:, 0:dst.shape[1]], ALU.pow).then_inc(ready, 1)

            for n_ in range(3):
                link(pl.memset(acc[n_], 0.0))
            link(pl.memset(mhalf[:, :], -0.5))
            pl.nop().then_inc(acc_zero, 1)
            link(pl.memset(ZI[:, :], 0))
            link(pl.memset(ident[:, :], 0.0))
            link(pl.memset(ones[:, :], 1.0))
            link(pl.memset(cmask[:, :, :], 1.0))
            link(pl.memset(tri[:, :], 1.0))
            link(pl.memset(amask[:, :, :], 0.0))
            link(pl.affine_select(out=ident[:, :], in_=ident[:, :], compare_op=ALU.not_equal, fill=1.0, base=0,
                                  pattern=[[-1, P]], channel_multiplier=1))
            link(pl.affine_select(out=tri[:, :], in_=tri[:, :], compare_op=ALU.is_gt, fill=0.0, base=0,
                                  pattern=[[1, P]], channel_multiplier=-1))
            link(pl.affine_select(out=cmask[:, 0, :], in_=cmask[:, 0, :], compare_op=ALU.is_ge, fill=0.0, base=0,
                                  pattern=[[1, P]], channel_multiplier=-1))
            link(pl.affine_select(out=cmask[:, 1, :], in_=cmask[:, 1, :], compare_op=ALU.is_ge, fill=0.0, base=0,
                                  pattern=[[-1, P]], channel_multiplier=1))
            link(pl.memset(cmask[0:CHUNK, :, CHUNK:P], 0.0))
            link(pl.memset(cmask[CHUNK:P, :, 0:CHUNK], 0.0))
            link(pl.affine_select(out=amask[:, 0, :], in_=amask[:, 0, :], compare_op=ALU.is_ge, fill=NEG, base=0,
                                  pattern=[[1, P]], channel_multiplier=-1))
            link(pl.affine_select(out=amask[:, 2, :], in_=amask[:, 2, :], compare_op=ALU.is_ge, fill=NEG, base=0,
                                  pattern=[[-1, P]], channel_multiplier=1))
            link(pl.iota(iot[:, :], pattern=[[1, 64]], base=0, channel_multiplier=0, allow_small_or_imprecise_dtypes=True))
            link(pl.iota(TI[:, :], pattern=[[P, NT]], base=0, channel_multiplier=1))
            pl.nop().then_inc(const_done, 1)
            for t in range(NT):
                pl.wait_ge(h_ssq, t + 1)
                rstd(st[:, t:t + 1], D, h_rstd)
            pl.wait_ge(pj_ev, 12 + 3 * NT)
            link(pl.memset(scanm, 1.0))
            link(pl.memset(scanm[:, 0:SEQ:CHUNK], 0.0))
            pl.nop().then_inc(scan_ready, 1)
            for t in range(NT):
                pl.wait_ge(og_ssq, t + 1)
                rstd(st[:, 48:52], DV, og_rstd)
            for t in range(NT):
                pl.wait_ge(y_ssq, t + 1)
                rstd(st[:, 16 + t:17 + t], D, y_rstd)
                pl.wait_ge(x1_ssq, t + 1)
                rstd(st[:, 24 + t:25 + t], D, x1_rstd)

            pl.wait_ge(plan_ready, 1)
            pl.wait_ge(zero_st, 16)
            for j in range(NT * TOPK):
                pl.indirect_dma_start(tok_dram, bass.IndirectOffsetOnAxis(ap=SLI[:, j:j + 1], axis=0),
                                      TI[:, j // TOPK:j // TOPK + 1], None).then_inc(tok_st, 16)
            pl.wait_ge(tok_st, 16 * NT * TOPK)
            for b in range(2):
                pl.wait_ge(h2_st[b], 16 * NT // 2)
            total = pl.value_load(CEI[0:1, NE:NE + 1], min_val=1, max_val=MAXB)
            hold()
            with pl.Fori(0, total + 1) as i:
                pl.wait_ge(held_done, i + 1)
                pl.wait_ge(tx_ps, i * 2 + 1)
                pl.dma_start(IX[:, :], tok_dram[bass.ds(i * BLK, BLK), :]).then_inc(ix_in, 16)
                pl.wait_ge(ix_in, i * 16 + 16)
                hold()
                pl.indirect_dma_start(XG, None, h2_dram, bass.IndirectOffsetOnAxis(ap=IX[:, 0:1], axis=0)).then_inc(xg_in, 16)
            def final_rstd(t):
                pl.wait_ge(f_ssq, t + 1)
                rstd(st[:, 40 + t:41 + t], D, f_rstd)

            for j in range(NT * TOPK):
                if j >= 16:
                    pl.wait_ge(f_acc, j - 15)
                    if j % TOPK == 0:
                        final_rstd(j // TOPK - 4)
                if j == 0:
                    pl.wait_ge(yb_st, total * 16 + 16)
                    pl.wait_ge(dn_used[1], total)
                    pl.wait_ge(held_done, total + 2)
                    hold()
                pl.indirect_dma_start(YR[:, j % 16, :], None, y_dram, bass.IndirectOffsetOnAxis(ap=SLI[:, j:j + 1], axis=0)).then_inc(yr_in[j % 16], 16)
            for t in range(NT - 4, NT):
                final_rstd(t)

        @block.tensor
        def _(pe):
            def tr(dst, src, n=P):
                return pe.transpose(dst, src, ident[0:n, 0:n])

            pe.wait_ge(const_done, 1)
            pe.wait_ge(small_in, 16 * N_SMALL)
            tr(PS[:, 0, 0:KD], cvec[:, :], KD)
            tr(PS[:, 0, 16:20], bgk[:, :], 4).then_inc(vec_T, 1)
            def modulation(n):
                if n % 4 == 0:
                    pe.wait_ge(ada_used, 8 * (n // 4) + 8)
                if n >= 2:
                    pe.wait_ge(mod_ready, n - 1)
                pe.matmul(PS[:, 6 + n % 2, :], ones[:, :], acc[n // 4][:, (n % 4) * 512:(n % 4 + 1) * 512], start=True, stop=True).then_inc(mod_ps, 1)

            for n in range(4):
                modulation(n)
            for t in range(NT):
                pe.wait_ge(h_row, t + 1)
                if t >= 2:
                    pe.wait_ge(h_ready, 2 * (t - 1))
                for k in range(KD):
                    m = tr(PS[:, 2 * (t % 2) + k // 4, (k % 4) * P:(k % 4 + 1) * P], xn[:, t % 2, k * P:(k + 1) * P])
                    if k % 4 == 3:
                        m.then_inc(h_tps, 1)
            j = 0

            def freed(q):
                if GJ <= q < GJ + NT:
                    pe.wait_ge(gg_done, q - GJ + 1)
                else:
                    pe.wait_ge(pj_ev, q + 1 - (NT if q >= GJ else 0))

            def bank():
                nonlocal j
                if j >= 6:
                    freed(j - 6)
                j += 1
                return (j - 1) % 6

            pe.wait_ge(h_ready, 2 * NT)
            for g, (what, c0, n, slot) in enumerate(groups):
                if g == 1:
                    for n_ in range(4, 12):
                        modulation(n_)
                    pe.wait_ge(mod_ready, 12)
                pe.wait_ge(win_in[slot], 16 * (g // 2 + 1))
                if what == "qk":
                    for a in range(4):
                        for s in range(2):
                            b = bank()
                            for k in range(KD):
                                m = pe.matmul(PS[:, b, :], win_ring[:, slot, k, a * P:(a + 1) * P], hT[:, k, s * 512:(s + 1) * 512],
                                              start=(k == 0), stop=(k == KD - 1))
                            m.then_inc(pj_ps, 1)
                    for d in range(2):
                        for s in range(2):
                            b = bank()
                            for k in range(KD):
                                m = pe.matmul(PS[0:RANK, b, :], wlr[:, k, d * RANK:(d + 1) * RANK], hT[:, k, s * 512:(s + 1) * 512],
                                              start=(k == 0), stop=(k == KD - 1))
                            m.then_inc(pj_ps, 1)
                else:
                    for t in range(NT):
                        b = bank()
                        for k in range(KD):
                            m = pe.matmul(PS[:, b, 0:n], hT[:, k, t * P:(t + 1) * P], win_ring[:, slot, k, 0:n],
                                          start=(k == 0), stop=(k == KD - 1))
                        m.then_inc(pj_ps, 1)
            freed(j - 1)

            def gate_logits(u, s):
                p, d = divmod(u, 2)
                if u or s:
                    pe.wait_ge(z_rd, 2 * u + s)
                pe.matmul(PS[:, 7, :], wgk[:, d, p * P:(p + 1) * P], LR[:, d, s * 512:(s + 1) * 512],
                          start=True, stop=True).then_inc(z_ps, 1)

            gate_logits(0, 0)
            gate_logits(0, 1)
            for u in range(4):
                p, d = divmod(u, 2)
                pe.wait_ge(gi_ready, u + 1)

                def first(i):
                    t = i if d == 0 else NT - 1 - i
                    n = 8 * u + i
                    ts = slice(t * P, (t + 1) * P)
                    if n:
                        pe.wait_ge(gl_ksr, n)
                        pe.wait_ge(gl_str, n)
                    tr(PS[:, 0, 0:P], GI[:, 3, ts]).then_inc(gl_ks, 1)
                    for h in range(2):
                        hs = slice(64 * h, 64 * h + 64)
                        m = pe.matmul(PS[:, 1 + h, 0:P], GI[hs, 1, ts], GI[hs, 0, ts], start=True, stop=True)
                    m.then_inc(gl_st, 1)

                first(0)
                for i in range(NT):
                    t = i if d == 0 else NT - 1 - i
                    n = 8 * u + i
                    order = (0, 1) if d == 0 else (1, 0)
                    if n:
                        pe.wait_ge(gl_ev, n)
                        pe.wait_ge(gl_s, 2 * n + u + (1 if i else 0))
                    pe.wait_ge(gl_ksr, n + 1)
                    for q, ch in enumerate(order):
                        cs = slice(64 * ch, 64 * ch + 64)
                        for h in range(2):
                            m = pe.matmul(PS[64 * h:64 * h + 64, 5 + ch, 0:P], KS[cs, n % 2, 64 * h:64 * h + 64],
                                          V[cs, t, (2 * p + h) * DV:(2 * p + h + 1) * DV], start=True, stop=True)
                        m.then_inc(gl_u, 1)
                    pe.wait_ge(gl_str, n + 1)
                    for h in range(2):
                        m = pe.matmul(PS[:, 3 + h, 0:P], ST[:, n % 2, h, :], V[:, t, (2 * p + h) * DV:(2 * p + h + 1) * DV],
                                      start=True, stop=False, skip_group_check=True)
                    m.then_inc(gl_in, 1)
                    if i + 1 < NT:
                        first(i + 1)
                    for q, ch in enumerate(order):
                        cs = slice(64 * ch, 64 * ch + 64)
                        pe.wait_ge(gl_s, 2 * n + u + 1 + q)
                        for h in range(2):
                            hs = slice(64 * h, 64 * h + 64)
                            m = pe.matmul(PS[cs, 3 + h, 0:P], GI[hs, 2, t * P + 64 * ch:t * P + 64 * ch + 64],
                                          S[hs, q, :], start=False, stop=True, skip_group_check=True)
                        m.then_inc(gl_o if q else gl_i, 1)
                    if u < 3 and i < 2:
                        gate_logits(u + 1, i)
            pe.wait_ge(gl_ev, 32)
            pe.wait_ge(rot_ready, 1)
            for t in range(NT):
                m = tr(PS[:, t // 4, (t % 4) * P:(t % 4 + 1) * P], AKV[:, t, 0:P])
                if t % 4 == 3:
                    m.then_inc(at_T, 1)
            pe.wait_ge(at_Tr, 2)

            def queries(t):
                if t:
                    pe.wait_ge(at_pr, 8 * t - 5)
                for cc in range(4):
                    m = tr(PS[:, 4, cc * P:(cc + 1) * P], AQ[:, t, cc * P:(cc + 1) * P])
                m.then_inc(at_T, 1)

            def scores(w):
                t, s = divmod(w, 2)
                lo, hi = max(0, t - 1), min(NT, t + 2)
                pe.wait_ge(at_Tr, 3 + t)
                for j in range(4):
                    cc, g = 2 * s + j // 2, j % 2
                    gs = slice(64 * g, 64 * g + 64)
                    if w:
                        pe.wait_ge(at_sr, 4 * w + j - 3)
                    pe.matmul(PS[:, j, 0:(hi - lo) * P], qT[gs, t % 2, cc * P:(cc + 1) * P], kT[gs, lo * P:hi * P],
                              start=True, stop=True).then_inc(at_s, 1)

            def products(w):
                t, s = divmod(w, 2)
                lo, hi = max(0, t - 1), min(NT, t + 2)

                def with_v(n):
                    q, g = 4 * w + n, n // 2
                    pe.wait_ge(at_pr, q + 1)
                    if w and n % 2 == 0:
                        pe.wait_ge(at_or, 2 * w + g - 1)
                    for b in range(hi - lo):
                        m = pe.matmul(PS[64 * (n % 2):64 * (n % 2) + 64, 6 + g, 0:P], AKV[:, lo + b, P + g * HD:P + (g + 1) * HD],
                                      PTv[q % 2][:, b * P:(b + 1) * P], start=(b == 0), stop=(b == hi - lo - 1))
                    if n % 2:
                        m.then_inc(at_o, 1)

                pe.wait_ge(at_n, 4 * w + 4)
                for n, j in enumerate(HEAD_ORDER):
                    q = 4 * w + n
                    if q >= 2:
                        pe.wait_ge(at_pr, q - 1)
                    for b in range(hi - lo):
                        m = tr(PS[:, 4 + q % 2, b * P:(b + 1) * P], SC[:, w % 2, j, b * P:(b + 1) * P])
                    m.then_inc(at_p, 1)
                    if n:
                        with_v(n - 1)
                with_v(3)

            queries(0)
            scores(0)
            for w in range(2 * NT):
                if w + 1 < 2 * NT:
                    if w % 2:
                        queries((w + 1) // 2)
                    scores(w + 1)
                products(w)
            for t in range(NT):
                pe.wait_ge(og_ready, t + 1)
                if t >= 2:
                    pe.wait_ge(og_Tr, t - 1)
                else:
                    pe.wait_ge(at_or, 32)
                for k in range(4):
                    m = tr(PS[:, t % 2, k * P:(k + 1) * P], O[:, t, k * P:(k + 1) * P])
                m.then_inc(og_T, 1)
            pe.wait_ge(og_Tr, NT)
            pe.wait_ge(wout_in, 16)

            def h2_transposed(t):
                pe.wait_ge(h2_row, t + 1)
                if t:
                    pe.wait_ge(h2_tr, 2 * t)
                for k in range(KD):
                    m = tr(PS[:, 4 + k // 4, (k % 4) * P:(k % 4 + 1) * P], xn2[:, t % 2, k * P:(k + 1) * P])
                    if k % 4 == 3:
                        m.then_inc(h2_tps, 1)

            def logits(t):
                pe.wait_ge(h2_tr, 2 * t + 2)
                if t:
                    pe.wait_ge(lg_ready, t)
                for k in range(KD):
                    m = pe.matmul(PS[:, 6, 0:NE], h2T[:, k, :], wrt[:, k, :], start=(k == 0), stop=(k == KD - 1))
                m.then_inc(lg_ps, 1)

            for t in range(NT + 2):
                if 2 <= t < NT:
                    pe.wait_ge(x1_ready, t - 1)
                if t < NT:
                    for k in range(KD):
                        for s in range(2):
                            m = pe.matmul(PS[:, 2 * (t % 2) + s, :], OT[:, k, t * P:(t + 1) * P], wout_sb[:, k, s * 512:(s + 1) * 512],
                                          start=(k == 0), stop=(k == KD - 1))
                    m.then_inc(y_ps, 1)
                if t >= 2:
                    logits(t - 2)
                if 1 <= t <= NT:
                    h2_transposed(t - 1)
            pe.wait_ge(mk_ready, 1)
            pe.matmul(PS[:, 0, 0:256], ones[:, :], MK[:, :, :].rearrange("p t e -> p (t e)"), start=True, stop=True)
            pe.matmul(PS[:, 1, 0:256], tri[:, :], MK[:, :, :].rearrange("p t e -> p (t e)"), start=True, stop=True).then_inc(po_ps, 1)
            for t in range(NT):
                m = tr(PS[0:NE, 2 + t // 4, (t % 4) * P:(t % 4 + 1) * P], GM[:, t, :])
            m.then_inc(gmt_ps, 1)
            pe.wait_ge(plan_ready, 1)
            pe.wait_ge(gmt_r, 1)

            def x_T(half, bk):
                for k in range(4):
                    m = tr(PS[:, bk, k * P:(k + 1) * P], XG[:, (4 * half + k) * P:(4 * half + k + 1) * P])
                m.then_inc(tx_ps, 1)
                return m

            total = pe.value_load(CEI[0:1, NE:NE + 1], min_val=1, max_val=MAXB)
            pe.nop().then_inc(tx_ps, 1)
            pe.wait_ge(xg_in, 16)
            x_T(0, 7)
            x_T(1, 6)
            with pe.Fori(0, total) as i:
                e1 = pe.value_load(EBI[0:1, bass.ds(i, 1)], min_val=1, max_val=NE)
                pe.wait_ge(tx_ready, i * 2 + 2)
                for h in range(2):
                    pe.wait_ge(gu_m, i * 2 + h + 1)
                    for k in range(KD):
                        if h == 0 and k % 2 == 0:
                            pe.wait_ge(gu_in[k // 2], e1 * 16)
                        for a in range(2):
                            m = pe.matmul(PS[:, 2 * h + a, :], XT[:, k, :], wgu[:, k, a * FF + h * 512:a * FF + (h + 1) * 512],
                                          start=(k == 0), stop=(k == KD - 1))
                        if h == 1 and k % 2 == 1:
                            m.then_inc(gu_used[k // 2], 1)
                        if h == 1 and k == 4:
                            pe.wait_ge(ab_ready, i * 2 + 2)
                            for kk in range(4):
                                mm = tr(PS[:, 6, kk * P:(kk + 1) * P], AB[:, 0, kk * P:(kk + 1) * P])
                            mm.then_inc(ta_ps, 1)
                    if h == 0:
                        m.then_inc(gu_ps, 1)
                pe.wait_ge(xg_in, i * 16 + 32)
                x_T(0, 7)
                pe.wait_ge(yb_rd, i + 1)
                pe.wait_ge(ta_ready, i * 2 + 2)
                pe.wait_ge(dn_in[0], e1 * 16)

                def down(k0, k1):
                    for k in range(k0, k1):
                        for s in range(2):
                            m = pe.matmul(PS[:, 4 + s, :], AT[:, k, :], wdn[:, k, s * 512:(s + 1) * 512],
                                          start=(k == 0), stop=(k == KD - 1))
                    return m

                down(0, 3)
                pe.wait_ge(ab_ready, i * 2 + 3)
                for k in range(4):
                    m = tr(PS[:, 0, k * P:(k + 1) * P], AB[:, 1, k * P:(k + 1) * P])
                m.then_inc(ta_ps, 1)
                x_T(1, 6)
                down(3, 4).then_inc(dn_used[0], 1)
                pe.wait_ge(ta_ready, i * 2 + 3)
                pe.wait_ge(dn_in[1], e1 * 16)
                down(4, KD).then_inc(dn_used[1], 1)
            for t in range(NT):
                if t == 0:
                    pe.wait_ge(yb_rd, total + 1)
                    pe.wait_ge(bdn_in, 16)
                if t >= 4:
                    pe.wait_ge(f_acc, 4 * (t - 3))
                for s in range(2):
                    m = pe.matmul(PS[:, 2 * (t % 4) + s, :], GMT[:, t, :], bdn[:, s * 512:(s + 1) * 512], start=True, stop=True)
                m.then_inc(bd_ps, 1)

        @block.scalar
        def _(a):
            n = 0

            def link(ins):
                nonlocal n
                n += 1
                ins.then_inc(act, 1)
                a.wait_ge(act, n)

            a.wait_ge(c_ready, 1)
            a.activation(cT[:, 1, :], cT[:, 0, :], ACT.Sigmoid).then_inc(silu_sig, 1)
            for t in range(NT):
                a.wait_ge(x_in[t // 4], 16)
                link(a.activation(SQ[:, :], X[:, t, :], ACT.Square, accum_out=st[:, t:t + 1]))
                a.nop().then_inc(h_ssq, 1)
            for t in range(NT):
                for s in range(2):
                    a.wait_ge(h_tps, 2 * t + s + 1)
                    a.activation(hT[:, 4 * s:4 * s + 4, t * P:(t + 1) * P],
                                 PS[:, 2 * (t % 2) + s, :].rearrange("p (k s) -> p k s", k=4), ACT.Copy).then_inc(h_ready, 1)
            j = 0
            for g, (what, c0, nn, slot) in enumerate(groups):
                if what == "qk":
                    for aa in range(4):
                        for s in range(2):
                            a.wait_ge(pj_ps, j + 1)
                            a.activation(QKT[:, aa, s * 512:(s + 1) * 512], PS[:, j % 6, :], ACT.Copy,
                                         scale=(DK ** -0.5 if aa < 2 else 1.0)).then_inc(pj_ev, 1)
                            j += 1
                    a.wait_ge(ada_used, 3 * KD)
                    for d in range(2):
                        for s in range(2):
                            a.wait_ge(pj_ps, j + 1)
                            a.activation(LR[:, d, s * 512:(s + 1) * 512], PS[0:RANK, j % 6, :], ACT.Copy).then_inc(pj_ev, 1)
                            j += 1
                    continue
                for t in range(NT):
                    a.wait_ge(pj_ps, j + 1)
                    if what == "v":
                        a.activation(V[:, t, :], PS[:, j % 6, :], ACT.Copy).then_inc(pj_ev, 1)
                    elif what == "g":
                        a.activation(GG[:, t, :], PS[:, j % 6, :], ACT.Sigmoid).then_inc(gg_sig, 1)
                    elif what == "aq":
                        a.activation(AQ[:, t, :].rearrange("p (c g d) -> p g c d", c=4, g=2),
                                     PS[:, j % 6, :].rearrange("p (g c d) -> p g c d", g=2, c=4), ACT.Copy).then_inc(pj_ev, 1)
                    else:
                        a.activation(AKV[:, t, :], PS[:, j % 6, 0:256], ACT.Copy).then_inc(pj_ev, 1)
                    j += 1
            gla = [0]
            def log_sigmoid(u):
                a.wait_ge(z_exp, u + 1)
                link(a.activation(GI[:, 5, :], GI[:, 5, :], ACT.Exp, scale=-1.0))
                a.activation(GI[:, 5, :], GI[:, 5, :], ACT.Ln, bias=1.0).then_inc(z_ln, 1)

            log_sigmoid(0)
            for u in range(4):
                a.wait_ge(ex_in, 2 * u + 2)
                if u:
                    a.wait_ge(gl_o, 8 * u)
                    a.wait_ge(gl_s, 17 * u)
                a.activation(GI[:, 0, :], GI[:, 6, :], ACT.Exp, scale=1.0 / 16).then_inc(ex_out, 1)
                a.activation(GI[:, 1, :], GI[:, 6, :], ACT.Exp, scale=-1.0 / 16).then_inc(ex_out, 1)
                a.activation(GI[:, 3, :], GI[:, 7, :], ACT.Exp, scale=1.0 / 16).then_inc(ex_out, 1)
                a.activation(GI[:, 2, :], GI[:, 4, :], ACT.Exp, scale=1.0 / 16).then_inc(ex_out, 1)
                last = CHUNK - 1 if u % 2 == 0 else 0
                a.activation(dec[:, :], GI[:, 4, last:SEQ:CHUNK], ACT.Exp, scale=1.0 / 16).then_inc(ex_out, 1)
                for i in range(NT):
                    m = 8 * u + i
                    a.wait_ge(gl_ks, m + 1)
                    if m >= 2:
                        a.wait_ge(gl_u, 2 * (m - 1))
                    a.activation(KS[:, m % 2, :], PS[:, 0, 0:P], ACT.Copy).then_inc(gl_ksr, 1)
                    if u < 3 and i == 3:
                        log_sigmoid(u + 1)
            for b in range(2):
                a.wait_ge(at_T, b + 1)
                a.activation(kT[:, b * 512:(b + 1) * 512], PS[:, b, :], ACT.Copy).then_inc(at_Tr, 1)

            def queries(t):
                a.wait_ge(at_T, 3 + t)
                a.activation(qT[:, t % 2, :], PS[:, 4, :], ACT.Copy).then_inc(at_Tr, 1)

            def width(w):
                t = w // 2
                return (min(NT, t + 2) - max(0, t - 1)) * P

            def exponential(w, j):
                a.wait_ge(at_m, w + 1)
                if j < 4:
                    sc = SC[:, w % 2, j, 0:width(w)]
                    a.activation(sc, sc, ACT.Exp, bias=am[:, w % 2, 1, j:j + 1], accum_out=am[:, w % 2, 2, j:j + 1]).then_inc(at_e, 1)
                else:
                    a.activation(am[:, w % 2, 4, :], am[:, w % 2, 3, :], ACT.Exp).then_inc(at_e, 1)

            def outputs(w, g):
                a.wait_ge(at_o, 2 * w + g + 1)
                t, s = divmod(w, 2)
                a.activation(OT[:, 4 + 2 * g + s, t * P:(t + 1) * P], PS[:, 6 + g, 0:P], ACT.Copy).then_inc(at_or, 1)

            queries(0)
            for j in range(5):
                exponential(0, j)
            for w in range(2 * NT):
                if w % 2 and w + 1 < 2 * NT:
                    queries((w + 1) // 2)
                for r in range(4):
                    q = 4 * w + r
                    a.wait_ge(at_p, q + 1)
                    if q >= 2:
                        a.wait_ge(at_o, q // 2)
                    a.activation(PTv[q % 2][:, 0:width(w)], PS[:, 4 + q % 2, 0:width(w)], ACT.Copy).then_inc(at_pr, 1)
                    if w + 1 < 2 * NT:
                        exponential(w + 1, r)
                    if r == 3:
                        outputs(w, 0)
                if w + 1 < 2 * NT:
                    exponential(w + 1, 4)
                outputs(w, 1)
            for t in range(NT):
                a.wait_ge(og_T, t + 1)
                a.activation(OT[:, 0:4, t * P:(t + 1) * P], PS[:, t % 2, :].rearrange("p (k s) -> p k s", k=4), ACT.Copy).then_inc(og_Tr, 1)

            def h2_out(t):
                for s in range(2):
                    a.wait_ge(h2_tps, 2 * t + s + 1)
                    if t:
                        a.wait_ge(lg_ps, t)
                    a.activation(h2T[:, 4 * s:4 * s + 4, :], PS[:, 4 + s, :].rearrange("p (k s) -> p k s", k=4), ACT.Copy).then_inc(h2_tr, 1)

            for t in range(NT):
                a.wait_ge(y_ps, t + 1)
                link(a.activation(SQ[:, :].rearrange("p (a n) -> p a n", a=2), PS[:, 2 * (t % 2):2 * (t % 2) + 2, :], ACT.Square,
                                  accum_out=st[:, 16 + t:17 + t]))
                a.nop().then_inc(y_ssq, 1)
                a.wait_ge(x1_ready, t + 1)
                link(a.activation(SQ[:, :], X[:, t, :], ACT.Square, accum_out=st[:, 24 + t:25 + t]))
                a.nop().then_inc(x1_ssq, 1)
                if t:
                    h2_out(t - 1)
            h2_out(NT - 1)
            a.wait_ge(g_exp, 1)
            link(a.activation(GT8[:, :, :], GT8[:, :, :], ACT.Exp))
            a.nop().then_inc(g_exp, 1)
            a.wait_ge(gmt_ps, 1)
            a.activation(GMT[:, :, :].rearrange("p (b t) s -> p b (t s)", b=2), PS[0:NE, 2:4, :], ACT.Copy).then_inc(gmt_r, 1)

            a.wait_ge(plan_ready, 1)
            total = a.value_load(CEI[0:1, NE:NE + 1], min_val=1, max_val=MAXB)

            def x_ev(half, bk, count):
                a.wait_ge(tx_ps, count)
                a.activation(XT[:, 4 * half:4 * half + 4, :], PS[:, bk, :].rearrange("p (k s) -> p k s", k=4), ACT.Copy).then_inc(tx_ready, 1)

            a.wait_ge(fill_st, N_FILL)
            a.nop().then_inc(ta_ready, 1)
            a.nop().then_inc(yb_rd, 1)
            a.nop().then_inc(yb_st, 16)
            x_ev(0, 7, 2)
            x_ev(1, 6, 3)
            with a.Fori(0, total) as i:
                def silu_part(h):
                    a.wait_ge(gu_g, i * 2 + h + 1)
                    a.wait_ge(ab_ready, i * 2 + h + 1)
                    a.activation(SG[:, h, :], GS[:, h, :], ACT.Sigmoid, scale=ALPHA).then_inc(gu_sig, 1)

                def act_T(h, bk):
                    a.wait_ge(ta_ps, i * 2 + h + 1)
                    a.activation(AT[:, 4 * h:4 * h + 4, :], PS[:, bk, :].rearrange("p (k s) -> p k s", k=4), ACT.Copy).then_inc(ta_ready, 1)

                silu_part(0)
                act_T(0, 6)
                x_ev(0, 7, i * 2 + 4)
                silu_part(1)
                act_T(1, 0)
                x_ev(1, 6, i * 2 + 5)
                a.wait_ge(dn_used[1], i + 1)
                a.wait_ge(yb_st, i * 16 + 16)
                a.activation(YS.rearrange("p (a n) -> p a n", a=2), PS[:, 4:6, :], ACT.Copy).then_inc(yb_rd, 1)
                a.wait_ge(yb_rd, i + 2)
                a.dma_start(y_dram[bass.ds(i * BLK, BLK), :], YS).then_inc(yb_st, 16)
            for t in range(NT):
                a.wait_ge(f_acc, 4 * (t + 1))
                link(a.activation(SQ[:, :], FO[:, t % 4, :], ACT.Square, accum_out=st[:, 40 + t:41 + t]))
                a.nop().then_inc(f_ssq, 1)

        @block.vector
        def _(v):
            n = 0

            def link(ins):
                nonlocal n
                n += 1
                ins.then_inc(dve, 1)
                v.wait_ge(dve, n)

            v.wait_ge(vec_T, 1)
            link(v.tensor_copy(cT[:, 0, :], PS[:, 0, 0:KD]))
            link(v.tensor_copy(bgT[:, :], PS[:, 0, 16:20]))
            v.nop().then_inc(c_ready, 1)
            v.wait_ge(silu_sig, 1)
            link(v.tensor_tensor(cT[:, 0, :], cT[:, 0, :], cT[:, 1, :], ALU.mult))
            v.wait_ge(bada_in, 48)
            def ada(j):
                nn, k = divmod(j, KD)
                v.wait_ge(ada_in[j % 4], 16 * (j // 4 + 1))
                if k:
                    v.wait_ge(ada_used, j)
                ac = acc[nn]
                v.scalar_tensor_tensor(out=ac, in0=ada_ring[:, j % 4, :], scalar=cT[:, 0, k:k + 1], in1=ac,
                                       op0=ALU.mult, op1=ALU.add).then_inc(ada_used, 1)
            def modulation(m):
                v.wait_ge(mod_ps, m + 1)
                what, s = divmod(m, 2)
                hs = slice(s * 512, (s + 1) * 512)
                src = PS[:, 6 + m % 2, :]
                if what in (0, 3):
                    ins = v.tensor_copy((SH1 if what == 0 else SH2)[:, hs], src)
                elif what in (1, 4):
                    dst = (S1 if what == 1 else S2)[:, hs]
                    ins = v.scalar_tensor_tensor(out=dst, in0=src, scalar=1.0, in1=dst, op0=ALU.add, op1=ALU.mult)
                else:
                    dst = (GP1 if what == 2 else GP2)[:, hs]
                    ins = v.tensor_tensor(dst, src, dst, ALU.mult)
                ins.then_inc(mod_ready, 1)

            for j in range(KD):
                ada(j)
            for m in range(4):
                modulation(m)
            v.wait_ge(mod_ready, 4)
            for t in range(NT):
                v.wait_ge(h_rstd, t + 1)
                if t >= 2:
                    v.wait_ge(h_tps, 2 * (t - 1))
                link(v.scalar_tensor_tensor(out=xn[:, t % 2, :], in0=X[:, t, :], scalar=st[:, t:t + 1], in1=S1, op0=ALU.mult, op1=ALU.mult))
                v.tensor_tensor(xn[:, t % 2, :], xn[:, t % 2, :], SH1, ALU.add).then_inc(h_row, 1)
            for j in range(KD, 3 * KD):
                ada(j)
            for m in range(4, 12):
                modulation(m)
            for t in range(NT):
                j = GJ + t
                v.wait_ge(gg_sig, t + 1)
                link(v.tensor_tensor(GG[:, t, :], PS[:, j % 6, :], GG[:, t, :], ALU.mult))
                v.nop().then_inc(gg_done, 1)
                v.tensor_tensor(GG[:, t, :].rearrange("p (h n) -> p h n", h=HEADS), GG[:, t, :].rearrange("p (h n) -> p h n", h=HEADS),
                                ggla[:, :].unsqueeze(1).broadcast_to([P, HEADS, DV]), ALU.mult).then_inc(dve, 1)
                n += 1
            chv = lambda ap: ap.rearrange("p (c s) -> p c s", s=CHUNK)
            def prepare(u, step):
                d = u % 2
                if step in (0, 1):
                    v.wait_ge(z_ps, 2 * u + step + 1)
                    v.tensor_scalar(GI[:, 4, step * 512:(step + 1) * 512], PS[:, 7, :], bgT[:, 2 * d + u // 2:2 * d + u // 2 + 1], None,
                                    ALU.add).then_inc(z_rd, 1)
                elif step == 2:
                    v.wait_ge(z_rd, 2 * u + 2)
                    v.scalar_tensor_tensor(out=GI[:, 5, :], in0=GI[:, 4, :], scalar=-1.0, in1=GI[:, 4, :], op0=ALU.mult, op1=ALU.max).then_inc(z_exp, 1)
                elif step == 3:
                    v.wait_ge(z_ln, u + 1)
                    link(v.scalar_tensor_tensor(out=GI[:, 7, :], in0=GI[:, 4, :], scalar=0.0, in1=GI[:, 5, :], op0=ALU.min, op1=ALU.subtract))
                elif step == 4:
                    if u == 0:
                        v.wait_ge(scan_ready, 1)
                    link(v.tensor_tensor_scan(GI[:, 4 if d == 0 else 6, :], scanm, GI[:, 7, :], 0.0, ALU.mult, ALU.add))
                elif step == 5 and d:
                    link(v.tensor_tensor(GI[:, 5, :], GI[:, 7, :], GI[:, 6, :], ALU.subtract))
                    link(v.tensor_tensor(chv(GI[:, 4, :]), chv(GI[:, 5, :]), chv(GI[:, 6, :])[:, :, CHUNK - 1:CHUNK].broadcast_to([P, NCH, CHUNK]), ALU.add))
                elif step == 6:
                    ref, last = (CHUNK // 2 - 1, CHUNK - 1) if d == 0 else (CHUNK // 2, 0)
                    b = chv(GI[:, 4, :])
                    v.tensor_tensor(chv(GI[:, 6, :]), b, b[:, :, ref:ref + 1].broadcast_to([P, NCH, CHUNK]), ALU.subtract).then_inc(ex_in, 1)
                    v.tensor_tensor(chv(GI[:, 7, :]), b[:, :, last:last + 1].broadcast_to([P, NCH, CHUNK]), b, ALU.subtract).then_inc(ex_in, 1)

            for step in range(7):
                prepare(0, step)
            for u in range(4):
                p, d = divmod(u, 2)
                q, k = QKT[:, p, :], QKT[:, 2 + p, :]
                if u:
                    v.wait_ge(gl_o, 8 * u)
                    v.wait_ge(gl_s, 17 * u)
                v.memset(S[:, 0, :], 0.0).then_inc(gl_s, 1)
                for part, (a_, src) in enumerate(((0, q), (1, k), (3, k), (2, q))):
                    v.wait_ge(ex_out, 5 * u + part + 1 + (part == 3))
                    ins = v.tensor_tensor(GI[:, a_, :], GI[:, a_, :], src, ALU.mult)
                link(ins)
                v.nop().then_inc(gi_ready, 1)

                def masked(i):
                    m = 8 * u + i
                    v.wait_ge(gl_st, m + 1)
                    if m >= 2:
                        v.wait_ge(gl_in, m - 1)
                    v.tensor_tensor(ST[:, m % 2, :, :], PS[:, 1:3, 0:P],
                                    cmask[:, d, :].unsqueeze(1).broadcast_to([P, 2, P]), ALU.mult).then_inc(gl_str, 1)

                masked(0)
                for i in range(NT):
                    t = i if d == 0 else NT - 1 - i
                    m = 8 * u + i
                    for qq, ch in enumerate((0, 1) if d == 0 else (1, 0)):
                        v.wait_ge(gl_u, 2 * m + qq + 1)
                        v.wait_ge(gl_s, 2 * m + u + 1 + qq)
                        if qq == 1:
                            if i + 1 < NT:
                                masked(i + 1)
                            v.wait_ge(gl_i, m + 1)
                        elif m:
                            v.wait_ge(gl_o, m)
                        v.scalar_tensor_tensor(out=S[:, 1 - qq, :], in0=S[:, qq, :], scalar=dec[:, 2 * t + ch:2 * t + ch + 1],
                                               in1=PS[:, 5 + ch, 0:P], op0=ALU.mult, op1=ALU.add).then_inc(gl_s, 1)
                    v.wait_ge(gl_o, m + 1)
                    o = O[:, t, 2 * p * DV:(2 * p + 2) * DV].rearrange("p (h n) -> p h n", h=2)
                    src = PS[:, 3:5, 0:P]
                    if d == 0:
                        v.tensor_copy(o, src).then_inc(gl_ev, 1)
                    else:
                        v.tensor_tensor(o, src, o, ALU.add).then_inc(gl_ev, 1)
                    if u < 3 and i < 7:
                        prepare(u + 1, i)
            v.wait_ge(gl_ev, 32)
            for t in range(NT):
                o = O[:, t, :].rearrange("p (h n) -> p h n", h=HEADS)
                tmp = XS[:, 0:512].rearrange("p (h n) -> p h n", h=HEADS)
                link(v.tensor_tensor(tmp, o, o, ALU.mult))
                v.tensor_reduce(st[:, 48:52], tmp, AX.X, ALU.add).then_inc(og_ssq, 1)
                v.wait_ge(og_rstd, t + 1)
                link(v.tensor_tensor(o, o, st[:, 48:52].unsqueeze(2).broadcast_to([P, HEADS, DV]), ALU.mult))
                v.tensor_tensor(O[:, t, :], O[:, t, :], GG[:, t, :], ALU.mult).then_inc(og_ready, 1)
            cos, sin = rot[:, 0, :, :], rot[:, 1, :, :]
            for buf, nh in ((AQ[:, :, :], QH), (AKV[:, :, 0:P], KVH)):
                hv = buf.rearrange("p t (h d) -> p t h d", d=HD)
                for h in range(nh):
                    x1, x2 = hv[:, :, h, 0:HALF], hv[:, :, h, HALF:ROT]
                    v.tensor_tensor(rtmp[:, 0, :, :], x1, cos, ALU.mult)
                    v.tensor_tensor(rtmp[:, 1, :, :], x2, sin, ALU.mult)
                    v.tensor_tensor(rtmp[:, 2, :, :], x2, cos, ALU.mult)
                    link(v.tensor_tensor(rtmp[:, 3, :, :], x1, sin, ALU.mult))
                    v.tensor_tensor(x1, rtmp[:, 0, :, :], rtmp[:, 1, :, :], ALU.subtract)
                    link(v.tensor_tensor(x2, rtmp[:, 2, :, :], rtmp[:, 3, :, :], ALU.add))
            v.nop().then_inc(rot_ready, 1)
            def masked_max(w):
                t, s = divmod(w, 2)
                lo, hi = max(0, t - 1), min(NT, t + 2)
                nn = (hi - lo) * P
                am0 = lo - (t - 1)
                A = am[:, w % 2, :, :]
                if w >= 2:
                    v.wait_ge(at_p, 4 * (w - 1))
                for j in range(4):
                    v.wait_ge(at_s, 4 * w + j + 1)
                    v.scalar_tensor_tensor(out=SC[:, w % 2, j, 0:nn].rearrange("p (b n) -> p b n", n=P),
                                           in0=PS[:, j, 0:nn].rearrange("p (b n) -> p b n", n=P), scalar=HD ** -0.5,
                                           in1=amask[:, am0:am0 + hi - lo, :], op0=ALU.mult, op1=ALU.add).then_inc(at_sr, 1)
                v.wait_ge(at_sr, 4 * w + 4)
                sk = sinkb[:, :].rearrange("p (g c) -> p c g", g=2)[:, 2 * s:2 * s + 2, :]
                pair = lambda row: A[:, row, :].rearrange("p (c g) -> p c g", g=2)
                link(v.tensor_reduce(A[:, 0, :], SC[:, w % 2, :, 0:nn], AX.X, ALU.max))
                link(v.tensor_tensor(pair(0), pair(0), sk, ALU.max))
                link(v.tensor_scalar(A[:, 1, :], A[:, 0, :], -1.0, None, ALU.mult))
                link(v.tensor_tensor(pair(3), sk, pair(0), ALU.subtract))
                v.nop().then_inc(at_m, 1)

            def normalised(w):
                nn = (min(NT, w // 2 + 2) - max(0, w // 2 - 1)) * P
                A = am[:, w % 2, :, :]
                v.wait_ge(at_e, 5 * w + 5)
                link(v.tensor_tensor(A[:, 5, :], A[:, 2, :], A[:, 4, :], ALU.add))
                link(v.reciprocal(A[:, 5, :], A[:, 5, :]))
                for j in HEAD_ORDER:
                    sc = SC[:, w % 2, j, 0:nn]
                    v.tensor_scalar(sc, sc, A[:, 5, j:j + 1], None, ALU.mult).then_inc(at_n, 1)

            masked_max(0)
            for w in range(2 * NT):
                if w + 1 < 2 * NT:
                    masked_max(w + 1)
                normalised(w)
            def top4(t):
                v.wait_ge(lg_ps, t + 1)
                link(v.tensor_tensor(LG[:, t, :], PS[:, 6, 0:NE], brt[:, :], ALU.add))
                v.nop().then_inc(lg_ready, 1)
                link(v.max(M8[:, t, :], LG[:, t, :]))
                link(v.max_index(I8[:, t, :], M8[:, t, :], LG[:, t, :]))

            v.wait_ge(fill_st, N_FILL)
            for t in range(NT):
                v.wait_ge(y_rstd, t + 1)
                for s in range(2):
                    v.scalar_tensor_tensor(out=XS[:, s * 512:(s + 1) * 512], in0=PS[:, 2 * (t % 2) + s, :], scalar=st[:, 16 + t:17 + t],
                                           in1=GP1[:, s * 512:(s + 1) * 512], op0=ALU.mult, op1=ALU.mult).then_inc(dve, 1)
                n += 2
                v.wait_ge(dve, n)
                v.tensor_tensor(X[:, t, :], X[:, t, :], XS[:, :], ALU.add).then_inc(x1_ready, 1)
                v.wait_ge(x1_rstd, t + 1)
                if t >= 2:
                    v.wait_ge(h2_tps, 2 * (t - 1))
                    v.wait_ge(h2_st[t % 2], 16 * (t // 2))
                link(v.scalar_tensor_tensor(out=xn2[:, t % 2, :], in0=X[:, t, :], scalar=st[:, 24 + t:25 + t], in1=S2, op0=ALU.mult, op1=ALU.mult))
                link(v.tensor_tensor(xn2[:, t % 2, :], xn2[:, t % 2, :], SH2, ALU.add))
                v.nop().then_inc(h2_row, 1)
                if t >= 2:
                    top4(t - 2)
            top4(NT - 2)
            top4(NT - 1)
            link(v.tensor_copy(IF[:, :, :], I8[:, :, 0:TOPK]))
            link(v.tensor_tensor(GT8[:, :, :], M8[:, :, 0:TOPK], M8[:, :, 0:1].broadcast_to([P, NT, TOPK]), ALU.subtract))
            v.nop().then_inc(g_exp, 1)
            for t in range(NT):
                v.tensor_tensor(OH[:, t, :, :], iot[:, 0:NE].unsqueeze(1).broadcast_to([P, TOPK, NE]),
                                IF[:, t, :].unsqueeze(2).broadcast_to([P, TOPK, NE]), ALU.is_equal).then_inc(dve, 1)
                n += 1
            v.wait_ge(dve, n)
            link(v.tensor_reduce(MK[:, :, :], OH[:, :, :, :].rearrange("p t k e -> p t e k"), AX.X, ALU.add))
            v.wait_ge(g_exp, 2)
            link(v.tensor_reduce(gsum[:, 0, :], GT8[:, :, :], AX.X, ALU.add))
            link(v.reciprocal(gsum[:, 1, :], gsum[:, 0, :]))
            link(v.tensor_tensor(GT8[:, :, :], GT8[:, :, :], gsum[:, 1, :].unsqueeze(2).broadcast_to([P, NT, TOPK]), ALU.mult))
            link(v.tensor_tensor(OM, OH[:, :, :, :], GT8[:, :, :].unsqueeze(3).broadcast_to([P, NT, TOPK, NE]), ALU.mult))
            link(v.tensor_reduce(GM[:, :, :], OM.rearrange("p t k e -> p t e k"), AX.X, ALU.add))
            v.nop().then_inc(mk_ready, 1)
            v.wait_ge(po_ps, 1)
            tot = PS[:, 0, 0:256].rearrange("p (t e) -> p t e", t=NT)
            link(v.tensor_copy(PO[:, :, :], PS[:, 1, 0:256].rearrange("p (t e) -> p t e", t=NT)))
            link(v.tensor_copy(cn[:, 0, :], tot[:, 0, :]))
            for t in range(1, NT):
                link(v.tensor_tensor(PO[:, t, :], PO[:, t, :], cn[:, 0, :], ALU.add))
                link(v.tensor_tensor(cn[:, 0, :], tot[:, t, :], cn[:, 0, :], ALU.add))
            link(v.tensor_scalar(cn[:, 1, :], cn[:, 0, :], float(BLK), 1.0, ALU.is_gt, ALU.add))
            for m in range(2, SEQ // BLK):
                link(v.scalar_tensor_tensor(out=cn[:, 1, :], in0=cn[:, 0, :], scalar=float(m * BLK), in1=cn[:, 1, :], op0=ALU.is_gt, op1=ALU.add))
            link(v.tensor_tensor_scan(cn[:, 2, :], ones[:, 0:NE], cn[:, 1, :], 0.0, ALU.mult, ALU.add))
            link(v.tensor_tensor(cn[:, 3, :], cn[:, 2, :], cn[:, 1, :], ALU.subtract))
            link(v.tensor_copy(CEI[:, 0:NE], cn[0:1, 3, :]))
            link(v.tensor_copy(CEI[:, NE:NE + 1], cn[0:1, 2, NE - 1:NE]))
            link(v.tensor_scalar(cn[:, 3, :], cn[:, 3, :], float(BLK), None, ALU.mult))
            link(v.tensor_tensor(PO[:, :, :], PO[:, :, :], cn[:, 3, :].unsqueeze(1).broadcast_to([P, NT, NE]), ALU.add))
            for t in range(NT):
                v.tensor_tensor(OM[:, t], OH[:, t, :, :], PO[:, t, :].unsqueeze(1).broadcast_to([P, TOPK, NE]), ALU.mult).then_inc(dve, 1)
                n += 1
            v.wait_ge(dve, n)
            link(v.tensor_reduce(SL[:, :, :], OM, AX.X, ALU.add))
            link(v.tensor_copy(SLI[:, :], SL[:, :, :].rearrange("p t k -> p (t k)")))
            eb = OMX[0:1, :].rearrange("p (b e) -> p b e", e=NE)
            link(v.tensor_tensor(eb, cn[0:1, 2, :].unsqueeze(1).broadcast_to([1, MAXB, NE]),
                                 iot[0:1, 0:MAXB].unsqueeze(2).broadcast_to([1, MAXB, NE]), ALU.is_le))
            link(v.tensor_reduce(EB[:, :], eb, AX.X, ALU.add))
            link(v.tensor_scalar(EB[:, :], EB[:, :], float(NE - 1), 1.0, ALU.min, ALU.add))
            link(v.tensor_copy(EBI[:, :], EB[:, :]))
            v.nop().then_inc(plan_ready, 1)

            total = v.value_load(CEI[0:1, NE:NE + 1], min_val=1, max_val=MAXB)
            v.nop().then_inc(gu_m, 1)
            v.nop().then_inc(ab_ready, 1)
            with v.Fori(0, total) as i:
                e1 = v.value_load(EBI[0:1, bass.ds(i, 1)], min_val=1, max_val=NE)
                v.wait_ge(bi_in, e1 * 16)
                for h in range(2):
                    hs = slice(h * 512, (h + 1) * 512)
                    v.wait_ge(gu_used[3] if h else gu_ps, i + 1)
                    v.tensor_tensor(GS[:, h, :], PS[:, 2 * h, :], BI[:, h * 512:(h + 1) * 512], ALU.add).then_inc(gu_add, 1)
                    v.tensor_tensor(US[:, h, :], PS[:, 2 * h + 1, :], BI[:, FF + h * 512:FF + (h + 1) * 512], ALU.add).then_inc(gu_m, 1)
                    v.wait_ge(gu_add, i * 2 + h + 1)
                    v.tensor_scalar(GS[:, h, :], GS[:, h, :], LIMIT, None, ALU.min).then_inc(gu_g, 1)
                    v.wait_ge(gu_m, i * 2 + h + 2)
                    v.nop().then_inc(bi_used, 1)
                    v.tensor_scalar(US[:, h, :], US[:, h, :], LIMIT, -LIMIT, ALU.min, ALU.max).then_inc(gu_c, 1)
                    v.wait_ge(gu_g, i * 2 + h + 1)
                    v.wait_ge(gu_c, i * 4 + 2 * h + 1)
                    v.scalar_tensor_tensor(out=US[:, h, :], in0=US[:, h, :], scalar=1.0, in1=GS[:, h, :], op0=ALU.add, op1=ALU.mult).then_inc(gu_c, 1)
                    v.wait_ge(gu_c, i * 4 + 2 * h + 2)
                    v.wait_ge(gu_sig, i * 2 + h + 1)
                    v.tensor_tensor(AB[:, h, :], US[:, h, :], SG[:, h, :], ALU.mult).then_inc(ab_ready, 1)
            for t in range(NT):
                v.wait_ge(bd_ps, t + 1)
                if t >= 4:
                    v.wait_ge(out_st[t % 4], 16 * (t // 4))
                f = FO[:, t % 4, :]
                for k in range(TOPK):
                    j = TOPK * t + k
                    v.wait_ge(yr_in[j % 16], 16 * (j // 16 + 1))
                    if k:
                        v.wait_ge(f_acc, j)
                    src = f.rearrange("p (a n) -> p a n", a=2) if k else PS[:, 2 * (t % 4):2 * (t % 4) + 2, :]
                    v.scalar_tensor_tensor(out=f.rearrange("p (a n) -> p a n", a=2), in0=YR[:, j % 16, :].rearrange("p (a n) -> p a n", a=2),
                                           scalar=GT8[:, t, k:k + 1], in1=src, op0=ALU.mult, op1=ALU.add).then_inc(f_acc, 1)
                v.wait_ge(f_rstd, t + 1)
                link(v.scalar_tensor_tensor(out=f, in0=f, scalar=st[:, 40 + t:41 + t], in1=GP2, op0=ALU.mult, op1=ALU.mult))
                v.tensor_tensor(f, f, X[:, t, :], ALU.add).then_inc(f_out, 1)


_INS = ['x', 'c', 'w_ada', 'b_ada', 'g_pre_mix', 'g_post_mix', 'w_in', 'w_gk_fwd', 'b_gk_fwd', 'w_gk_bwd', 'b_gk_bwd',
        'g_gla_out', 'attn_sink', 'w_out', 'g_pre_ffn', 'g_post_ffn', 'w_router', 'b_router',
        'w_gate_up', 'b_gate_up', 'w_down', 'b_down']
_OUTS = [((1, SEQ, D), 'float32')]


def kernel(**inputs):
    import numpy as _np
    import concourse.bacc as _bacc
    from concourse import mybir as _mybir
    from concourse.bass_utils import run_bass_kernel_spmd as _run

    nc = _bacc.Bacc("TRN2", target_bir_lowering=False, num_devices=1)
    arrays, args = {}, []
    for name in _INS:
        a = _np.ascontiguousarray(inputs[name])
        arrays[f"in_{name}_dram"] = a
        args.append(nc.dram_tensor(f"in_{name}_dram", a.shape, _mybir.dt.from_np(a.dtype), kind="ExternalInput").ap())
    for i, (shape, dtype) in enumerate(_OUTS):
        dt = _mybir.dt.from_np(_np.dtype(dtype))
        args.append(nc.dram_tensor(f"out_{i}_dram", shape, dt, kind="ExternalOutput").ap())
    block_kernel(nc, *args)
    r = _run(nc, [arrays], core_ids=[0])
    return r.results[0]["out_0_dram"]
```

```python
from contextlib import ExitStack

import numpy as np

import concourse.bass as bass
from concourse import mybir

P = 128
D = 1024
SEQ = 1024
NT = SEQ // P
KD = D // P
HEADS, DK, DV, RANK = 4, 64, 128, 16
CHUNK = 64
NCH = SEQ // CHUNK
QH, KVH, HD = 8, 2, 64
ROT = HD // 4
HALF = ROT // 2
THETA = 500000.0
NE, TOPK, FF = 32, 4, 1024
BLK = P
MAXB = SEQ * TOPK // BLK + NE
NS, RING = 3 * KD, 4
EPS = 1e-6
LIMIT, ALPHA = 7.0, 1.702
NEG = -1e30

F32 = mybir.dt.float32
F32R = mybir.dt.float32r
I32 = mybir.dt.int32
U32 = mybir.dt.uint32
ALU = mybir.AluOpType
ACT = mybir.ActivationFunctionType
AX = mybir.AxisListType

C_Q, C_K, C_V, C_G, C_LR, C_AQ, C_AK = 0, 256, 512, 1024, 1536, 1568, 2080


def rotary_table():
    inv = (np.float32(THETA) ** (np.float32(-2.0) * np.arange(HALF, dtype=np.float32) / np.float32(ROT))).astype(np.float32)
    ang = (np.arange(SEQ, dtype=np.float32)[:, None] * inv[None, :]).astype(np.float32)
    t = np.stack([np.cos(ang), np.sin(ang)]).astype(np.float32)
    return np.ascontiguousarray(t.reshape(2, NT, P, HALF).transpose(2, 0, 1, 3).reshape(P, 2 * NT * HALF))


def block_kernel(nc, x, c, w_ada, b_ada, g_pre_mix, g_post_mix, w_in, w_gk_fwd, b_gk_fwd, w_gk_bwd, b_gk_bwd,
                 g_gla_out, attn_sink, w_out, g_pre_ffn, g_post_ffn, w_router, b_router,
                 w_gate_up, b_gate_up, w_down, b_down, out):
    ctx = ExitStack()
    with ctx:
        def sb(name, shape, dt=F32):
            return ctx.enter_context(nc.sbuf_tensor(name, shape, dt))

        def sem(name):
            return ctx.enter_context(nc.semaphore(name))

        ctx.enter_context(nc.allow_non_contiguous_dma(reason="small index and vector loads"))

        h2_dram = nc.dram_tensor("h2_rows", [SEQ, D], F32, kind="Internal").ap()
        tok_dram = nc.dram_tensor("slot_token", [(MAXB + 1) * BLK, 1], I32, kind="Internal").ap()
        x1_dram = nc.dram_tensor("x1_rows", [SEQ, D], F32, kind="Internal").ap()
        mod_dram = nc.dram_tensor("mod_rows", [1, 4 * D], F32, kind="Internal").ap()
        y_dram = nc.dram_tensor("expert_rows", [MAXB * BLK, D], F32, kind="Internal").ap()
        rot_dram = nc.inline_tensor(rotary_table(), name="rotary_table")
        rot_dram = rot_dram.ap() if hasattr(rot_dram, "ap") else rot_dram

        W = sb("W", [P, 24576])
        R = sb("R", [P, 12288])
        Q = sb("Q", [P, 12288], F32R)
        hT = W[:, 0:8192].rearrange("p (k s) -> p k s", k=KD)
        ada_ring = W[:, 8192:16384].rearrange("p (r n) -> p r n", r=4)
        AQ = W[:, 8192:12288].rearrange("p (t n) -> p t n", t=NT)
        AKV = W[:, 12288:14336].rearrange("p (t n) -> p t n", t=NT)
        LR = W[0:RANK, 14336:16384].rearrange("p (b s) -> p b s", b=2)
        win_ring = W[:, 16384:24576].rearrange("p (r k n) -> p r k n", r=2, k=KD)
        GI = W[:, 16384:24576].rearrange("p (a s) -> p a s", a=8)
        wout_sb = W[:, 16384:24576].rearrange("p (k n) -> p k n", k=KD)
        O = W[:, 0:4096].rearrange("p (t n) -> p t n", t=NT)
        QKT = R[:, 0:4096].rearrange("p (a s) -> p a s", a=4)
        V = R[:, 4096:8192].rearrange("p (t n) -> p t n", t=NT)
        GG = R[:, 8192:12288].rearrange("p (t n) -> p t n", t=NT)
        acc = [R[:, 10240:12288], R[:, 4096:6144], R[:, 6144:8192]]
        xn = R[:, 0:2048].rearrange("p (b d) -> p b d", b=2)
        S1 = R[:, 8192:9216]
        SH1 = R[:, 9216:10240]
        OT = R[:, 0:8192].rearrange("p (k s) -> p k s", k=KD)
        kT = R[:, 8192:9216]
        qT = R[:, 9216:10240].rearrange("p (b n) -> p b n", b=2)
        SC = W[:, 4096:7168].rearrange("p (b j n) -> p b j n", b=2, j=4)
        xn2 = R[:, 8192:10240].rearrange("p (b d) -> p b d", b=2)
        h2T = R[:, 10240:11264].rearrange("p (k s) -> p k s", k=KD)
        raw = W[:, :].rearrange("p (s n) -> p s n", s=NS)
        hi = Q[:, 0:4096].rearrange("p (r n) -> p r n", r=RING)
        lo = Q[:, 4096:8192].rearrange("p (r n) -> p r n", r=RING)
        hi_f = hi.bitcast(F32)
        XG = R[:, 0:1024]
        XTh = Q[:, 8192:9216].rearrange("p (k s) -> p k s", k=KD)
        XTl = Q[:, 9216:10240].rearrange("p (k s) -> p k s", k=KD)
        ATh = Q[:, 10240:11264].rearrange("p (k s) -> p k s", k=KD)
        ATl = Q[:, 11264:12288].rearrange("p (k s) -> p k s", k=KD)
        AB = R[:, 1024:2048].rearrange("p (h n) -> p h n", h=2)
        YS = R[:, 2048:3072]
        BI = R[:, 3072:5120].rearrange("p (h a n) -> p h a n", h=2, a=2)
        GU = R[:, 5120:6144].rearrange("p (a n) -> p a n", a=2)
        GS, US = GU[:, 0, :], GU[:, 1, :]
        SG = R[:, 6144:6656]
        YR = W[:, 0:16384].rearrange("p (r n) -> p r n", r=16)
        FO = R[:, 0:4096].rearrange("p (r n) -> p r n", r=4)

        MODR = R[:, 8192:12288].rearrange("p (j n) -> p j n", j=4)
        GP1, S2, SH2 = (W[:, 5120 + j * D:5120 + (j + 1) * D] for j in range(3))
        GP2 = R[:, 11264:12288]
        XI = [W[:, 20480 + t * D:20480 + (t + 1) * D] for t in range(4)] + [R[:, 2048 + t * D:2048 + (t + 1) * D] for t in range(2)]
        X1 = W[:, 8192:16384].rearrange("p (t d) -> p t d", t=NT)
        XR = W[:, 16384:24576].rearrange("p (t d) -> p t d", t=NT)
        ident = sb("ident", [P, P])
        ones = sb("ones", [P, P])
        tri = sb("tri", [P, P])
        cmask = sb("cmask", [P, 2, P])
        amask = sb("amask", [P, 3, P])
        scanm = W[:, 7168:8192]
        rot = sb("rot", [P, 2, NT, HALF])
        rtmp = W[:, 6144:6400].rearrange("p (a t f) -> p a t f", a=4, t=NT)
        cvec = sb("cvec", [KD, P])
        cT = sb("cT", [P, 2, KD])
        bgk = sb("bgk", [4, P])
        bgT = sb("bgT", [P, 4])
        wgk = sb("wgk", [RANK, 2, 256])
        wlr = sb("wlr", [P, KD, 2 * RANK])
        wrt = sb("wrt", [P, KD, NE])
        ggla = sb("ggla", [P, DV])
        sinkb = sb("sinkb", [P, QH])
        brt = sb("brt", [P, NE])
        st = sb("st", [P, 64])
        held_done = sem("held_done")
        held = sb("held", [P, 1])
        mhalf = sb("mhalf", [P, HEADS])
        dec = sb("dec", [P, NCH])
        KS = W[:, 5120:5376].rearrange("p (b n) -> p b n", b=2)
        ST = W[:, 5376:5888].rearrange("p (b h n) -> p b h n", b=2, h=2)
        S = W[:, 5888:6144].rearrange("p (h n) -> p h n", h=2)
        am = sb("am", [P, 2, 6, 4])
        LG = W[:, 3584:3840].rearrange("p (t e) -> p t e", t=NT)
        M8 = sb("M8", [P, NT, 8])
        I8 = sb("I8", [P, NT, 8], U32)
        IF = sb("IF", [P, NT, TOPK])
        GT8 = sb("GT8", [P, NT, TOPK])
        gsum = sb("gsum", [P, 2, NT])
        OH = W[:, 2048:3072].rearrange("p (t k e) -> p t k e", t=NT, k=TOPK)
        OM = R[:, 11264:12288].rearrange("p (t k e) -> p t k e", t=NT, k=TOPK)
        MK = W[:, 3072:3328].rearrange("p (t e) -> p t e", t=NT)
        GM = W[:, 3840:4096].rearrange("p (t e) -> p t e", t=NT)
        GMT = R[0:NE, 10240:11264].rearrange("p (t e) -> p t e", t=NT)
        PO = W[:, 3328:3584].rearrange("p (t e) -> p t e", t=NT)
        cn = sb("cn", [P, 4, NE])
        iot = sb("iot", [P, 64])
        SL = sb("SL", [P, NT, TOPK])
        SLI = sb("SLI", [P, NT * TOPK], I32)
        TI = sb("TI", [P, NT], I32)
        EB = sb("EB", [1, MAXB])
        EBI = sb("EBI", [1, MAXB], I32)
        CEI = sb("CEI", [1, 2 * NE], I32)
        ZI = sb("ZI", [P, MAXB + 1], I32)
        IX = sb("IX", [P, 1], I32)
        bdn = R[0:NE, 9216:10240]
        PTv = [W[:, 7168:7552], W[:, 7552:7936]]
        SQ = sb("SQ", [P, D], mybir.dt.bfloat16)
        XS = W[:, 4096:5120]
        OMX = W[0:1, 0:MAXB * NE]
        PS = ctx.enter_context(nc.psum_tensor("PS", [P, 8, 512], F32))

        x_in = [sem(f"x_in{b}") for b in range(3)]
        g_in = sem("g_in")
        mod_st = sem("mod_st")
        rows_in = sem("rows_in")
        x_again = [sem(f"x_again{b}") for b in range(2)]
        gp2_in = sem("gp2_in")
        small_in = sem("small_in")
        bada_in = sem("bada_in")
        acc_zero = sem("acc_zero")
        const_done = sem("const_done")
        ada_in = [sem(f"ada_in{r}") for r in range(4)]
        ada_used = sem("ada_used")
        win_in = [sem(f"win_in{r}") for r in range(2)]
        wlr_in = sem("wlr_in")
        vec_T = sem("vec_T")
        c_ready = sem("c_ready")
        silu_sig = sem("silu_sig")
        mod_ps = sem("mod_ps")
        mod_ready = sem("mod_ready")
        dve = sem("dve")
        act = sem("act")
        pool = sem("pool")
        h_ssq = sem("h_ssq")
        og_ssq = sem("og_ssq")
        f_rstd = sem("f_rstd")
        x1_rstd = sem("x1_rstd")
        y_rstd = sem("y_rstd")
        og_rstd = sem("og_rstd")
        h_rstd = sem("h_rstd")
        h_row = sem("h_row")
        h_tps = sem("h_tps")
        h_ready = sem("h_ready")
        pj_ps = sem("pj_ps")
        pj_ev = sem("pj_ev")
        gg_sig = sem("gg_sig")
        gg_done = sem("gg_done")
        z_ps = sem("z_ps")
        z_rd = sem("z_rd")
        z_exp = sem("z_exp")
        z_ln = sem("z_ln")
        la_ready = sem("la_ready")
        ex_in = sem("ex_in")
        ex_out = sem("ex_out")
        gi_ready = sem("gi_ready")
        gl_ks = sem("gl_ks")
        gl_ksr = sem("gl_ksr")
        gl_st = sem("gl_st")
        gl_str = sem("gl_str")
        gl_u = sem("gl_u")
        gl_s = sem("gl_s")
        gl_o = sem("gl_o")
        gl_i = sem("gl_i")
        gl_in = sem("gl_in")
        gl_ev = sem("gl_ev")
        og_ready = sem("og_ready")
        rot_ready = sem("rot_ready")
        at_T = sem("at_T")
        at_Tr = sem("at_Tr")
        at_s = sem("at_s")
        at_sr = sem("at_sr")
        at_m = sem("at_m")
        at_e = sem("at_e")
        at_n = sem("at_n")
        at_p = sem("at_p")
        at_pr = sem("at_pr")
        at_o = sem("at_o")
        at_or = sem("at_or")
        og_T = sem("og_T")
        og_Tr = sem("og_Tr")
        wout_in = sem("wout_in")
        y_ps = sem("y_ps")
        y_ssq = sem("y_ssq")
        x1_ready = sem("x1_ready")
        x1_ssq = sem("x1_ssq")
        h2_row = sem("h2_row")
        h2_st = [sem(f"h2_st{b}") for b in range(2)]
        h2_tps = sem("h2_tps")
        h2_tr = sem("h2_tr")
        lg_ps = sem("lg_ps")
        lg_ready = sem("lg_ready")
        g_exp = sem("g_exp")
        mk_ready = sem("mk_ready")
        po_ps = sem("po_ps")
        gmt_ps = sem("gmt_ps")
        gmt_r = sem("gmt_r")
        plan_ready = sem("plan_ready")
        zero_st = sem("zero_st")
        tok_st = sem("tok_st")
        w_piece = [sem(f"w_piece{g}") for g in range(6)]
        bi_in = sem("bi_in")
        x1_st = sem("x1_st")
        x1_in = [sem(f"x1_in{b}") for b in range(2)]
        hi_done = sem("hi_done")
        lo_done = sem("lo_done")
        ring_used = sem("ring_used")
        ix_in = sem("ix_in")
        xg_in = sem("xg_in")
        tx_ps = sem("tx_ps")
        xh_done = sem("xh_done")
        xl_done = sem("xl_done")
        ah_done = sem("ah_done")
        al_done = sem("al_done")
        gu_g = sem("gu_g")
        gu_m = sem("gu_m")
        gu_c = sem("gu_c")
        gu_sig = sem("gu_sig")
        ab_ready = sem("ab_ready")
        ta_ps = sem("ta_ps")
        yb_rd = sem("yb_rd")
        yb_st = sem("yb_st")
        fill_st = sem("fill_st")
        yr_in = [sem(f"yr_in{r}") for r in range(16)]
        bd_ps = sem("bd_ps")
        bdn_in = sem("bdn_in")
        scan_ready = sem("scan_ready")
        f_acc = sem("f_acc")
        f_ssq = sem("f_ssq")
        f_out = sem("f_out")
        out_st = [sem(f"out_st{b}") for b in range(4)]

        N_SMALL = 12
        HEAD_ORDER = (0, 2, 1, 3)
        N_FILL = 16 * (MAXB - NE) // NT
        GJ = 12 + NT
        groups = [("qk", C_Q, 512, 0), ("v", C_V, 512, 1), ("g", C_G, 512, 0), ("aq", C_AQ, 512, 1), ("akv", C_AK, 256, 0)]

        block = ctx.enter_context(nc.Block())

        @block.sync
        def _(sp):
            small = 0

            def load(dst, src):
                nonlocal small
                sp.dma_start(dst, src).then_inc(small_in, 16)
                small += 1

            load(cvec[:, :], c.rearrange("a (k p) -> (a k) p", p=P))
            load(bgk[0:2, :], b_gk_fwd.rearrange("a (k p) -> (a k) p", p=P))
            load(bgk[2:4, :], b_gk_bwd.rearrange("a (k p) -> (a k) p", p=P))
            load(wgk[:, 0, :], w_gk_fwd[0])
            load(wgk[:, 1, :], w_gk_bwd[0])
            load(wrt[:, :, :], w_router[0].rearrange("(k p) e -> p k e", p=P))
            load(rot[:, :, :, :].rearrange("p a t f -> p (a t f)"), rot_dram)
            load(S1, g_pre_mix.broadcast_to([P, D]))
            load(ggla[:, :], g_gla_out.broadcast_to([P, DV]))
            load(sinkb[:, :], attn_sink.broadcast_to([P, QH]))
            load(brt[:, :], b_router.broadcast_to([P, NE]))
            load(wlr[:, :, :], w_in[0, :, C_LR:C_LR + 2 * RANK].rearrange("(k p) n -> p k n", p=P))
            assert small == N_SMALL, small
            sp.wait_ge(acc_zero, 1)
            for n in range(3):
                sp.dma_start(acc[n][0:1, :], b_ada[:, n * 2048:(n + 1) * 2048]).then_inc(bada_in, 16)

            def ada(j):
                n, k = divmod(j, KD)
                if j >= 4:
                    sp.wait_ge(ada_used, j - 3)
                sp.dma_start(ada_ring[:, j % 4, :], w_ada[0, k * P:(k + 1) * P, n * 2048:(n + 1) * 2048]).then_inc(ada_in[j % 4], 16)

            def project(g):
                _, c0, n, slot = groups[g]
                if g >= 2:
                    sp.wait_ge(pj_ps, (8, 20, 28)[g - 2])
                sp.dma_start(win_ring[:, slot, :, 0:n], w_in[0, :, c0:c0 + n].rearrange("(k p) n -> p k n", p=P)).then_inc(win_in[slot], 16)

            for j in range(KD):
                ada(j)
            sp.dma_start(W[:, 20480:24576].rearrange("p (t d) -> p t d", t=4), x[0, 0:512, :].rearrange("(t p) d -> p t d", p=P)).then_inc(x_in[0], 16)
            sp.dma_start(R[:, 2048:4096].rearrange("p (t d) -> p t d", t=2), x[0, 512:768, :].rearrange("(t p) d -> p t d", p=P)).then_inc(x_in[1], 16)
            sp.wait_ge(h_row, 2)
            sp.dma_start(W[:, 20480:22528].rearrange("p (t d) -> p t d", t=2), x[0, 768:1024, :].rearrange("(t p) d -> p t d", p=P)).then_inc(x_in[2], 16)
            project(0)
            for j in range(KD, 2 * KD):
                ada(j)
            for j in range(2 * KD, 3 * KD):
                ada(j)
            sp.wait_ge(h_row, NT)
            for j_, vec in ((0, g_post_mix), (1, g_pre_ffn), (3, g_post_ffn)):
                sp.dma_start(MODR[:, j_, :], vec.broadcast_to([P, D])).then_inc(g_in, 16)
            project(1)
            sp.wait_ge(mod_ready, 12)
            sp.dma_start(mod_dram, R[0:1, 8192:12288]).then_inc(mod_st, 16)
            for g in range(2, 5):
                project(g)
            sp.wait_ge(h_ready, 2 * NT)
            for b in range(NE, MAXB, NT):
                sp.dma_start(y_dram[b * BLK:(b + NT) * BLK, :].rearrange("(t p) d -> p t d", p=P),
                             W[:, 0:8192].rearrange("p (t d) -> p t d", t=NT)).then_inc(fill_st, 16)
            sp.wait_ge(gl_o, 32)
            sp.dma_start(wout_sb[:, :, :], w_out[0].rearrange("(k p) n -> p k n", p=P)).then_inc(wout_in, 16)
            sp.wait_ge(const_done, 1)
            sp.dma_start(tok_dram.rearrange("(p b) a -> p (b a)", p=P), ZI[:, :]).then_inc(zero_st, 16)
            sp.wait_ge(at_or, 4 * NT)
            sp.wait_ge(mod_st, 16)
            sp.dma_start(W[:, 5120:8192], mod_dram[:, 0:3 * D].broadcast_to([P, 3 * D])).then_inc(rows_in, 16)
            for b in range(2):
                sp.dma_start(X1[:, 4 * b:4 * b + 4, :], x[0, b * 512:(b + 1) * 512, :].rearrange("(t p) d -> p t d", p=P)).then_inc(x_again[b], 16)
            for t in range(NT):
                sp.wait_ge(h2_row, t + 1)
                sp.dma_start(h2_dram[t * P:(t + 1) * P, :], xn2[:, t % 2, :]).then_inc(h2_st[t % 2], 16)
                sp.dma_start(x1_dram[t * P:(t + 1) * P, :], X1[:, t, :]).then_inc(x1_st, 16)

            def weights(e, before):
                def split(g):
                    if before is not None:
                        sp.wait_ge(lo_done, before * NS + RING * (g + 1))

                for g in range(4):
                    h, k0 = g // 2, 4 * (g % 2)
                    split(g)
                    for a_ in range(2):
                        c0 = a_ * FF + h * 512
                        sp.dma_start(raw[:, 4 * g:4 * g + 4, a_ * 512:(a_ + 1) * 512],
                                     w_gate_up[0, bass.ds(e, 1), k0 * P:(k0 + 4) * P, c0:c0 + 512].rearrange("a (k p) n -> p (a k) n", p=P)).then_inc(w_piece[g], 16)
                if before is not None:
                    sp.wait_ge(gu_m, before * 2 + 1)
                for h in range(2):
                    sp.dma_start(BI[:, h, :, :], b_gate_up[0, bass.ds(e, 1), :].rearrange("o (a h n) -> o h a n", a=2, h=2)[:, h, :, :]
                                 .broadcast_to([P, 2, 512])).then_inc(bi_in, 16)
                for g in range(2):
                    split(4 + g)
                    sp.dma_start(raw[:, 16 + 4 * g:20 + 4 * g, :],
                                 w_down[0, bass.ds(e, 1), g * 512:(g + 1) * 512, :].rearrange("a (k p) n -> p (a k) n", p=P)).then_inc(w_piece[4 + g], 16)

            sp.wait_ge(y_ps, NT)
            sp.wait_ge(plan_ready, 1)
            sp.wait_ge(gmt_r, 1)
            for b in range(2):
                sp.wait_ge(h2_st[b], 16 * NT // 2)
            sp.dma_start(bdn[:, :], b_down[0]).then_inc(bdn_in, 16)
            sp.dma_start(GP2, mod_dram[:, 3 * D:4 * D].broadcast_to([P, D])).then_inc(gp2_in, 16)
            sp.wait_ge(x1_st, 16 * NT)
            weights(0, None)
            with sp.Fori(1, NE) as e:
                before = sp.value_load(CEI[0:1, bass.ds(e, 1)], min_val=1, max_val=MAXB)
                weights(e, before)
            total = sp.value_load(CEI[0:1, NE:NE + 1], min_val=1, max_val=MAXB)
            sp.wait_ge(lo_done, total * NS + NS)
            for b in range(2):
                sp.dma_start(XR[:, 4 * b:4 * b + 4, :], x1_dram[b * 512:(b + 1) * 512, :].rearrange("(t p) d -> p t d", p=P)).then_inc(x1_in[b], 16)
            for t in range(NT):
                sp.wait_ge(f_out, t + 1)
                sp.dma_start(out[0, t * P:(t + 1) * P, :], FO[:, t % 4, :]).then_inc(out_st[t % 4], 16)
            for b in range(4):
                sp.wait_ge(out_st[b], 32)

        @block.gpsimd
        def _(pl):
            n = 0

            def link(ins):
                nonlocal n
                n += 1
                ins.then_inc(pool, 1)
                pl.wait_ge(pool, n)

            def hold():
                pl.tensor_tensor(held[:, 0:1], mhalf[:, 0:1], mhalf[:, 1:2], ALU.mult).then_inc(held_done, 1)

            def rstd(dst, dim, ready):
                link(pl.tensor_scalar(dst, dst, 1.0 / dim, EPS, ALU.mult, ALU.add))
                pl.tensor_tensor(dst, dst, mhalf[:, 0:dst.shape[1]], ALU.pow).then_inc(ready, 1)

            for n_ in range(3):
                link(pl.memset(acc[n_], 0.0))
            link(pl.memset(mhalf[:, :], -0.5))
            pl.nop().then_inc(acc_zero, 1)
            link(pl.memset(ZI[:, :], 0))
            link(pl.memset(ident[:, :], 0.0))
            link(pl.memset(ones[:, :], 1.0))
            link(pl.memset(cmask[:, :, :], 1.0))
            link(pl.memset(tri[:, :], 1.0))
            link(pl.memset(amask[:, :, :], 0.0))
            link(pl.affine_select(out=ident[:, :], in_=ident[:, :], compare_op=ALU.not_equal, fill=1.0, base=0,
                                  pattern=[[-1, P]], channel_multiplier=1))
            link(pl.affine_select(out=tri[:, :], in_=tri[:, :], compare_op=ALU.is_gt, fill=0.0, base=0,
                                  pattern=[[1, P]], channel_multiplier=-1))
            link(pl.affine_select(out=cmask[:, 0, :], in_=cmask[:, 0, :], compare_op=ALU.is_ge, fill=0.0, base=0,
                                  pattern=[[1, P]], channel_multiplier=-1))
            link(pl.affine_select(out=cmask[:, 1, :], in_=cmask[:, 1, :], compare_op=ALU.is_ge, fill=0.0, base=0,
                                  pattern=[[-1, P]], channel_multiplier=1))
            link(pl.memset(cmask[0:CHUNK, :, CHUNK:P], 0.0))
            link(pl.memset(cmask[CHUNK:P, :, 0:CHUNK], 0.0))
            link(pl.affine_select(out=amask[:, 0, :], in_=amask[:, 0, :], compare_op=ALU.is_ge, fill=NEG, base=0,
                                  pattern=[[1, P]], channel_multiplier=-1))
            link(pl.affine_select(out=amask[:, 2, :], in_=amask[:, 2, :], compare_op=ALU.is_ge, fill=NEG, base=0,
                                  pattern=[[-1, P]], channel_multiplier=1))
            link(pl.iota(iot[:, :], pattern=[[1, 64]], base=0, channel_multiplier=0, allow_small_or_imprecise_dtypes=True))
            link(pl.iota(TI[:, :], pattern=[[P, NT]], base=0, channel_multiplier=1))
            pl.nop().then_inc(const_done, 1)
            for t in range(NT):
                pl.wait_ge(h_ssq, t + 1)
                rstd(st[:, t:t + 1], D, h_rstd)
            pl.wait_ge(fill_st, N_FILL)
            pl.wait_ge(pj_ev, 12 + 3 * NT)
            link(pl.memset(scanm, 1.0))
            link(pl.memset(scanm[:, 0:SEQ:CHUNK], 0.0))
            pl.nop().then_inc(scan_ready, 1)
            for t in range(NT):
                pl.wait_ge(og_ssq, t + 1)
                rstd(st[:, 48:52], DV, og_rstd)
            for t in range(NT):
                pl.wait_ge(y_ssq, t + 1)
                rstd(st[:, 16 + t:17 + t], D, y_rstd)
                pl.wait_ge(x1_ssq, t + 1)
                rstd(st[:, 24 + t:25 + t], D, x1_rstd)

            pl.wait_ge(plan_ready, 1)
            pl.wait_ge(zero_st, 16)
            for j in range(NT * TOPK):
                pl.indirect_dma_start(tok_dram, bass.IndirectOffsetOnAxis(ap=SLI[:, j:j + 1], axis=0),
                                      TI[:, j // TOPK:j // TOPK + 1], None).then_inc(tok_st, 16)
            pl.wait_ge(tok_st, 16 * NT * TOPK)
            for b in range(2):
                pl.wait_ge(h2_st[b], 16 * NT // 2)
            total = pl.value_load(CEI[0:1, NE:NE + 1], min_val=1, max_val=MAXB)
            hold()
            with pl.Fori(0, total + 1) as i:
                pl.wait_ge(held_done, i + 1)
                pl.wait_ge(tx_ps, i + 1)
                pl.dma_start(IX[:, :], tok_dram[bass.ds(i * BLK, BLK), :]).then_inc(ix_in, 16)
                pl.wait_ge(ix_in, i * 16 + 16)
                hold()
                pl.indirect_dma_start(XG, None, h2_dram, bass.IndirectOffsetOnAxis(ap=IX[:, 0:1], axis=0)).then_inc(xg_in, 16)
            def final_rstd(t):
                pl.wait_ge(f_ssq, t + 1)
                rstd(st[:, 40 + t:41 + t], D, f_rstd)

            for j in range(NT * TOPK):
                if j >= 16:
                    pl.wait_ge(f_acc, j - 15)
                    if j % TOPK == 0:
                        final_rstd(j // TOPK - 4)
                if j == 0:
                    pl.wait_ge(yb_st, total * 16 + 16)
                    pl.wait_ge(lo_done, total * NS + NS)
                    pl.wait_ge(held_done, total + 2)
                    hold()
                pl.indirect_dma_start(YR[:, j % 16, :], None, y_dram, bass.IndirectOffsetOnAxis(ap=SLI[:, j:j + 1], axis=0)).then_inc(yr_in[j % 16], 16)
            for t in range(NT - 4, NT):
                final_rstd(t)

        @block.tensor
        def _(pe):
            def tr(dst, src, n=P):
                return pe.transpose(dst, src, ident[0:n, 0:n])

            pe.wait_ge(const_done, 1)
            pe.wait_ge(small_in, 16 * N_SMALL)
            tr(PS[:, 0, 0:KD], cvec[:, :], KD)
            tr(PS[:, 0, 16:20], bgk[:, :], 4).then_inc(vec_T, 1)
            def modulation(n):
                if n % 4 == 0:
                    pe.wait_ge(ada_used, 8 * (n // 4) + 8)
                if n >= 2:
                    pe.wait_ge(mod_ready, n - 1)
                pe.matmul(PS[:, 6 + n % 2, :], ones[:, :], acc[n // 4][:, (n % 4) * 512:(n % 4 + 1) * 512], start=True, stop=True).then_inc(mod_ps, 1)

            for n in range(4):
                modulation(n)
            for t in range(NT):
                pe.wait_ge(h_row, t + 1)
                if t >= 2:
                    pe.wait_ge(h_ready, 2 * (t - 1))
                for k in range(KD):
                    m = tr(PS[:, 2 * (t % 2) + k // 4, (k % 4) * P:(k % 4 + 1) * P], xn[:, t % 2, k * P:(k + 1) * P])
                    if k % 4 == 3:
                        m.then_inc(h_tps, 1)
            j = 0

            def freed(q):
                if GJ <= q < GJ + NT:
                    pe.wait_ge(gg_done, q - GJ + 1)
                else:
                    pe.wait_ge(pj_ev, q + 1 - (NT if q >= GJ else 0))

            def bank():
                nonlocal j
                if j >= 6:
                    freed(j - 6)
                j += 1
                return (j - 1) % 6

            pe.wait_ge(h_ready, 2 * NT)
            for g, (what, c0, n, slot) in enumerate(groups):
                if g == 1:
                    for n_ in range(4, 12):
                        modulation(n_)
                    pe.wait_ge(mod_ready, 12)
                pe.wait_ge(win_in[slot], 16 * (g // 2 + 1))
                if what == "qk":
                    for a in range(4):
                        for s in range(2):
                            b = bank()
                            for k in range(KD):
                                m = pe.matmul(PS[:, b, :], win_ring[:, slot, k, a * P:(a + 1) * P], hT[:, k, s * 512:(s + 1) * 512],
                                              start=(k == 0), stop=(k == KD - 1))
                            m.then_inc(pj_ps, 1)
                    for d in range(2):
                        for s in range(2):
                            b = bank()
                            for k in range(KD):
                                m = pe.matmul(PS[0:RANK, b, :], wlr[:, k, d * RANK:(d + 1) * RANK], hT[:, k, s * 512:(s + 1) * 512],
                                              start=(k == 0), stop=(k == KD - 1))
                            m.then_inc(pj_ps, 1)
                else:
                    for t in range(NT):
                        b = bank()
                        for k in range(KD):
                            m = pe.matmul(PS[:, b, 0:n], hT[:, k, t * P:(t + 1) * P], win_ring[:, slot, k, 0:n],
                                          start=(k == 0), stop=(k == KD - 1))
                        m.then_inc(pj_ps, 1)
            freed(j - 1)

            def gate_logits(u, s):
                p, d = divmod(u, 2)
                if u or s:
                    pe.wait_ge(z_rd, 2 * u + s)
                pe.matmul(PS[:, 7, :], wgk[:, d, p * P:(p + 1) * P], LR[:, d, s * 512:(s + 1) * 512],
                          start=True, stop=True).then_inc(z_ps, 1)

            gate_logits(0, 0)
            gate_logits(0, 1)
            for u in range(4):
                p, d = divmod(u, 2)
                pe.wait_ge(gi_ready, u + 1)

                def first(i):
                    t = i if d == 0 else NT - 1 - i
                    n = 8 * u + i
                    ts = slice(t * P, (t + 1) * P)
                    if n:
                        pe.wait_ge(gl_ksr, n)
                        pe.wait_ge(gl_str, n)
                    tr(PS[:, 0, 0:P], GI[:, 3, ts]).then_inc(gl_ks, 1)
                    for h in range(2):
                        hs = slice(64 * h, 64 * h + 64)
                        m = pe.matmul(PS[:, 1 + h, 0:P], GI[hs, 1, ts], GI[hs, 0, ts], start=True, stop=True)
                    m.then_inc(gl_st, 1)

                first(0)
                for i in range(NT):
                    t = i if d == 0 else NT - 1 - i
                    n = 8 * u + i
                    order = (0, 1) if d == 0 else (1, 0)
                    if n:
                        pe.wait_ge(gl_ev, n)
                        pe.wait_ge(gl_s, 2 * n + u + (1 if i else 0))
                    pe.wait_ge(gl_ksr, n + 1)
                    for q, ch in enumerate(order):
                        cs = slice(64 * ch, 64 * ch + 64)
                        for h in range(2):
                            m = pe.matmul(PS[64 * h:64 * h + 64, 5 + ch, 0:P], KS[cs, n % 2, 64 * h:64 * h + 64],
                                          V[cs, t, (2 * p + h) * DV:(2 * p + h + 1) * DV], start=True, stop=True)
                        m.then_inc(gl_u, 1)
                    pe.wait_ge(gl_str, n + 1)
                    for h in range(2):
                        m = pe.matmul(PS[:, 3 + h, 0:P], ST[:, n % 2, h, :], V[:, t, (2 * p + h) * DV:(2 * p + h + 1) * DV],
                                      start=True, stop=False, skip_group_check=True)
                    m.then_inc(gl_in, 1)
                    if i + 1 < NT:
                        first(i + 1)
                    for q, ch in enumerate(order):
                        cs = slice(64 * ch, 64 * ch + 64)
                        pe.wait_ge(gl_s, 2 * n + u + 1 + q)
                        for h in range(2):
                            hs = slice(64 * h, 64 * h + 64)
                            m = pe.matmul(PS[cs, 3 + h, 0:P], GI[hs, 2, t * P + 64 * ch:t * P + 64 * ch + 64],
                                          S[hs, q, :], start=False, stop=True, skip_group_check=True)
                        m.then_inc(gl_o if q else gl_i, 1)
                    if u < 3 and i < 2:
                        gate_logits(u + 1, i)
            pe.wait_ge(gl_ev, 32)
            pe.wait_ge(rot_ready, 1)
            for t in range(NT):
                m = tr(PS[:, t // 4, (t % 4) * P:(t % 4 + 1) * P], AKV[:, t, 0:P])
                if t % 4 == 3:
                    m.then_inc(at_T, 1)
            pe.wait_ge(at_Tr, 2)

            def queries(t):
                if t:
                    pe.wait_ge(at_pr, 8 * t - 5)
                for cc in range(4):
                    m = tr(PS[:, 4, cc * P:(cc + 1) * P], AQ[:, t, cc * P:(cc + 1) * P])
                m.then_inc(at_T, 1)

            def scores(w):
                t, s = divmod(w, 2)
                lo, hi = max(0, t - 1), min(NT, t + 2)
                pe.wait_ge(at_Tr, 3 + t)
                for j in range(4):
                    cc, g = 2 * s + j // 2, j % 2
                    gs = slice(64 * g, 64 * g + 64)
                    if w:
                        pe.wait_ge(at_sr, 4 * w + j - 3)
                    pe.matmul(PS[:, j, 0:(hi - lo) * P], qT[gs, t % 2, cc * P:(cc + 1) * P], kT[gs, lo * P:hi * P],
                              start=True, stop=True).then_inc(at_s, 1)

            def products(w):
                t, s = divmod(w, 2)
                lo, hi = max(0, t - 1), min(NT, t + 2)

                def with_v(n):
                    q, g = 4 * w + n, n // 2
                    pe.wait_ge(at_pr, q + 1)
                    if w and n % 2 == 0:
                        pe.wait_ge(at_or, 2 * w + g - 1)
                    for b in range(hi - lo):
                        m = pe.matmul(PS[64 * (n % 2):64 * (n % 2) + 64, 6 + g, 0:P], AKV[:, lo + b, P + g * HD:P + (g + 1) * HD],
                                      PTv[q % 2][:, b * P:(b + 1) * P], start=(b == 0), stop=(b == hi - lo - 1))
                    if n % 2:
                        m.then_inc(at_o, 1)

                pe.wait_ge(at_n, 4 * w + 4)
                for n, j in enumerate(HEAD_ORDER):
                    q = 4 * w + n
                    if q >= 2:
                        pe.wait_ge(at_pr, q - 1)
                    for b in range(hi - lo):
                        m = tr(PS[:, 4 + q % 2, b * P:(b + 1) * P], SC[:, w % 2, j, b * P:(b + 1) * P])
                    m.then_inc(at_p, 1)
                    if n:
                        with_v(n - 1)
                with_v(3)

            queries(0)
            scores(0)
            for w in range(2 * NT):
                if w + 1 < 2 * NT:
                    if w % 2:
                        queries((w + 1) // 2)
                    scores(w + 1)
                products(w)
            for t in range(NT):
                pe.wait_ge(og_ready, t + 1)
                if t >= 2:
                    pe.wait_ge(og_Tr, t - 1)
                else:
                    pe.wait_ge(at_or, 32)
                for k in range(4):
                    m = tr(PS[:, t % 2, k * P:(k + 1) * P], O[:, t, k * P:(k + 1) * P])
                m.then_inc(og_T, 1)
            pe.wait_ge(og_Tr, NT)
            pe.wait_ge(wout_in, 16)

            def h2_transposed(t):
                pe.wait_ge(h2_row, t + 1)
                if t:
                    pe.wait_ge(h2_tr, 2 * t)
                for k in range(KD):
                    m = tr(PS[:, 4 + k // 4, (k % 4) * P:(k % 4 + 1) * P], xn2[:, t % 2, k * P:(k + 1) * P])
                    if k % 4 == 3:
                        m.then_inc(h2_tps, 1)

            def logits(t):
                pe.wait_ge(h2_tr, 2 * t + 2)
                if t:
                    pe.wait_ge(lg_ready, t)
                for k in range(KD):
                    m = pe.matmul(PS[:, 6, 0:NE], h2T[:, k, :], wrt[:, k, :], start=(k == 0), stop=(k == KD - 1))
                m.then_inc(lg_ps, 1)

            for t in range(NT + 2):
                if 2 <= t < NT:
                    pe.wait_ge(x1_ready, t - 1)
                if t < NT:
                    for k in range(KD):
                        for s in range(2):
                            m = pe.matmul(PS[:, 2 * (t % 2) + s, :], OT[:, k, t * P:(t + 1) * P], wout_sb[:, k, s * 512:(s + 1) * 512],
                                          start=(k == 0), stop=(k == KD - 1))
                    m.then_inc(y_ps, 1)
                if t >= 2:
                    logits(t - 2)
                if 1 <= t <= NT:
                    h2_transposed(t - 1)
            pe.wait_ge(mk_ready, 1)
            pe.matmul(PS[:, 0, 0:256], ones[:, :], MK[:, :, :].rearrange("p t e -> p (t e)"), start=True, stop=True)
            pe.matmul(PS[:, 1, 0:256], tri[:, :], MK[:, :, :].rearrange("p t e -> p (t e)"), start=True, stop=True).then_inc(po_ps, 1)
            for t in range(NT):
                m = tr(PS[0:NE, 2 + t // 4, (t % 4) * P:(t % 4 + 1) * P], GM[:, t, :])
            m.then_inc(gmt_ps, 1)
            pe.wait_ge(plan_ready, 1)
            pe.wait_ge(gmt_r, 1)

            def x_T():
                for k in range(KD):
                    m = tr(PS[:, 6 + k // 4, (k % 4) * P:(k % 4 + 1) * P], XG[:, k * P:(k + 1) * P])
                m.then_inc(tx_ps, 1)

            def product(s, i):
                h, k = divmod(s, KD)
                rows_h, rows_l = (XTh, XTl) if h < 2 else (ATh, ATl)
                pe.wait_ge(lo_done, i * NS + (NS + s + 1))
                for step, (rows, piece) in enumerate(((rows_h, hi), (rows_h, lo), (rows_l, hi))):
                    for a in range(2):
                        m = pe.matmul(PS[:, 2 * h + a, :], rows[:, k, :], piece[:, s % RING, a * 512:(a + 1) * 512],
                                      start=(k == 0 and step == 0), stop=(k == KD - 1 and step == 2))
                m.then_inc(ring_used, 1)

            def act_T(h, bk):
                for k in range(4):
                    m = tr(PS[:, bk, k * P:(k + 1) * P], AB[:, h, k * P:(k + 1) * P])
                m.then_inc(ta_ps, 1)

            total = pe.value_load(CEI[0:1, NE:NE + 1], min_val=1, max_val=MAXB)
            pe.nop().then_inc(tx_ps, 1)
            pe.nop().then_inc(ring_used, RING)
            pe.wait_ge(xg_in, 16)
            x_T()
            with pe.Fori(0, total) as i:
                pe.wait_ge(xl_done, i + 1)
                pe.wait_ge(gu_m, i * 2 + 1)
                for s in range(0, 12):
                    product(s, i)
                pe.wait_ge(ab_ready, i * 2 + 2)
                act_T(0, 6)
                for s in range(12, 16):
                    product(s, i)
                pe.wait_ge(xg_in, i * 16 + 32)
                pe.wait_ge(al_done, i * 2 + 1)
                x_T()
                pe.wait_ge(yb_rd, i + 1)
                for s in range(16, 19):
                    product(s, i)
                pe.wait_ge(ab_ready, i * 2 + 3)
                act_T(1, 0)
                product(19, i)
                pe.wait_ge(al_done, i * 2 + 2)
                for s in range(20, NS):
                    product(s, i)
            for t in range(NT):
                if t == 0:
                    pe.wait_ge(yb_rd, total + 1)
                    pe.wait_ge(bdn_in, 16)
                if t >= 4:
                    pe.wait_ge(f_acc, 4 * (t - 3))
                for s in range(2):
                    m = pe.matmul(PS[:, 2 * (t % 4) + s, :], GMT[:, t, :], bdn[:, s * 512:(s + 1) * 512], start=True, stop=True)
                m.then_inc(bd_ps, 1)

        @block.scalar
        def _(a):
            n = 0

            def link(ins):
                nonlocal n
                n += 1
                ins.then_inc(act, 1)
                a.wait_ge(act, n)

            a.wait_ge(c_ready, 1)
            a.activation(cT[:, 1, :], cT[:, 0, :], ACT.Sigmoid).then_inc(silu_sig, 1)
            for t in range(NT):
                a.wait_ge(x_in[0 if t < 4 else t // 2 - 1], 16)
                link(a.activation(SQ[:, :], XI[t % 6], ACT.Square, accum_out=st[:, t:t + 1]))
                a.nop().then_inc(h_ssq, 1)
            for t in range(NT):
                for s in range(2):
                    a.wait_ge(h_tps, 2 * t + s + 1)
                    a.activation(hT[:, 4 * s:4 * s + 4, t * P:(t + 1) * P],
                                 PS[:, 2 * (t % 2) + s, :].rearrange("p (k s) -> p k s", k=4), ACT.Copy).then_inc(h_ready, 1)
            j = 0
            for g, (what, c0, nn, slot) in enumerate(groups):
                if what == "qk":
                    for aa in range(4):
                        for s in range(2):
                            a.wait_ge(pj_ps, j + 1)
                            a.activation(QKT[:, aa, s * 512:(s + 1) * 512], PS[:, j % 6, :], ACT.Copy,
                                         scale=(DK ** -0.5 if aa < 2 else 1.0)).then_inc(pj_ev, 1)
                            j += 1
                    a.wait_ge(ada_used, 3 * KD)
                    for d in range(2):
                        for s in range(2):
                            a.wait_ge(pj_ps, j + 1)
                            a.activation(LR[:, d, s * 512:(s + 1) * 512], PS[0:RANK, j % 6, :], ACT.Copy).then_inc(pj_ev, 1)
                            j += 1
                    continue
                for t in range(NT):
                    a.wait_ge(pj_ps, j + 1)
                    if what == "v":
                        a.activation(V[:, t, :], PS[:, j % 6, :], ACT.Copy).then_inc(pj_ev, 1)
                    elif what == "g":
                        if t == 0:
                            a.wait_ge(mod_st, 16)
                        a.activation(GG[:, t, :], PS[:, j % 6, :], ACT.Sigmoid).then_inc(gg_sig, 1)
                    elif what == "aq":
                        a.activation(AQ[:, t, :].rearrange("p (c g d) -> p g c d", c=4, g=2),
                                     PS[:, j % 6, :].rearrange("p (g c d) -> p g c d", g=2, c=4), ACT.Copy).then_inc(pj_ev, 1)
                    else:
                        a.activation(AKV[:, t, :], PS[:, j % 6, 0:256], ACT.Copy).then_inc(pj_ev, 1)
                    j += 1
            a.wait_ge(fill_st, N_FILL)

            def log_sigmoid(u):
                a.wait_ge(z_exp, u + 1)
                link(a.activation(GI[:, 5, :], GI[:, 5, :], ACT.Exp, scale=-1.0))
                a.activation(GI[:, 5, :], GI[:, 5, :], ACT.Ln, bias=1.0).then_inc(z_ln, 1)

            log_sigmoid(0)
            for u in range(4):
                a.wait_ge(ex_in, 2 * u + 2)
                if u:
                    a.wait_ge(gl_o, 8 * u)
                    a.wait_ge(gl_s, 17 * u)
                a.activation(GI[:, 0, :], GI[:, 6, :], ACT.Exp, scale=1.0 / 16).then_inc(ex_out, 1)
                a.activation(GI[:, 1, :], GI[:, 6, :], ACT.Exp, scale=-1.0 / 16).then_inc(ex_out, 1)
                a.activation(GI[:, 3, :], GI[:, 7, :], ACT.Exp, scale=1.0 / 16).then_inc(ex_out, 1)
                a.activation(GI[:, 2, :], GI[:, 4, :], ACT.Exp, scale=1.0 / 16).then_inc(ex_out, 1)
                last = CHUNK - 1 if u % 2 == 0 else 0
                a.activation(dec[:, :], GI[:, 4, last:SEQ:CHUNK], ACT.Exp, scale=1.0 / 16).then_inc(ex_out, 1)
                for i in range(NT):
                    m = 8 * u + i
                    a.wait_ge(gl_ks, m + 1)
                    if m >= 2:
                        a.wait_ge(gl_u, 2 * (m - 1))
                    a.activation(KS[:, m % 2, :], PS[:, 0, 0:P], ACT.Copy).then_inc(gl_ksr, 1)
                    if u < 3 and i == 3:
                        log_sigmoid(u + 1)
            for b in range(2):
                a.wait_ge(at_T, b + 1)
                a.activation(kT[:, b * 512:(b + 1) * 512], PS[:, b, :], ACT.Copy).then_inc(at_Tr, 1)

            def queries(t):
                a.wait_ge(at_T, 3 + t)
                a.activation(qT[:, t % 2, :], PS[:, 4, :], ACT.Copy).then_inc(at_Tr, 1)

            def width(w):
                t = w // 2
                return (min(NT, t + 2) - max(0, t - 1)) * P

            def exponential(w, j):
                a.wait_ge(at_m, w + 1)
                if j < 4:
                    sc = SC[:, w % 2, j, 0:width(w)]
                    a.activation(sc, sc, ACT.Exp, bias=am[:, w % 2, 1, j:j + 1], accum_out=am[:, w % 2, 2, j:j + 1]).then_inc(at_e, 1)
                else:
                    a.activation(am[:, w % 2, 4, :], am[:, w % 2, 3, :], ACT.Exp).then_inc(at_e, 1)

            def outputs(w, g):
                a.wait_ge(at_o, 2 * w + g + 1)
                t, s = divmod(w, 2)
                a.activation(OT[:, 4 + 2 * g + s, t * P:(t + 1) * P], PS[:, 6 + g, 0:P], ACT.Copy).then_inc(at_or, 1)

            queries(0)
            for j in range(5):
                exponential(0, j)
            for w in range(2 * NT):
                if w % 2 and w + 1 < 2 * NT:
                    queries((w + 1) // 2)
                for r in range(4):
                    q = 4 * w + r
                    a.wait_ge(at_p, q + 1)
                    if q >= 2:
                        a.wait_ge(at_o, q // 2)
                    a.activation(PTv[q % 2][:, 0:width(w)], PS[:, 4 + q % 2, 0:width(w)], ACT.Copy).then_inc(at_pr, 1)
                    if w + 1 < 2 * NT:
                        exponential(w + 1, r)
                    if r == 3:
                        outputs(w, 0)
                if w + 1 < 2 * NT:
                    exponential(w + 1, 4)
                outputs(w, 1)
            for t in range(NT):
                a.wait_ge(og_T, t + 1)
                a.activation(OT[:, 0:4, t * P:(t + 1) * P], PS[:, t % 2, :].rearrange("p (k s) -> p k s", k=4), ACT.Copy).then_inc(og_Tr, 1)

            def h2_out(t):
                for s in range(2):
                    a.wait_ge(h2_tps, 2 * t + s + 1)
                    if t:
                        a.wait_ge(lg_ps, t)
                    a.activation(h2T[:, 4 * s:4 * s + 4, :], PS[:, 4 + s, :].rearrange("p (k s) -> p k s", k=4), ACT.Copy).then_inc(h2_tr, 1)

            for t in range(NT):
                a.wait_ge(y_ps, t + 1)
                link(a.activation(SQ[:, :].rearrange("p (a n) -> p a n", a=2), PS[:, 2 * (t % 2):2 * (t % 2) + 2, :], ACT.Square,
                                  accum_out=st[:, 16 + t:17 + t]))
                a.nop().then_inc(y_ssq, 1)
                a.wait_ge(x1_ready, t + 1)
                link(a.activation(SQ[:, :], X1[:, t, :], ACT.Square, accum_out=st[:, 24 + t:25 + t]))
                a.nop().then_inc(x1_ssq, 1)
                if t:
                    h2_out(t - 1)
            h2_out(NT - 1)
            a.wait_ge(g_exp, 1)
            link(a.activation(GT8[:, :, :], GT8[:, :, :], ACT.Exp))
            a.nop().then_inc(g_exp, 1)
            a.wait_ge(gmt_ps, 1)
            a.activation(GMT[:, :, :].rearrange("p (b t) s -> p b (t s)", b=2), PS[0:NE, 2:4, :], ACT.Copy).then_inc(gmt_r, 1)

            a.wait_ge(plan_ready, 1)
            last = a.value_load(CEI[0:1, NE + 1:NE + 2], min_val=NE - 1, max_val=MAXB - 1)

            def high(s, i, e1, ahead=False):
                if s % 4 == 0:
                    a.wait_ge(w_piece[s // 4], e1 * (32 if s < 16 else 16))
                if s == 8:
                    a.wait_ge(bi_in, e1 * 32)
                if i is not None:
                    a.wait_ge(ring_used, i * NS + (s + 1 + (NS if ahead else 0)))
                elif s >= RING:
                    a.wait_ge(ring_used, s + 1)
                a.activation(hi[:, s % RING, :], raw[:, s, :], ACT.Copy).then_inc(hi_done, 1)

            def x_high(count):
                a.wait_ge(tx_ps, count)
                a.activation(Q[:, 8192:9216].rearrange("p (a n) -> p a n", a=2), PS[:, 6:8, :], ACT.Copy).then_inc(xh_done, 1)

            a.nop().then_inc(yb_rd, 1)
            a.nop().then_inc(yb_st, 16)
            for s in range(12):
                if s == RING:
                    x_high(2)
                high(s, None, 1)

            def from_sigmoid(i, e1, e_next):
                def sigmoid(h):
                    a.wait_ge(gu_g, i * 2 + (h + 1))
                    a.activation(SG, GS, ACT.Sigmoid, scale=ALPHA).then_inc(gu_sig, 1)

                def act_high(h, bk):
                    a.wait_ge(ta_ps, i * 2 + (h + 1))
                    a.activation(ATh[:, 4 * h:4 * h + 4, :], PS[:, bk, :].rearrange("p (k s) -> p k s", k=4), ACT.Copy).then_inc(ah_done, 1)

                sigmoid(0)
                for s in range(12, 15):
                    high(s, i, e1)
                act_high(0, 6)
                for s in range(15, 20):
                    high(s, i, e1)
                sigmoid(1)
                if e_next is not None:
                    x_high(i + 3)
                high(20, i, e1)
                high(21, i, e1)
                act_high(1, 0)
                high(22, i, e1)
                high(23, i, e1)
                if e_next is not None:
                    for s in range(3):
                        high(s, i, e_next, ahead=True)
                a.wait_ge(ring_used, i * NS + (NS + RING))
                a.wait_ge(yb_st, i * 16 + 16)
                a.activation(YS.rearrange("p (a n) -> p a n", a=2), PS[:, 4:6, :], ACT.Copy).then_inc(yb_rd, 1)
                if e_next is not None:
                    high(3, i, e_next, ahead=True)
                a.wait_ge(yb_rd, i + 2)
                a.dma_start(y_dram[bass.ds(i * BLK, BLK), :], YS).then_inc(yb_st, 16)
                if e_next is not None:
                    for s in range(RING, 12):
                        high(s, i, e_next, ahead=True)

            with a.Fori(0, last) as i:
                e1 = a.value_load(EBI[0:1, bass.ds(i, 1)], min_val=1, max_val=NE)
                e_next = a.value_load(EBI[0:1, bass.ds(i + 1, 1)], min_val=1, max_val=NE)
                from_sigmoid(i, e1, e_next)
            from_sigmoid(last, NE, None)
            for t in range(NT):
                a.wait_ge(f_acc, 4 * (t + 1))
                link(a.activation(SQ[:, :], FO[:, t % 4, :], ACT.Square, accum_out=st[:, 40 + t:41 + t]))
                a.nop().then_inc(f_ssq, 1)

        @block.vector
        def _(v):
            n = 0

            def link(ins):
                nonlocal n
                n += 1
                ins.then_inc(dve, 1)
                v.wait_ge(dve, n)

            v.wait_ge(vec_T, 1)
            link(v.tensor_copy(cT[:, 0, :], PS[:, 0, 0:KD]))
            link(v.tensor_copy(bgT[:, :], PS[:, 0, 16:20]))
            v.nop().then_inc(c_ready, 1)
            v.wait_ge(silu_sig, 1)
            link(v.tensor_tensor(cT[:, 0, :], cT[:, 0, :], cT[:, 1, :], ALU.mult))
            v.wait_ge(bada_in, 48)
            def ada(j):
                nn, k = divmod(j, KD)
                v.wait_ge(ada_in[j % 4], 16 * (j // 4 + 1))
                if k:
                    v.wait_ge(ada_used, j)
                ac = acc[nn]
                v.scalar_tensor_tensor(out=ac, in0=ada_ring[:, j % 4, :], scalar=cT[:, 0, k:k + 1], in1=ac,
                                       op0=ALU.mult, op1=ALU.add).then_inc(ada_used, 1)
            def modulation(m):
                v.wait_ge(mod_ps, m + 1)
                what, s = divmod(m, 2)
                hs = slice(s * 512, (s + 1) * 512)
                src = PS[:, 6 + m % 2, :]
                if what in (0, 3):
                    ins = v.tensor_copy((SH1 if what == 0 else MODR[:, 2, :])[:, hs], src)
                elif what in (1, 4):
                    dst = (S1 if what == 1 else MODR[:, 1, :])[:, hs]
                    ins = v.scalar_tensor_tensor(out=dst, in0=src, scalar=1.0, in1=dst, op0=ALU.add, op1=ALU.mult)
                else:
                    dst = (MODR[:, 0, :] if what == 2 else MODR[:, 3, :])[:, hs]
                    ins = v.tensor_tensor(dst, src, dst, ALU.mult)
                ins.then_inc(mod_ready, 1)

            for j in range(KD):
                ada(j)
            for m in range(4):
                modulation(m)
            v.wait_ge(mod_ready, 4)
            for t in range(NT):
                v.wait_ge(h_rstd, t + 1)
                if t >= 2:
                    v.wait_ge(h_tps, 2 * (t - 1))
                link(v.scalar_tensor_tensor(out=xn[:, t % 2, :], in0=XI[t % 6], scalar=st[:, t:t + 1], in1=S1, op0=ALU.mult, op1=ALU.mult))
                v.tensor_tensor(xn[:, t % 2, :], xn[:, t % 2, :], SH1, ALU.add).then_inc(h_row, 1)
            for j in range(KD, 3 * KD):
                ada(j)
            v.wait_ge(g_in, 48)
            for m in range(4, 12):
                modulation(m)
            for t in range(NT):
                j = GJ + t
                v.wait_ge(gg_sig, t + 1)
                link(v.tensor_tensor(GG[:, t, :], PS[:, j % 6, :], GG[:, t, :], ALU.mult))
                v.nop().then_inc(gg_done, 1)
                v.tensor_tensor(GG[:, t, :].rearrange("p (h n) -> p h n", h=HEADS), GG[:, t, :].rearrange("p (h n) -> p h n", h=HEADS),
                                ggla[:, :].unsqueeze(1).broadcast_to([P, HEADS, DV]), ALU.mult).then_inc(dve, 1)
                n += 1
            chv = lambda ap: ap.rearrange("p (c s) -> p c s", s=CHUNK)
            def prepare(u, step):
                d = u % 2
                if step in (0, 1):
                    v.wait_ge(z_ps, 2 * u + step + 1)
                    v.tensor_scalar(GI[:, 4, step * 512:(step + 1) * 512], PS[:, 7, :], bgT[:, 2 * d + u // 2:2 * d + u // 2 + 1], None,
                                    ALU.add).then_inc(z_rd, 1)
                elif step == 2:
                    v.wait_ge(z_rd, 2 * u + 2)
                    v.scalar_tensor_tensor(out=GI[:, 5, :], in0=GI[:, 4, :], scalar=-1.0, in1=GI[:, 4, :], op0=ALU.mult, op1=ALU.max).then_inc(z_exp, 1)
                elif step == 3:
                    v.wait_ge(z_ln, u + 1)
                    link(v.scalar_tensor_tensor(out=GI[:, 7, :], in0=GI[:, 4, :], scalar=0.0, in1=GI[:, 5, :], op0=ALU.min, op1=ALU.subtract))
                elif step == 4:
                    if u == 0:
                        v.wait_ge(scan_ready, 1)
                    link(v.tensor_tensor_scan(GI[:, 4 if d == 0 else 6, :], scanm, GI[:, 7, :], 0.0, ALU.mult, ALU.add))
                elif step == 5 and d:
                    link(v.tensor_tensor(GI[:, 5, :], GI[:, 7, :], GI[:, 6, :], ALU.subtract))
                    link(v.tensor_tensor(chv(GI[:, 4, :]), chv(GI[:, 5, :]), chv(GI[:, 6, :])[:, :, CHUNK - 1:CHUNK].broadcast_to([P, NCH, CHUNK]), ALU.add))
                elif step == 6:
                    ref, last = (CHUNK // 2 - 1, CHUNK - 1) if d == 0 else (CHUNK // 2, 0)
                    b = chv(GI[:, 4, :])
                    v.tensor_tensor(chv(GI[:, 6, :]), b, b[:, :, ref:ref + 1].broadcast_to([P, NCH, CHUNK]), ALU.subtract).then_inc(ex_in, 1)
                    v.tensor_tensor(chv(GI[:, 7, :]), b[:, :, last:last + 1].broadcast_to([P, NCH, CHUNK]), b, ALU.subtract).then_inc(ex_in, 1)

            for step in range(7):
                prepare(0, step)
            v.wait_ge(fill_st, N_FILL)
            for u in range(4):
                p, d = divmod(u, 2)
                q, k = QKT[:, p, :], QKT[:, 2 + p, :]
                if u:
                    v.wait_ge(gl_o, 8 * u)
                    v.wait_ge(gl_s, 17 * u)
                v.memset(S[:, 0, :], 0.0).then_inc(gl_s, 1)
                for part, (a_, src) in enumerate(((0, q), (1, k), (3, k), (2, q))):
                    v.wait_ge(ex_out, 5 * u + part + 1 + (part == 3))
                    ins = v.tensor_tensor(GI[:, a_, :], GI[:, a_, :], src, ALU.mult)
                link(ins)
                v.nop().then_inc(gi_ready, 1)

                def masked(i):
                    m = 8 * u + i
                    v.wait_ge(gl_st, m + 1)
                    if m >= 2:
                        v.wait_ge(gl_in, m - 1)
                    v.tensor_tensor(ST[:, m % 2, :, :], PS[:, 1:3, 0:P],
                                    cmask[:, d, :].unsqueeze(1).broadcast_to([P, 2, P]), ALU.mult).then_inc(gl_str, 1)

                masked(0)
                for i in range(NT):
                    t = i if d == 0 else NT - 1 - i
                    m = 8 * u + i
                    for qq, ch in enumerate((0, 1) if d == 0 else (1, 0)):
                        v.wait_ge(gl_u, 2 * m + qq + 1)
                        v.wait_ge(gl_s, 2 * m + u + 1 + qq)
                        if qq == 1:
                            if i + 1 < NT:
                                masked(i + 1)
                            v.wait_ge(gl_i, m + 1)
                        elif m:
                            v.wait_ge(gl_o, m)
                        v.scalar_tensor_tensor(out=S[:, 1 - qq, :], in0=S[:, qq, :], scalar=dec[:, 2 * t + ch:2 * t + ch + 1],
                                               in1=PS[:, 5 + ch, 0:P], op0=ALU.mult, op1=ALU.add).then_inc(gl_s, 1)
                    v.wait_ge(gl_o, m + 1)
                    o = O[:, t, 2 * p * DV:(2 * p + 2) * DV].rearrange("p (h n) -> p h n", h=2)
                    src = PS[:, 3:5, 0:P]
                    if d == 0:
                        v.tensor_copy(o, src).then_inc(gl_ev, 1)
                    else:
                        v.tensor_tensor(o, src, o, ALU.add).then_inc(gl_ev, 1)
                    if u < 3 and i < 7:
                        prepare(u + 1, i)
            v.wait_ge(gl_ev, 32)
            for t in range(NT):
                o = O[:, t, :].rearrange("p (h n) -> p h n", h=HEADS)
                tmp = XS[:, 0:512].rearrange("p (h n) -> p h n", h=HEADS)
                link(v.tensor_tensor(tmp, o, o, ALU.mult))
                v.tensor_reduce(st[:, 48:52], tmp, AX.X, ALU.add).then_inc(og_ssq, 1)
                v.wait_ge(og_rstd, t + 1)
                link(v.tensor_tensor(o, o, st[:, 48:52].unsqueeze(2).broadcast_to([P, HEADS, DV]), ALU.mult))
                v.tensor_tensor(O[:, t, :], O[:, t, :], GG[:, t, :], ALU.mult).then_inc(og_ready, 1)
            cos, sin = rot[:, 0, :, :], rot[:, 1, :, :]
            for buf, nh in ((AQ[:, :, :], QH), (AKV[:, :, 0:P], KVH)):
                hv = buf.rearrange("p t (h d) -> p t h d", d=HD)
                for h in range(nh):
                    x1, x2 = hv[:, :, h, 0:HALF], hv[:, :, h, HALF:ROT]
                    v.tensor_tensor(rtmp[:, 0, :, :], x1, cos, ALU.mult)
                    v.tensor_tensor(rtmp[:, 1, :, :], x2, sin, ALU.mult)
                    v.tensor_tensor(rtmp[:, 2, :, :], x2, cos, ALU.mult)
                    link(v.tensor_tensor(rtmp[:, 3, :, :], x1, sin, ALU.mult))
                    v.tensor_tensor(x1, rtmp[:, 0, :, :], rtmp[:, 1, :, :], ALU.subtract)
                    link(v.tensor_tensor(x2, rtmp[:, 2, :, :], rtmp[:, 3, :, :], ALU.add))
            v.nop().then_inc(rot_ready, 1)
            def masked_max(w):
                t, s = divmod(w, 2)
                lo, hi = max(0, t - 1), min(NT, t + 2)
                nn = (hi - lo) * P
                am0 = lo - (t - 1)
                A = am[:, w % 2, :, :]
                if w >= 2:
                    v.wait_ge(at_p, 4 * (w - 1))
                for j in range(4):
                    v.wait_ge(at_s, 4 * w + j + 1)
                    v.scalar_tensor_tensor(out=SC[:, w % 2, j, 0:nn].rearrange("p (b n) -> p b n", n=P),
                                           in0=PS[:, j, 0:nn].rearrange("p (b n) -> p b n", n=P), scalar=HD ** -0.5,
                                           in1=amask[:, am0:am0 + hi - lo, :], op0=ALU.mult, op1=ALU.add).then_inc(at_sr, 1)
                v.wait_ge(at_sr, 4 * w + 4)
                sk = sinkb[:, :].rearrange("p (g c) -> p c g", g=2)[:, 2 * s:2 * s + 2, :]
                pair = lambda row: A[:, row, :].rearrange("p (c g) -> p c g", g=2)
                link(v.tensor_reduce(A[:, 0, :], SC[:, w % 2, :, 0:nn], AX.X, ALU.max))
                link(v.tensor_tensor(pair(0), pair(0), sk, ALU.max))
                link(v.tensor_scalar(A[:, 1, :], A[:, 0, :], -1.0, None, ALU.mult))
                link(v.tensor_tensor(pair(3), sk, pair(0), ALU.subtract))
                v.nop().then_inc(at_m, 1)

            def normalised(w):
                nn = (min(NT, w // 2 + 2) - max(0, w // 2 - 1)) * P
                A = am[:, w % 2, :, :]
                v.wait_ge(at_e, 5 * w + 5)
                link(v.tensor_tensor(A[:, 5, :], A[:, 2, :], A[:, 4, :], ALU.add))
                link(v.reciprocal(A[:, 5, :], A[:, 5, :]))
                for j in HEAD_ORDER:
                    sc = SC[:, w % 2, j, 0:nn]
                    v.tensor_scalar(sc, sc, A[:, 5, j:j + 1], None, ALU.mult).then_inc(at_n, 1)

            masked_max(0)
            for w in range(2 * NT):
                if w + 1 < 2 * NT:
                    masked_max(w + 1)
                normalised(w)
            def top4(t):
                v.wait_ge(lg_ps, t + 1)
                link(v.tensor_tensor(LG[:, t, :], PS[:, 6, 0:NE], brt[:, :], ALU.add))
                v.nop().then_inc(lg_ready, 1)
                link(v.max(M8[:, t, :], LG[:, t, :]))
                link(v.max_index(I8[:, t, :], M8[:, t, :], LG[:, t, :]))

            v.wait_ge(rows_in, 16)
            for t in range(NT):
                v.wait_ge(y_rstd, t + 1)
                for s in range(2):
                    v.scalar_tensor_tensor(out=XS[:, s * 512:(s + 1) * 512], in0=PS[:, 2 * (t % 2) + s, :], scalar=st[:, 16 + t:17 + t],
                                           in1=GP1[:, s * 512:(s + 1) * 512], op0=ALU.mult, op1=ALU.mult).then_inc(dve, 1)
                n += 2
                v.wait_ge(dve, n)
                v.wait_ge(x_again[t // 4], 16)
                v.tensor_tensor(X1[:, t, :], X1[:, t, :], XS[:, :], ALU.add).then_inc(x1_ready, 1)
                v.wait_ge(x1_rstd, t + 1)
                if t >= 2:
                    v.wait_ge(h2_tps, 2 * (t - 1))
                    v.wait_ge(h2_st[t % 2], 16 * (t // 2))
                link(v.scalar_tensor_tensor(out=xn2[:, t % 2, :], in0=X1[:, t, :], scalar=st[:, 24 + t:25 + t], in1=S2, op0=ALU.mult, op1=ALU.mult))
                link(v.tensor_tensor(xn2[:, t % 2, :], xn2[:, t % 2, :], SH2, ALU.add))
                v.nop().then_inc(h2_row, 1)
                if t >= 2:
                    top4(t - 2)
            top4(NT - 2)
            top4(NT - 1)
            link(v.tensor_copy(IF[:, :, :], I8[:, :, 0:TOPK]))
            link(v.tensor_tensor(GT8[:, :, :], M8[:, :, 0:TOPK], M8[:, :, 0:1].broadcast_to([P, NT, TOPK]), ALU.subtract))
            v.nop().then_inc(g_exp, 1)
            for t in range(NT):
                v.tensor_tensor(OH[:, t, :, :], iot[:, 0:NE].unsqueeze(1).broadcast_to([P, TOPK, NE]),
                                IF[:, t, :].unsqueeze(2).broadcast_to([P, TOPK, NE]), ALU.is_equal).then_inc(dve, 1)
                n += 1
            v.wait_ge(dve, n)
            link(v.tensor_reduce(MK[:, :, :], OH[:, :, :, :].rearrange("p t k e -> p t e k"), AX.X, ALU.add))
            v.wait_ge(g_exp, 2)
            link(v.tensor_reduce(gsum[:, 0, :], GT8[:, :, :], AX.X, ALU.add))
            link(v.reciprocal(gsum[:, 1, :], gsum[:, 0, :]))
            link(v.tensor_tensor(GT8[:, :, :], GT8[:, :, :], gsum[:, 1, :].unsqueeze(2).broadcast_to([P, NT, TOPK]), ALU.mult))
            link(v.tensor_tensor(OM, OH[:, :, :, :], GT8[:, :, :].unsqueeze(3).broadcast_to([P, NT, TOPK, NE]), ALU.mult))
            link(v.tensor_reduce(GM[:, :, :], OM.rearrange("p t k e -> p t e k"), AX.X, ALU.add))
            v.nop().then_inc(mk_ready, 1)
            v.wait_ge(po_ps, 1)
            tot = PS[:, 0, 0:256].rearrange("p (t e) -> p t e", t=NT)
            link(v.tensor_copy(PO[:, :, :], PS[:, 1, 0:256].rearrange("p (t e) -> p t e", t=NT)))
            link(v.tensor_copy(cn[:, 0, :], tot[:, 0, :]))
            for t in range(1, NT):
                link(v.tensor_tensor(PO[:, t, :], PO[:, t, :], cn[:, 0, :], ALU.add))
                link(v.tensor_tensor(cn[:, 0, :], tot[:, t, :], cn[:, 0, :], ALU.add))
            link(v.tensor_scalar(cn[:, 1, :], cn[:, 0, :], float(BLK), 1.0, ALU.is_gt, ALU.add))
            for m in range(2, SEQ // BLK):
                link(v.scalar_tensor_tensor(out=cn[:, 1, :], in0=cn[:, 0, :], scalar=float(m * BLK), in1=cn[:, 1, :], op0=ALU.is_gt, op1=ALU.add))
            link(v.tensor_tensor_scan(cn[:, 2, :], ones[:, 0:NE], cn[:, 1, :], 0.0, ALU.mult, ALU.add))
            link(v.tensor_tensor(cn[:, 3, :], cn[:, 2, :], cn[:, 1, :], ALU.subtract))
            link(v.tensor_copy(CEI[:, 0:NE], cn[0:1, 3, :]))
            link(v.tensor_copy(CEI[:, NE:NE + 1], cn[0:1, 2, NE - 1:NE]))
            link(v.tensor_scalar(cn[0:1, 1, 0:1], cn[0:1, 2, NE - 1:NE], 1.0, None, ALU.subtract))
            link(v.tensor_copy(CEI[:, NE + 1:NE + 2], cn[0:1, 1, 0:1]))
            link(v.tensor_scalar(cn[:, 3, :], cn[:, 3, :], float(BLK), None, ALU.mult))
            link(v.tensor_tensor(PO[:, :, :], PO[:, :, :], cn[:, 3, :].unsqueeze(1).broadcast_to([P, NT, NE]), ALU.add))
            for t in range(NT):
                v.tensor_tensor(OM[:, t], OH[:, t, :, :], PO[:, t, :].unsqueeze(1).broadcast_to([P, TOPK, NE]), ALU.mult).then_inc(dve, 1)
                n += 1
            v.wait_ge(dve, n)
            link(v.tensor_reduce(SL[:, :, :], OM, AX.X, ALU.add))
            link(v.tensor_copy(SLI[:, :], SL[:, :, :].rearrange("p t k -> p (t k)")))
            eb = OMX[0:1, :].rearrange("p (b e) -> p b e", e=NE)
            link(v.tensor_tensor(eb, cn[0:1, 2, :].unsqueeze(1).broadcast_to([1, MAXB, NE]),
                                 iot[0:1, 0:MAXB].unsqueeze(2).broadcast_to([1, MAXB, NE]), ALU.is_le))
            link(v.tensor_reduce(EB[:, :], eb, AX.X, ALU.add))
            link(v.tensor_scalar(EB[:, :], EB[:, :], float(NE - 1), 1.0, ALU.min, ALU.add))
            link(v.tensor_copy(EBI[:, :], EB[:, :]))
            v.nop().then_inc(plan_ready, 1)

            last = v.value_load(CEI[0:1, NE + 1:NE + 2], min_val=NE - 1, max_val=MAXB - 1)
            v.nop().then_inc(gu_m, 1)
            v.nop().then_inc(ab_ready, 1)
            v.nop().then_inc(lo_done, NS)

            def low(s, i, ahead=False):
                v.wait_ge(hi_done, s + 1 if i is None else i * NS + (s + 1 + (NS if ahead else 0)))
                v.tensor_tensor(lo[:, s % RING, :], raw[:, s, :], hi_f[:, s % RING, :], ALU.subtract).then_inc(lo_done, 1)

            def x_low(count):
                v.wait_ge(xh_done, count)
                v.tensor_tensor(Q[:, 9216:10240].rearrange("p (a n) -> p a n", a=2), PS[:, 6:8, :],
                                Q[:, 8192:9216].bitcast(F32).rearrange("p (a n) -> p a n", a=2), ALU.subtract).then_inc(xl_done, 1)

            for s in range(RING):
                low(s, None)
            x_low(1)
            def block(i, more):
                def act_low(h, bk):
                    v.wait_ge(ah_done, i * 2 + (h + 1))
                    v.tensor_tensor(ATl[:, 4 * h:4 * h + 4, :], PS[:, bk, :].rearrange("p (k s) -> p k s", k=4),
                                    ATh[:, 4 * h:4 * h + 4, :].bitcast(F32), ALU.subtract).then_inc(al_done, 1)

                def glu(h):
                    v.wait_ge(ring_used, i * NS + (8 * (h + 1) + RING))
                    v.tensor_tensor(GU, PS[:, 2 * h:2 * h + 2, :], BI[:, h, :, :], ALU.add).then_inc(gu_m, 1)
                    v.wait_ge(gu_m, i * 2 + (h + 2))
                    v.tensor_scalar(GS, GS, LIMIT, None, ALU.min).then_inc(gu_g, 1)
                    v.tensor_scalar(US, US, LIMIT, -LIMIT, ALU.min, ALU.max).then_inc(gu_c, 1)
                    v.wait_ge(gu_g, i * 2 + (h + 1))
                    v.wait_ge(gu_c, i * 4 + (2 * h + 1))
                    v.scalar_tensor_tensor(out=US, in0=US, scalar=1.0, in1=GS, op0=ALU.add, op1=ALU.mult).then_inc(gu_c, 1)
                    v.wait_ge(gu_c, i * 4 + (2 * h + 2))
                    v.wait_ge(gu_sig, i * 2 + (h + 1))
                    v.tensor_tensor(AB[:, h, :], US, SG, ALU.mult).then_inc(ab_ready, 1)

                for s in range(RING, 10):
                    low(s, i)
                glu(0)
                for s in range(10, 15):
                    low(s, i)
                act_low(0, 6)
                for s in range(15, 18):
                    low(s, i)
                glu(1)
                low(18, i)
                low(19, i)
                if more:
                    x_low(i + 2)
                low(20, i)
                act_low(1, 0)
                for s in range(21, NS):
                    low(s, i)
                if more:
                    for s in range(RING):
                        low(s, i, ahead=True)

            with v.Fori(0, last) as i:
                block(i, True)
            block(last, False)
            for t in range(NT):
                v.wait_ge(bd_ps, t + 1)
                if t >= 4:
                    v.wait_ge(out_st[t % 4], 16 * (t // 4))
                f = FO[:, t % 4, :]
                for k in range(TOPK):
                    j = TOPK * t + k
                    v.wait_ge(yr_in[j % 16], 16 * (j // 16 + 1))
                    if k:
                        v.wait_ge(f_acc, j)
                    src = f.rearrange("p (a n) -> p a n", a=2) if k else PS[:, 2 * (t % 4):2 * (t % 4) + 2, :]
                    v.scalar_tensor_tensor(out=f.rearrange("p (a n) -> p a n", a=2), in0=YR[:, j % 16, :].rearrange("p (a n) -> p a n", a=2),
                                           scalar=GT8[:, t, k:k + 1], in1=src, op0=ALU.mult, op1=ALU.add).then_inc(f_acc, 1)
                v.wait_ge(f_rstd, t + 1)
                if t == 0:
                    v.wait_ge(gp2_in, 16)
                v.wait_ge(x1_in[t // 4], 16)
                link(v.scalar_tensor_tensor(out=f, in0=f, scalar=st[:, 40 + t:41 + t], in1=GP2, op0=ALU.mult, op1=ALU.mult))
                v.tensor_tensor(f, f, XR[:, t, :], ALU.add).then_inc(f_out, 1)


_INS = ['x', 'c', 'w_ada', 'b_ada', 'g_pre_mix', 'g_post_mix', 'w_in', 'w_gk_fwd', 'b_gk_fwd', 'w_gk_bwd', 'b_gk_bwd',
        'g_gla_out', 'attn_sink', 'w_out', 'g_pre_ffn', 'g_post_ffn', 'w_router', 'b_router',
        'w_gate_up', 'b_gate_up', 'w_down', 'b_down']
_OUTS = [((1, SEQ, D), 'float32')]


def kernel(**inputs):
    import numpy as _np
    import concourse.bacc as _bacc
    from concourse import mybir as _mybir
    from concourse.bass_utils import run_bass_kernel_spmd as _run

    nc = _bacc.Bacc("TRN2", target_bir_lowering=False, num_devices=1)
    arrays, args = {}, []
    for name in _INS:
        a = _np.ascontiguousarray(inputs[name])
        arrays[f"in_{name}_dram"] = a
        args.append(nc.dram_tensor(f"in_{name}_dram", a.shape, _mybir.dt.from_np(a.dtype), kind="ExternalInput").ap())
    for i, (shape, dtype) in enumerate(_OUTS):
        dt = _mybir.dt.from_np(_np.dtype(dtype))
        args.append(nc.dram_tensor(f"out_{i}_dram", shape, dt, kind="ExternalOutput").ap())
    block_kernel(nc, *args)
    r = _run(nc, [arrays], core_ids=[0])
    return r.results[0]["out_0_dram"]
```
